# Optimizing a Trainium2 kernel written in Bass

```python
import jax, jax.numpy as jnp
from jax import lax
import numpy as np

D_MODEL = 1024
BATCH = 1
SEQ = 256
DEPTH = 1

D_RNN = 1024
RNN_BLOCKS = 8
RNN_BW = D_RNN // RNN_BLOCKS
CONV_W = 4
LRU_C = 8.0
N_HEADS = 8
HEAD_DIM = 128
D_ATTN = N_HEADS * HEAD_DIM
MOBA_BLOCK = 256
MOBA_TOPK = 3
Q_CHUNK = 32
N_BRANCH = 2
D_FF = 2816
FFN_CONV_W = 3

D_IN = 2 * D_RNN + 3 * D_ATTN + N_BRANCH * D_MODEL
EPS = 1e-6
NEG = -1e30


def rmsnorm(x, g):
    xf = x.astype(jnp.float32)
    y = xf * lax.rsqrt(jnp.mean(xf * xf, axis=-1, keepdims=True) + EPS)
    return (y * g.astype(jnp.float32)).astype(x.dtype)

def causal_dwconv(x, w, b):
    width = w.shape[0]
    s = x.shape[1]
    xp = jnp.pad(x, ((0, 0), (width - 1, 0), (0, 0)))
    y = b
    for k in range(width):
        y = y + xp[:, k:k + s] * w[k]
    return y

def rg_lru(x, w_r, b_r, w_i, b_i, lam):
    bsz, s, _ = x.shape
    xb = x.reshape(bsz, s, RNN_BLOCKS, RNN_BW)
    r = jax.nn.sigmoid(jnp.einsum('bsnc,ncd->bsnd', xb, w_r) + b_r).reshape(bsz, s, D_RNN)
    i = jax.nn.sigmoid(jnp.einsum('bsnc,ncd->bsnd', xb, w_i) + b_i).reshape(bsz, s, D_RNN)
    log_a = (-LRU_C * r.astype(jnp.float32)) * jax.nn.softplus(-lam.astype(jnp.float32))
    a = jnp.exp(log_a)
    mult = jnp.sqrt(-jnp.expm1(2.0 * log_a))
    bx = mult * (i * x).astype(jnp.float32)

    def combine(c1, c2):
        a1, b1 = c1
        a2, b2 = c2
        return a1 * a2, a2 * b1 + b2

    _, h = lax.associative_scan(combine, (a, bx), axis=1)
    return h.astype(x.dtype)

def moba_attention(q, k, v):
    bsz, nh, s, hd = q.shape
    nb = -(-s // MOBA_BLOCK)
    s_pad = nb * MOBA_BLOCK
    pad = ((0, 0), (0, 0), (0, s_pad - s), (0, 0))
    q = jnp.pad(q, pad)
    k = jnp.pad(k, pad)
    v = jnp.pad(v, pad)
    kb = k.reshape(bsz, nh, nb, MOBA_BLOCK, hd)
    vb = v.reshape(bsz, nh, nb, MOBA_BLOCK, hd)
    k_mean = jnp.mean(kb.astype(jnp.float32), axis=3)
    n_sel = min(MOBA_TOPK, nb)
    n_chunks = s_pad // Q_CHUNK
    scale = HEAD_DIM ** -0.5
    qc = q.reshape(bsz, nh, n_chunks, Q_CHUNK, hd).transpose(2, 0, 1, 3, 4)
    gather = jax.vmap(jax.vmap(lambda t, ix: t[ix]))

    def chunk_fn(args):
        ci, qi = args
        q_pos = ci * Q_CHUNK + jnp.arange(Q_CHUNK)
        own = (ci * Q_CHUNK) // MOBA_BLOCK
        gate = jnp.einsum('bhqd,bhnd->bhqn', qi.astype(jnp.float32), k_mean)
        gate = jnp.where(jnp.arange(nb) < own, gate, NEG)
        _, idx = lax.top_k(gate, n_sel)
        slot_ok = jnp.arange(n_sel) < own
        k_sel = gather(kb, idx)
        v_sel = gather(vb, idx)
        k_own = lax.dynamic_slice_in_dim(k, own * MOBA_BLOCK, MOBA_BLOCK, axis=2)
        v_own = lax.dynamic_slice_in_dim(v, own * MOBA_BLOCK, MOBA_BLOCK, axis=2)
        s_sel = jnp.einsum('bhqd,bhqnkd->bhqnk', qi, k_sel).astype(jnp.float32) * scale
        s_sel = jnp.where(slot_ok[:, None], s_sel, NEG).reshape(bsz, nh, Q_CHUNK, n_sel * MOBA_BLOCK)
        s_own = jnp.einsum('bhqd,bhkd->bhqk', qi, k_own).astype(jnp.float32) * scale
        k_pos = own * MOBA_BLOCK + jnp.arange(MOBA_BLOCK)
        s_own = jnp.where(k_pos[None, :] <= q_pos[:, None], s_own, NEG)
        p = jax.nn.softmax(jnp.concatenate([s_sel, s_own], axis=-1), axis=-1).astype(v.dtype)
        p_sel = p[..., :n_sel * MOBA_BLOCK].reshape(bsz, nh, Q_CHUNK, n_sel, MOBA_BLOCK)
        p_own = p[..., n_sel * MOBA_BLOCK:]
        return (jnp.einsum('bhqnk,bhqnkd->bhqd', p_sel, v_sel)
                + jnp.einsum('bhqk,bhkd->bhqd', p_own, v_own))

    o = lax.map(chunk_fn, (jnp.arange(n_chunks), qc))
    o = o.transpose(1, 2, 0, 3, 4).reshape(bsz, nh, s_pad, hd)[:, :, :s]
    return o

def first_inputs(seed: int = 0) -> dict:
    key = jax.random.key(seed)
    ks = jax.random.split(key, 24)
    f32 = jnp.float32
    L = DEPTH

    def nrm(k, shape, scale):
        return jax.random.normal(k, shape, f32) * scale

    a0 = jax.random.uniform(ks[9], (L, D_RNN), f32, 0.9, 0.999)
    s0 = a0 ** (1.0 / LRU_C)
    lru_lambda = jnp.log(s0) - jnp.log1p(-s0)
    return {
        "x": jax.random.normal(ks[0], (BATCH, SEQ, D_MODEL), f32),
        "norm1_g": 1.0 + nrm(ks[1], (L, D_MODEL), 0.02),
        "w_in": nrm(ks[2], (L, D_MODEL, D_IN), D_MODEL ** -0.5),
        "conv_w": nrm(ks[3], (L, CONV_W, D_RNN), CONV_W ** -0.5),
        "conv_b": nrm(ks[4], (L, D_RNN), 0.01),
        "w_r": nrm(ks[5], (L, RNN_BLOCKS, RNN_BW, RNN_BW), RNN_BW ** -0.5),
        "b_r": nrm(ks[6], (L, RNN_BLOCKS, RNN_BW), 0.01),
        "w_i": nrm(ks[7], (L, RNN_BLOCKS, RNN_BW, RNN_BW), RNN_BW ** -0.5),
        "b_i": nrm(ks[8], (L, RNN_BLOCKS, RNN_BW), 0.01),
        "lru_lambda": lru_lambda,
        "q_norm_g": 1.0 + nrm(ks[10], (L, HEAD_DIM), 0.02),
        "k_norm_g": 1.0 + nrm(ks[11], (L, HEAD_DIM), 0.02),
        "w_proj_rnn": nrm(ks[12], (L, D_RNN, D_MODEL), D_RNN ** -0.5),
        "w_proj_attn": nrm(ks[13], (L, D_ATTN, D_MODEL), D_ATTN ** -0.5),
        "w_out": nrm(ks[14], (L, D_MODEL, D_MODEL), D_MODEL ** -0.5),
        "norm2_g": 1.0 + nrm(ks[15], (L, D_MODEL), 0.02),
        "w_up": nrm(ks[16], (L, D_MODEL, D_FF), D_MODEL ** -0.5),
        "w_gate": nrm(ks[17], (L, D_MODEL, D_FF), D_MODEL ** -0.5),
        "ffn_conv_w": nrm(ks[18], (L, FFN_CONV_W, D_FF), FFN_CONV_W ** -0.5),
        "ffn_conv_b": nrm(ks[19], (L, D_FF), 0.01),
        "w_down": nrm(ks[20], (L, D_FF, D_MODEL), D_FF ** -0.5),
    }

def first_block(x, norm1_g, w_in, conv_w, conv_b, w_r, b_r, w_i, b_i, lru_lambda,
              q_norm_g, k_norm_g, w_proj_rnn, w_proj_attn, w_out, norm2_g,
              w_up, w_gate, ffn_conv_w, ffn_conv_b, w_down):
    bsz, s, _ = x.shape
    cuts = np.cumsum([D_RNN, D_RNN, D_ATTN, D_ATTN, D_ATTN])
    for l in range(DEPTH):
        h = rmsnorm(x, norm1_g[l])
        u = jnp.einsum('bsd,de->bse', h, w_in[l])
        x_rnn, g_rnn, q, k, v, g_br = jnp.split(u, list(cuts), axis=-1)
        xa = causal_dwconv(x_rnn, conv_w[l], conv_b[l])
        ya = rg_lru(xa, w_r[l], b_r[l], w_i[l], b_i[l], lru_lambda[l]) * jax.nn.gelu(g_rnn)
        q = rmsnorm(q.reshape(bsz, s, N_HEADS, HEAD_DIM), q_norm_g[l]).transpose(0, 2, 1, 3)
        k = rmsnorm(k.reshape(bsz, s, N_HEADS, HEAD_DIM), k_norm_g[l]).transpose(0, 2, 1, 3)
        v = v.reshape(bsz, s, N_HEADS, HEAD_DIM).transpose(0, 2, 1, 3)
        yb = moba_attention(q, k, v).transpose(0, 2, 1, 3).reshape(bsz, s, D_ATTN)
        gates = jax.nn.sigmoid(g_br).reshape(bsz, s, N_BRANCH, D_MODEL)
        merged = (gates[:, :, 0] * jnp.einsum('bsc,cd->bsd', ya, w_proj_rnn[l])
                  + gates[:, :, 1] * jnp.einsum('bsc,cd->bsd', yb, w_proj_attn[l]))
        x = x + jnp.einsum('bsd,de->bse', merged, w_out[l])
        h = rmsnorm(x, norm2_g[l])
        up = causal_dwconv(jnp.einsum('bsd,df->bsf', h, w_up[l]), ffn_conv_w[l], ffn_conv_b[l])
        act = jax.nn.gelu(up) * jnp.einsum('bsd,df->bsf', h, w_gate[l])
        x = x + jnp.einsum('bsf,fd->bsd', act, w_down[l])
    return x


ROPE_THETA = 10000.0
BLOCK = 128

HEAD_DIM_2 = 64
SWA_HEADS = 8
SWA_KV_HEADS = 2
SWA_GROUP = SWA_HEADS // SWA_KV_HEADS
WINDOW = 128

MLA_HEADS = 8
MLA_NOPE_DIM = 64
MLA_ROPE_DIM = 32
MLA_V_DIM = 64
MLA_QK_DIM = MLA_NOPE_DIM + MLA_ROPE_DIM
Q_LORA_RANK = 384
KV_LORA_RANK = 256

D_FF_2 = -(-8 * D_MODEL // (3 * 256)) * 256

IN_SIZES = [
    SWA_HEADS * HEAD_DIM_2,
    SWA_KV_HEADS * HEAD_DIM_2,
    SWA_KV_HEADS * HEAD_DIM_2,
    Q_LORA_RANK,
    KV_LORA_RANK,
    MLA_ROPE_DIM,
    D_MODEL,
    D_MODEL,
]
IN_WIDTH = int(sum(IN_SIZES))
IN_OFFSETS = [int(v) for v in np.cumsum(IN_SIZES)[:-1]]


def rmsnorm_2(x, g):
    xf = x.astype(jnp.float32)
    xf = xf * lax.rsqrt(jnp.mean(xf * xf, axis=-1, keepdims=True) + EPS)
    return (xf * g.astype(jnp.float32)).astype(x.dtype)

def rope_tables(seq, dim):
    inv = ROPE_THETA ** (-jnp.arange(0, dim, 2, dtype=jnp.float32) / dim)
    ang = jnp.arange(seq, dtype=jnp.float32)[:, None] * inv[None, :]
    return jnp.cos(ang)[:, None, :], jnp.sin(ang)[:, None, :]

def apply_rope(x, cos, sin):
    xf = x.astype(jnp.float32)
    x1, x2 = jnp.split(xf, 2, axis=-1)
    out = jnp.concatenate([x1 * cos - x2 * sin, x2 * cos + x1 * sin], axis=-1)
    return out.astype(x.dtype)

def swa_sink_attention(q, k, v, sinks):
    B, S = q.shape[0], q.shape[1]
    nb = S // BLOCK
    qb = q.reshape(B, nb, BLOCK, SWA_KV_HEADS, SWA_GROUP, HEAD_DIM_2)

    def band(t):
        tp = jnp.pad(t, ((0, 0), (BLOCK, 0), (0, 0), (0, 0)))
        tb = tp.reshape(B, nb + 1, BLOCK, SWA_KV_HEADS, HEAD_DIM_2)
        return jnp.concatenate([tb[:, :-1], tb[:, 1:]], axis=2)

    kw, vw = band(k), band(v)
    s = jnp.einsum('bnqhgd,bnkhd->bnhgqk', qb, kw,
                   preferred_element_type=jnp.float32) * (HEAD_DIM_2 ** -0.5)
    qi = jnp.arange(BLOCK)[:, None]
    kj = jnp.arange(2 * BLOCK)[None, :]
    diff = qi - kj + BLOCK
    band_ok = (diff >= 0) & (diff < WINDOW)
    kpos = jnp.arange(nb)[:, None] * BLOCK + kj - BLOCK
    mask = band_ok[None] & (kpos >= 0)[:, None, :]
    s = jnp.where(mask[None, :, None, None], s, -jnp.inf)
    sink = sinks.astype(jnp.float32).reshape(1, 1, SWA_KV_HEADS, SWA_GROUP, 1, 1)
    m = jnp.maximum(jnp.max(s, axis=-1, keepdims=True), sink)
    p = jnp.exp(s - m)
    denom = jnp.sum(p, axis=-1, keepdims=True) + jnp.exp(sink - m)
    p = (p / denom).astype(v.dtype)
    o = jnp.einsum('bnhgqk,bnkhd->bnqhgd', p, vw)
    return o.reshape(B, S, SWA_HEADS * HEAD_DIM_2)

def mla_attention(q_nope, q_rope, k_nope, k_rope, v):
    B, S = q_nope.shape[0], q_nope.shape[1]
    nb = S // BLOCK
    scale = MLA_QK_DIM ** -0.5
    kpos = jnp.arange(S)

    def to_blocks(t):
        return jnp.moveaxis(t.reshape(B, nb, BLOCK, *t.shape[2:]), 1, 0)

    def one_block(args):
        qn, qr, n = args
        s = (jnp.einsum('bqhd,bkhd->bhqk', qn, k_nope, preferred_element_type=jnp.float32)
             + jnp.einsum('bqhr,bkr->bhqk', qr, k_rope, preferred_element_type=jnp.float32)) * scale
        qpos = n * BLOCK + jnp.arange(BLOCK)
        causal = kpos[None, :] <= qpos[:, None]
        s = jnp.where(causal[None, None], s, -jnp.inf)
        p = jax.nn.softmax(s, axis=-1).astype(v.dtype)
        return jnp.einsum('bhqk,bkhd->bqhd', p, v)

    o = lax.map(one_block, (to_blocks(q_nope), to_blocks(q_rope), jnp.arange(nb)))
    return jnp.moveaxis(o, 0, 1).reshape(B, S, MLA_HEADS * MLA_V_DIM)

def second_inputs(seed: int = 0) -> dict:
    key = jax.random.key(seed)
    ks = jax.random.split(key, 17)
    f32 = jnp.float32

    def w(k, shape, fan_in):
        return jax.random.normal(k, shape, f32) * (fan_in ** -0.5)

    def gain(k, shape):
        return 1.0 + 0.02 * jax.random.normal(k, shape, f32)

    L = DEPTH
    return {
        "x": jax.random.normal(ks[0], (BATCH, SEQ, D_MODEL), f32),
        "mix_norm_g": gain(ks[1], (L, D_MODEL)),
        "w_in": w(ks[2], (L, D_MODEL, IN_WIDTH), D_MODEL),
        "swa_sinks": 0.5 * jax.random.normal(ks[3], (L, SWA_HEADS), f32),
        "q_norm_g": gain(ks[4], (L, Q_LORA_RANK)),
        "w_uq": w(ks[5], (L, Q_LORA_RANK, MLA_HEADS * MLA_QK_DIM), Q_LORA_RANK),
        "kv_norm_g": gain(ks[6], (L, KV_LORA_RANK)),
        "w_ukv": w(ks[7], (L, KV_LORA_RANK, MLA_HEADS * (MLA_NOPE_DIM + MLA_V_DIM)), KV_LORA_RANK),
        "w_o_swa": w(ks[8], (L, SWA_HEADS * HEAD_DIM_2, D_MODEL), SWA_HEADS * HEAD_DIM_2),
        "w_o_mla": w(ks[9], (L, MLA_HEADS * MLA_V_DIM, D_MODEL), MLA_HEADS * MLA_V_DIM),
        "w_out": w(ks[10], (L, D_MODEL, D_MODEL), D_MODEL),
        "ffn_norm_g": gain(ks[11], (L, D_MODEL)),
        "w_gate": w(ks[12], (L, D_MODEL, D_FF_2), D_MODEL),
        "w_up": w(ks[13], (L, D_MODEL, D_FF_2), D_MODEL),
        "w_down": w(ks[14], (L, D_FF_2, D_MODEL), D_FF_2),
        "final_norm_g": gain(ks[15], (D_MODEL,)),
    }

def second_block(x, mix_norm_g, w_in, swa_sinks, q_norm_g, w_uq, kv_norm_g, w_ukv,
              w_o_swa, w_o_mla, w_out, ffn_norm_g, w_gate, w_up, w_down, final_norm_g):
    B, S = x.shape[0], x.shape[1]
    cos_a, sin_a = rope_tables(S, HEAD_DIM_2)
    cos_b, sin_b = rope_tables(S, MLA_ROPE_DIM)

    for l in range(DEPTH):
        h = rmsnorm_2(x, mix_norm_g[l])
        proj = h @ w_in[l]
        qa, ka, va, q_lat, kv_lat, k_r, g_a, g_b = jnp.split(proj, IN_OFFSETS, axis=-1)

        qa = apply_rope(qa.reshape(B, S, SWA_HEADS, HEAD_DIM_2), cos_a, sin_a)
        ka = apply_rope(ka.reshape(B, S, SWA_KV_HEADS, HEAD_DIM_2), cos_a, sin_a)
        va = va.reshape(B, S, SWA_KV_HEADS, HEAD_DIM_2)
        o_a = swa_sink_attention(qa, ka, va, swa_sinks[l])

        cq = rmsnorm_2(q_lat, q_norm_g[l])
        qb = (cq @ w_uq[l]).reshape(B, S, MLA_HEADS, MLA_QK_DIM)
        q_nope, q_rope = jnp.split(qb, [MLA_NOPE_DIM], axis=-1)
        q_rope = apply_rope(q_rope, cos_b, sin_b)
        ckv = rmsnorm_2(kv_lat, kv_norm_g[l])
        kvb = (ckv @ w_ukv[l]).reshape(B, S, MLA_HEADS, MLA_NOPE_DIM + MLA_V_DIM)
        k_nope, vb = jnp.split(kvb, [MLA_NOPE_DIM], axis=-1)
        k_rope = apply_rope(k_r[:, :, None, :], cos_b, sin_b)[:, :, 0, :]
        o_b = mla_attention(q_nope, q_rope, k_nope, k_rope, vb)

        y = jax.nn.sigmoid(g_a) * (o_a @ w_o_swa[l]) + jax.nn.sigmoid(g_b) * (o_b @ w_o_mla[l])
        x = x + y @ w_out[l]

        h = rmsnorm_2(x, ffn_norm_g[l])
        x = x + (jax.nn.silu(h @ w_gate[l]) * (h @ w_up[l])) @ w_down[l]

    return rmsnorm_2(x, final_norm_g)


def setup_inputs(seed=0):
    out = dict(first_inputs(seed))
    for name, value in second_inputs(seed + 1).items():
        if name != "x":
            out[name + "_2"] = value
    return out


def reference(
    x, norm1_g, w_in, conv_w, conv_b, w_r, b_r, w_i, b_i, lru_lambda, q_norm_g, k_norm_g,
    w_proj_rnn, w_proj_attn, w_out, norm2_g, w_up, w_gate, ffn_conv_w, ffn_conv_b, w_down,
    mix_norm_g_2, w_in_2, swa_sinks_2, q_norm_g_2, w_uq_2, kv_norm_g_2, w_ukv_2, w_o_swa_2,
    w_o_mla_2, w_out_2, ffn_norm_g_2, w_gate_2, w_up_2, w_down_2, final_norm_g_2,
):
    x = first_block(
        x, norm1_g, w_in, conv_w, conv_b, w_r, b_r, w_i, b_i, lru_lambda, q_norm_g, k_norm_g,
        w_proj_rnn, w_proj_attn, w_out, norm2_g, w_up, w_gate, ffn_conv_w, ffn_conv_b, w_down,
    )
    return second_block(
        x, mix_norm_g_2, w_in_2, swa_sinks_2, q_norm_g_2, w_uq_2, kv_norm_g_2, w_ukv_2,
        w_o_swa_2, w_o_mla_2, w_out_2, ffn_norm_g_2, w_gate_2, w_up_2, w_down_2, final_norm_g_2,
    )


_drawn_inputs = setup_inputs


def setup_inputs(seed=0):
    import zlib

    import numpy as np

    out = dict(_drawn_inputs(seed))
    spreads = {}
    factors = {'norm1_g': 6.286,
     'conv_b': 3.466,
     'b_r': 8.0,
     'b_i': 8.0,
     'q_norm_g': 8.0,
     'k_norm_g': 8.0,
     'norm2_g': 3.353,
     'ffn_conv_b': 8.0,
     'mix_norm_g_2': 8.0,
     'swa_sinks_2': 165.083,
     'q_norm_g_2': 8.0,
     'kv_norm_g_2': 8.0,
     'ffn_norm_g_2': 13.455,
     'final_norm_g_2': 23.969}
    for name, (base, spread) in spreads.items():
        noise = np.random.default_rng([zlib.crc32(name.encode()), seed]).standard_normal(out[name].shape)
        drawn = base * np.exp(spread * noise) if base else spread * noise
        out[name] = __import__('jax').numpy.asarray(drawn.astype(out[name].dtype))
    for name, factor in factors.items():
        out[name] = (out[name] * factor).astype(out[name].dtype)
    return out
```

```python
import numpy as np
import concourse.bass as bass
from concourse import mybir
from contextlib import ExitStack

P = 128
SEQ = 256
HALVES = SEQ // P
D = 1024
KD = D // P
FF = 2816
FT = FF // P
HEADS = 8
SLAB = 2048
WIDE = SLAB // KD
RING = 3
EPS = 1e-6
NEG = -1e30
KW = 4
FKW = 3
D_IN2 = 3488
SEQ_COLS = 1440
QLAT, KVLAT = 384, 256
OFF_KA, OFF_VA, OFF_QL, OFF_KVL, OFF_KR = 512, 640, 768, 1152, 1408
MLA_D, NOPE, ROPE, VD = 96, 64, 32, 64

G1, CONVW, CONVB, BR, BI, LAM, G2, MIXG, FFNG, QLG, KVLG, QG, KG = (
    0, 8, 40, 48, 56, 64, 72, 80, 88, 96, 99, 101, 102)
PROWS = 103
FROWS = FKW * FT + FT


def slab_plan():
    plan = [("w_in", "cols", WIDE * i) for i in range(8)]
    plan += [("w_ri", "blocks", 0)]
    plan += [("w_in", "cols", WIDE * i) for i in range(8, 28)]
    plan += [(w, "cols", WIDE * i) for w in ("w_proj_rnn", "w_proj_attn", "w_out") for i in range(4)]
    ffn1 = len(plan)
    plan += [("ffn1", "loop", i) for i in range(3 * (FF // WIDE))]
    plan += [("w_in_2", "cols", WIDE * i) for i in range(6)]
    plan += [("w_in_2", "cols", SEQ_COLS + WIDE * i) for i in range(4)]
    plan += [("w_uq_2", "rows3", 0), ("w_uq_2", "rows3", QLAT), ("w_ukv_2", "rows2", 0)]
    plan += [("w_in_2", "cols", SEQ_COLS + WIDE * i) for i in range(4, 8)]
    plan += [("w_o_swa_2", "swa", 512 * i) for i in range(2)]
    plan += [("w_o_mla_2", "rows4", 512 * i) for i in range(2)]
    plan += [("w_out_2", "cols", WIDE * i) for i in range(4)]
    ffn2 = len(plan)
    plan += [("ffn2", "loop", i) for i in range(3 * (FF // WIDE))]
    return plan, ffn1, ffn2


PLAN, FFN1, FFN2 = slab_plan()
SLABS = len(PLAN)
STEPS = FF // WIDE
S_XR, S_G, S_RI, S_Q, S_K, S_V, S_GATE, S_PR, S_PA, S_OUT = 0, 4, 8, 9, 13, 17, 21, 29, 33, 37
S2_SEQ, S2_GA, S2_UQ, S2_UKV, S2_GB = FFN1 + 33, FFN1 + 39, FFN1 + 43, FFN1 + 45, FFN1 + 46
S2_OSWA, S2_OMLA, S2_OUT = FFN1 + 50, FFN1 + 52, FFN1 + 54


def group_plan():
    groups = []
    for s, (_, kind, _) in enumerate(PLAN):
        if kind == "loop":
            if s in (FFN1, FFN2):
                groups += [(s, i, "dve") for i in range(2 * STEPS)]
        elif kind == "blocks":
            groups += [(s, i, "act") for i in range(8)]
        elif S_Q <= s < S_GATE or S2_SEQ <= s < S2_GA:
            groups.append((s, 0, "act"))
        elif S2_UQ <= s < S2_UKV:
            groups += [(s, i, "act") for i in range(2)]
        elif s == S2_UKV:
            groups += [(s, i, "act") for i in range(4)]
        elif S2_OSWA <= s < S2_OUT:
            groups += [(s, i, "dve") for i in range(2)]
        else:
            groups.append((s, 0, "dve"))
    return groups


GROUPS = group_plan()
GROUP_OF = {(s, i): g for g, (s, i, _) in enumerate(GROUPS)}


def emptied(g):
    who = GROUPS[g][2]
    return who, sum(1 for x in GROUPS[:g + 1] if x[2] == who)


LAG_S, LAG_PT, LAG_PV = 1, 3, 4


def steps_at(s):
    if S_GATE <= s < S_PR + LAG_PV:
        return [s - S_GATE]
    if S2_GA <= s < S2_UQ:
        return [100 + 2 * (s - S2_GA) + i for i in range(2)]
    if S2_GB <= s < S2_OSWA + 2:
        return [108 + 2 * (s - S2_GB) + i for i in range(2)]
    return []


def unit_of(step):
    if 0 <= step < HEADS:
        return step
    if 100 <= step < 100 + 2 * HEADS:
        return step - 100 + HEADS
    return None


def program(nc, t):
    f32, f32r = mybir.dt.float32, mybir.dt.float32r
    ALU, ACT, AX = mybir.AluOpType, mybir.ActivationFunctionType, mybir.AxisListType.X
    with ExitStack() as ctx:
        def sb(name, shape, dt=f32):
            return ctx.enter_context(nc.sbuf_tensor(name, shape, dt))

        def sem(name):
            return ctx.enter_context(nc.semaphore(name))

        raw = [sb(f"raw{i}", [P, SLAB]) for i in range(RING)]
        whi = [sb(f"whi{i}", [P, SLAB], f32r) for i in range(RING)]
        wlo = [sb(f"wlo{i}", [P, SLAB], f32r) for i in range(RING)]
        pairs = [(sb(f"ahi{i}", [P, KD, SEQ], f32r), sb(f"alo{i}", [P, KD, SEQ], f32r)) for i in range(3)]
        X = sb("x_res", [P, KD, SEQ])
        XA = sb("xa", [P, SLAB])
        GG = sb("gg", [P, SLAB])
        VV = sb("vv", [P, SLAB])
        T0 = sb("gate0", [P, KD, SEQ])
        T1 = sb("gate1", [P, KD, SEQ])
        QK = sb("qk", [P, 2 * SLAB])
        qT = sb("qT", [P, 2, SEQ])
        kT = sb("kT", [P, 2, SEQ])
        sm = sb("sm", [P, 2, 3 * P])
        pr = sb("pr", [P, 3, 3 * P])
        pT = sb("pT", [P, 2, 3 * P])
        masks = sb("masks", [P, 2, 3 * P])
        ident = sb("ident", [P, P])
        ones = sb("ones", [P, P])
        pcol = sb("pcol", [P, PROWS])
        fcol = sb("fcol", [P, FROWS])
        halfb = sb("halfb", [P, 16])
        sp = sb("sp", [P, 8, KD])
        qkg = sb("qkg", [P, 1])
        epst = sb("epst", [P, 1])
        ropeA = sb("ropeA", [P, 2, HALVES, 32])
        ropeB = sb("ropeB", [P, 2, HALVES, 16])
        krr = sb("krr", [P, HALVES, ROPE])
        sinks = sb("sinks", [P, 2, HEADS])
        rowt = sb("rowt", [1, HEADS])
        root = sb("root", [P, SEQ])
        root2 = sb("root2", [P, 2])
        rstd_bc = sb("rstd_bc", [P, SEQ])
        rstd_sq = sb("rstd_sq", [P, 2])
        ssqk = sb("ssqk", [P, 2, HALVES, HEADS])
        rqk = sb("rqk", [P, 2, HALVES, HEADS])
        cq = sb("cq", [P, 2, HALVES, HEADS])
        ss2 = sb("ss2", [P, 2, 2])
        r2 = sb("r2", [P, 2, 2])
        mx = sb("mx", [P, 2, 2])
        nb = sb("nb", [P, 3, 2])
        sums = sb("sums", [P, 3, 2])
        esink = sb("esink", [P, 3, 2])
        rinv = sb("rinv", [P, 2, 2])
        junk = pT[:, 0, :]
        fin = sb("fin", [P, 4])

        xpos = GG[:, :].rearrange("p (h d) -> p h d", h=HALVES)
        prow = QK[:, 0:P]
        frow = QK[:, P:2 * P]
        SQ = VV[:, :].rearrange("p (k n) -> p k n", k=KD)
        xrp = QK[:, 1024:1024 + 2 * (SEQ + KW - 1)].rearrange("p (m n) -> p m n", m=2)
        xa = XA[:, :].rearrange("p (k n) -> p k n", k=KD)
        gg = GG[:, :].rearrange("p (k n) -> p k n", k=KD)
        q_s = QK[:, 0:SLAB].rearrange("p (h d) -> p h d", h=HALVES)
        k_s = QK[:, SLAB:2 * SLAB].rearrange("p (h d) -> p h d", h=HALVES)
        v_s = VV[:, :].rearrange("p (h d) -> p h d", h=HALVES)
        rnn_t = pr[:, :, :].rearrange("p a n -> p (a n)")[:, 0:4 * SEQ].rearrange("p (a n) -> p a n", a=4)
        rnn_sq = sm[:, :, :].rearrange("p a n -> p (a n)")[:, 0:2 * SEQ].rearrange("p (a n) -> p a n", a=2)
        rope_t = T1[:, 0:4, :]
        u2 = QK[:, 0:HALVES * SEQ_COLS].rearrange("p (h d) -> p h d", h=HALVES)
        vb = QK[:, HALVES * SEQ_COLS:HALVES * SEQ_COLS + HALVES * HEADS * VD].rearrange(
            "p (h d) -> p h d", h=HALVES)
        q_r = VV[:, 0:1024].rearrange("p (h d) -> p h d", h=HALVES)
        k_r = VV[:, 1024:1280].rearrange("p (h d) -> p h d", h=HALVES)
        qb = XA[:, 0:HALVES * HEADS * MLA_D].rearrange("p (h n d) -> p h n d", h=HALVES, n=HEADS)
        qbf = XA[:, 0:HALVES * HEADS * MLA_D].rearrange("p (h d) -> p h d", h=HALVES)
        kf = GG[:, 0:HALVES * HEADS * MLA_D].rearrange("p (h n d) -> p h n d", h=HALVES, n=HEADS)
        upn = QK[:, 0:2 * (SEQ + FKW - 1)].rearrange("p (m n) -> p m n", m=2)
        cv = QK[:, 1024:1536].rearrange("p (m n) -> p m n", m=2)
        gt = QK[:, 1536:2048].rearrange("p (m n) -> p m n", m=2)
        actf = QK[:, 2048:2560].rearrange("p (m n) -> p m n", m=2)
        acthi, actlo = pairs[1][0][:, 0:2, :], pairs[1][1][:, 0:2, :]
        fing = T0[:, 0:4, :].rearrange("p k n -> p (k n)")
        frow_g = QK[0:1, 3072:4096]
        outp = GG[:, :].rearrange("p (h d) -> p h d", h=HALVES)

        ps = [ctx.enter_context(nc.psum_tensor(f"ps{i}", [P, 512], f32)) for i in range(8)]
        PST, PSS, PSPT, PSPV, PSA, PSB = ps[2], ps[3], ps[4], ps[5], ps[6], ps[7]

        in_x, in_par, in_misc, out_done = sem("in_x"), sem("in_par"), sem("in_misc"), sem("out_done")
        raw_in = [sem(f"raw_in{i}") for i in range(RING)]
        hi_ready, lo_ready, down_used = sem("hi_ready"), sem("lo_ready"), sem("down_used")
        group_done = sem("group_done")
        bank_free = {"act": sem("bank_free_act"), "dve": sem("bank_free_dve")}
        act_step, dve_step = sem("act_step"), sem("dve_step")
        dve_loop = [sem("dve_loop0"), sem("dve_loop1")]
        par_T, par_ready, sp_exp, consts = sem("par_T"), sem("par_ready"), sem("sp_exp"), sem("consts")
        sp_in, sp_ready = sem("sp_in"), sem("sp_ready")
        xT_done, x_ready = sem("xT_done"), sem("x_ready")
        h_hi, h_lo, sq_ready, ssum, rms_root, rstd_ready = (
            sem(n) for n in ("h_hi", "h_lo", "sq_ready", "ssum", "rms_root", "rstd_ready"))
        xa_ready, xa_hi, xa_lo = sem("xa_ready"), sem("xa_hi"), sem("xa_lo")
        g_ready = sem("g_ready")
        t_ready, sqt_ready, ya_ready, ya_hi, ya_lo = (
            sem(n) for n in ("t_ready", "sqt_ready", "ya_ready", "ya_hi", "ya_lo"))
        qk_ss, qk_scaled, v_ready = sem("qk_ss"), sem("qk_scaled"), sem("v_ready")
        gate_t = sem("gate_t")
        aT, aTe, aS, aM, aE, aN, aPT, aPTe, aPV, aH, aL = (sem(n) for n in (
            "att_T", "att_T_out", "att_S", "att_max", "att_exp", "att_norm", "att_PT", "att_PT_out",
            "att_PV", "yb_hi", "yb_lo"))
        merged, m_hi, m_lo = sem("merged"), sem("m_hi"), sem("m_lo")
        rope_q, cq_ss, cq_r, cq_s, cq_T, cq_hi, cq_lo = (sem(n) for n in (
            "rope_q", "cq_ss", "cq_r", "cq_scaled", "cq_T", "cq_hi", "cq_lo"))
        qb_ready, kv_ready, mla_ready, rope_k = sem("qb_ready"), sem("kv_ready"), sem("mla_ready"), sem("rope_k")
        sink_T, sink_ready = sem("sink_T"), sem("sink_ready")
        f_conv, f_glu, f_act, f_hi, f_lo = (sem(n) for n in ("f_conv", "f_glu", "f_act", "f_hi", "f_lo"))
        fin_T, fin_ready, fin_ss, fin_root, y_ready = (
            sem(n) for n in ("fin_T", "fin_ready", "fin_ss", "fin_root", "y_ready"))
        block = ctx.enter_context(nc.Block())

        U2_FREE = [emptied(GROUP_OF[(s, 0)])[1] for s in range(S2_SEQ, S2_GA)]

        def used_value(s):
            base = FFN2 if s >= FFN2 else FFN1
            if base <= s < base + 3 * STEPS:
                i = s - base
                n0 = 0 if base == FFN1 else STEPS
                if i < 2:
                    return group_done, GROUP_OF[(base, 0)] + i + 1
                j, kind = divmod(i - 2, 3)
                if i == 3 * STEPS - 1 or kind == 2:
                    return down_used, n0 + (STEPS if i == 3 * STEPS - 1 else j + 1)
                return group_done, GROUP_OF[(base, 0)] + 2 * (j + 1) + kind + 1
            return group_done, max(g for (x, _), g in GROUP_OF.items() if x == s) + 1

        def x_value(n, c):
            if n % 2 == 0:
                return x_ready, 2 * n + c // 2 + 1
            return bank_free["dve"], emptied(GROUP_OF[((S_OUT if n == 1 else S2_OUT) + c // 2, 0)])[1]

        def raw_value(s):
            return 32 * (s // RING + 1)

        @block.sync
        def _(sp_eng):
            e = sp_eng
            e.dma_start(xpos, t["x"][0].rearrange("(h p) d -> p h d", p=P)).then_inc(in_x, 16)
            e.dma_start(ident[:, :], t["ident"]).then_inc(in_x, 16)

            def halves(slot, src_of, view):
                for a in range(2):
                    e.dma_start(view[64 * a:64 * a + 64], src_of(a)).then_inc(raw_in[slot], 16)

            def load(s):
                name, kind, arg = PLAN[s]
                slot = s % RING
                if s >= RING:
                    e.wait_ge(lo_ready, s - RING + 1)
                r = raw[slot]
                if kind == "blocks":
                    for i, w in enumerate(("w_r", "w_i")):
                        e.dma_start(r[:, 1024 * i:1024 * i + 1024].rearrange("p (n d) -> p n d", n=8),
                                    t[w][0].rearrange("n c d -> c n d")).then_inc(raw_in[slot], 16)
                    return
                w = t[name][0]
                if kind == "cols":
                    width = min(WIDE, w.shape[1] - arg)
                    view = r[:, :].rearrange("p (k n) -> p k n", k=KD)[:, :, 0:width]
                    src = w.rearrange("(k a p) n -> a p k n", a=2, p=64)
                    halves(slot, lambda a: src[a][:, :, arg:arg + width], view)
                elif kind == "swa":
                    view = r[:, :].rearrange("p (k n) -> p k n", k=4)
                    src = w.rearrange("(a k p) n -> a p k n", a=2, p=64)
                    halves(slot, lambda a: src[a][:, :, arg:arg + 512], view)
                else:
                    k, width = {"rows4": (4, 512), "rows3": (3, QLAT), "rows2": (2, 1024)}[kind]
                    view = r[:, 0:k * width].rearrange("p (k n) -> p k n", k=k)
                    src = w.rearrange("(k a p) n -> a p k n", a=2, p=64)
                    halves(slot, lambda a: src[a][:, :, arg:arg + width], view)

            def load_cols(s, slot, name, j, free=True):
                if free:
                    e.wait_ge(lo_ready, s - RING + 1)
                src = t[name][0].rearrange("(k a p) n -> a p k n", a=2, p=64)
                view = raw[slot][:, :].rearrange("p (k n) -> p k n", k=KD)
                halves(slot, lambda a: src[a][:, :, bass.ts(j, WIDE)], view)

            def load_down(s, slot, name, j):
                e.wait_ge(lo_ready, s - RING + 1)
                src = t[name][0].rearrange("(j k a p) n -> a p j k n", k=2, a=2, p=64)
                view = raw[slot][:, :].rearrange("p (k n) -> p k n", k=2)
                halves(slot, lambda a: src[a][:, j], view)

            def ffn(base, up, gate, down):
                load_cols(base, base % RING, up, 0)
                load_cols(base + 1, (base + 1) % RING, gate, 0)
                with e.Fori(1, STEPS) as j:
                    s = j * 3 + (base - 1)
                    load_cols(s, (base + 2) % RING, up, j)
                    load_cols(s + 1, base % RING, gate, j)
                    load_down(s + 2, (base + 1) % RING, down, j - 1)
                load_down(base + 3 * STEPS - 1, (base + 3 * STEPS - 1) % RING, down, STEPS - 1)

            load(0)
            rows = [(G1, "norm1_g", 8), (CONVB, "conv_b", 8), (BR, "b_r", 8),
                    (BI, "b_i", 8), (LAM, "lru_lambda", 8), (G2, "norm2_g", 8), (MIXG, "mix_norm_g_2", 8),
                    (FFNG, "ffn_norm_g_2", 8), (QLG, "q_norm_g_2", 3), (KVLG, "kv_norm_g_2", 2),
                    (QG, "q_norm_g", 1), (KG, "k_norm_g", 1)]
            for r0, name, n in rows:
                src = t[name][0] if name in ("b_r", "b_i") else t[name][0].rearrange("(k p) -> k p", p=P)
                e.dma_start(prow[r0:r0 + n, :], src).then_inc(in_par, 16)
            e.dma_start(prow[CONVW:CONVW + KW * KD, :],
                        t["conv_w"][0].rearrange("w (k p) -> (w k) p", p=P)).then_inc(in_par, 16)
            e.dma_start(frow[0:FKW * FT, :],
                        t["ffn_conv_w"][0].rearrange("w (k p) -> (w k) p", p=P)).then_inc(in_par, 16)
            e.dma_start(frow[FKW * FT:FROWS, :],
                        t["ffn_conv_b"][0].rearrange("(k p) -> k p", p=P)).then_inc(in_par, 16)
            load(1)
            load(2)
            e.dma_start(masks[:, :, :], t["masks"]).then_inc(in_misc, 16)
            for c in range(2):
                e.dma_start(ropeA[:, c], t["rope_a"][c].rearrange("(h p) d -> p h d", p=P)).then_inc(in_misc, 16)
                e.dma_start(ropeB[:, c], t["rope_b"][c].rearrange("(h p) d -> p h d", p=P)).then_inc(in_misc, 16)
            e.dma_start(rowt[:, :], t["swa_sinks_2"]).then_inc(in_misc, 16)
            for s in range(RING, FFN1):
                load(s)
            ffn(FFN1, "w_up", "w_gate", "w_down")
            for s in range(S2_SEQ, FFN2):
                load(s)
            ffn(FFN2, "w_up_2", "w_gate_2", "w_down_2")
            e.wait_ge(lo_ready, SLABS)
            e.wait_ge(f_act, 2 * STEPS)
            e.dma_start(frow_g, t["final_norm_g"].rearrange("(a n) -> a n", a=1)).then_inc(in_x, 16)
            for h in range(HALVES):
                e.wait_ge(y_ready, h + 1)
                e.dma_start(t["out"][0][P * h:P * h + P, :], outp[:, h, :]).then_inc(out_done, 16)
            e.wait_ge(out_done, 16 * HALVES)

        @block.scalar
        def _(e):
            count = [0]

            def link(ins):
                count[0] += 1
                ins.then_inc(act_step, 1)
                e.wait_ge(act_step, count[0])

            def hi(slot, raw_v, used):
                e.wait_ge(raw_in[slot], raw_v)
                if used:
                    e.wait_ge(*used)
                e.activation(whi[slot][:, :], raw[slot][:, :], ACT.Copy).then_inc(hi_ready, 1)

            def pre(s):
                if s < SLABS:
                    hi(s % RING, raw_value(s), used_value(s - RING) if s >= RING else None)

            def free_bank(ins):
                ins.then_inc(bank_free["act"], 1)

            def norm(n, pair, g0, h_dst, seq):
                for c in range(KD):
                    e.wait_ge(*x_value(n, c))
                    e.activation(h_dst[:, c, :], X[:, c, :], ACT.Copy,
                                 scale=pcol[:, g0 + c:g0 + c + 1]).then_inc(h_hi, 1)
                for c in range(2):
                    e.activation(SQ[:, 4 * c:4 * c + 4, :], X[:, 4 * c:4 * c + 4, :], ACT.Square).then_inc(sq_ready, 1)

            def roots(n, seq):
                e.wait_ge(ssum, n + 1)
                if seq:
                    e.activation(root2[:, :], PSB[:, 0:2], ACT.Sqrt, bias=epst[:, :], scale=1.0 / D)
                e.activation(root[:, :], PSA[:, 0:SEQ], ACT.Sqrt, bias=epst[:, :], scale=1.0 / D).then_inc(rms_root, 1)

            def att(step):
                kind_base = 0 if step < 100 else 100
                u = unit_of(step)
                if u is not None and not (8 <= u < 16 and u % 2):
                    n_t = t_count(u)
                    b = tbuf(u)
                    e.wait_ge(aT, n_t)
                    if n_t > 2:
                        e.wait_ge(aS, last_reader_of_tbuf(u))
                    d = MLA_D if u >= 16 else P
                    e.activation(qT[0:d, b, :], PST[0:d, 0:SEQ], ACT.Copy)
                    e.activation(kT[0:d, b, :], PST[0:d, SEQ:2 * SEQ], ACT.Copy,
                                 **({"scale": qkg[:, :]} if u < 8 else {})).then_inc(aTe, 1)
                u = unit_of(step - LAG_PT) if step - LAG_PT >= kind_base else None
                if u is not None:
                    e.wait_ge(aPT, u + 1)
                    if u >= 2:
                        e.wait_ge(aPV, u - 1)
                    e.activation(pT[:, u % 2, :], PSPT[:, 0:3 * P], ACT.Copy).then_inc(aPTe, 1)
                u = unit_of(step - LAG_PV) if step - LAG_PV >= kind_base else None
                if u is not None:
                    e.wait_ge(aPV, u + 1)
                    rows, chunk = yb_place(u)
                    e.activation(pairs[2][0][rows, chunk, :], PSPV[rows, 0:SEQ], ACT.Copy).then_inc(aH, 1)
                u = unit_of(step - LAG_S) if step - LAG_S >= kind_base else None
                if u is not None:
                    e.wait_ge(aM, u + 1)
                    if u >= 3:
                        e.wait_ge(aPT, u - 2)
                    for h in range(HALVES):
                        cols = slice(0, P) if h == 0 else slice(P, 3 * P)
                        if u < 8:
                            scale = cq[:, 0, h, u:u + 1]
                        else:
                            scale = (64 ** -0.5) if u < 16 else MLA_D ** -0.5
                        ins = e.activation(pr[:, u % 3, cols], sm[:, u % 2, cols], ACT.Exp,
                                           bias=nb[:, u % 3, h:h + 1], scale=scale,
                                           accum_out=sums[:, u % 3, h:h + 1])
                    if 8 <= u < 16:
                        hd = swa_head(u)
                        ins = e.activation(esink[:, u % 3, :], nb[:, u % 3, :], ACT.Exp,
                                           bias=sinks[:, 0, hd:hd + 1])
                    ins.then_inc(aE, 1)

            e.wait_ge(par_T, 1)
            e.wait_ge(consts, 1)
            e.activation(pcol[:, :], PSA[:, 0:PROWS], ACT.Copy)
            e.activation(fcol[:, :], PSB[:, 0:FROWS], ACT.Copy).then_inc(par_ready, 1)
            e.wait_ge(par_ready, 1)
            pre(0)
            norm(0, 0, G1, pairs[0][0], True)
            e.wait_ge(sp_in, 1)
            e.activation(sp[:, 1, :], sp[:, 0, :], ACT.Exp, scale=-1.0).then_inc(sp_exp, 1)
            pre(1)
            pre(2)
            roots(0, True)
            for s in range(S_XR, S_G):
                pre(s + 3)
                e.wait_ge(xa_ready, s + 1)
                e.activation(pairs[1][0][:, 2 * s:2 * s + 2, :], xa[:, 2 * s:2 * s + 2, :], ACT.Copy).then_inc(xa_hi, 1)
            for s in range(S_G, S_RI):
                pre(s + 3)
                i = s - S_G
                e.wait_ge(bank_free["dve"], s + 1)
                e.activation(gg[:, 2 * i:2 * i + 2, :], gg[:, 2 * i:2 * i + 2, :], ACT.Gelu_apprx_tanh).then_inc(g_ready, 1)
            for i in range(8):
                g = GROUP_OF[(S_RI, i)]
                e.wait_ge(group_done, g + 1)
                for m in range(2):
                    blk = 2 * (i % 4) + m
                    dst = (T0 if i < 4 else T1)[:, blk, :]
                    ins = e.activation(dst, ps[g % 2][:, SEQ * m:SEQ * m + SEQ], ACT.Tanh, scale=0.5,
                                       bias=halfb[:, 8 * (i // 4) + blk:8 * (i // 4) + blk + 1])
                free_bank(ins)
            e.wait_ge(bank_free["act"], 8)
            e.wait_ge(sp_ready, 1)
            pre(S_RI + 3)
            for m in range(KD):
                e.activation(T0[:, m, :], T0[:, m, :], ACT.Tanh, scale=sp[:, 7, m:m + 1],
                             bias=sp[:, 7, m:m + 1]).then_inc(t_ready, 1)
            e.wait_ge(t_ready, KD)

            def evac_qkv(s, dst, i):
                g = GROUP_OF[(s, 0)]
                e.wait_ge(group_done, g + 1)
                for h in range(HALVES):
                    ins = e.activation(dst[:, h, WIDE * i:WIDE * i + WIDE], ps[g % 2][:, 256 * h:256 * h + 256],
                                       ACT.Copy, scale=rstd_sq[:, h:h + 1])
                free_bank(ins)
                e.wait_ge(bank_free["act"], emptied(g)[1])

            def rnn_chunk(m):
                if m < KD:
                    if m >= 2:
                        e.wait_ge(ya_ready, m - 1)
                    e.activation(rnn_sq[:, m % 2, :], T0[:, m, :], ACT.Sqrt).then_inc(sqt_ready, 1)
                if m >= 1:
                    e.wait_ge(ya_ready, m)
                    e.activation(pairs[1][0][:, m - 1, :], rnn_t[:, 2 + (m - 1) % 2, :], ACT.Copy).then_inc(ya_hi, 1)

            for s in range(S_Q, S_V):
                pre(s + 3)
                which, i = divmod(s - S_Q, 4)
                dst = (q_s, k_s)[which]
                evac_qkv(s, dst, i)
                for h in range(HALVES):
                    for hd in (2 * i, 2 * i + 1):
                        e.activation(junk[:, 0:P], dst[:, h, P * hd:P * hd + P], ACT.Square,
                                     accum_out=ssqk[:, which, h, hd:hd + 1]).then_inc(act_step, 1)
                        count[0] += 1
                        e.wait_ge(act_step, count[0])
                rnn_chunk(s - S_Q)
            e.activation(rqk[:, :, :, :], ssqk[:, :, :, :], ACT.Sqrt, bias=epst[:, :], scale=1.0 / P).then_inc(qk_ss, 1)
            for s in range(S_V, S_GATE):
                pre(s + 3)
                if s == S_V:
                    rnn_chunk(KD)
                evac_qkv(s, v_s, s - S_V)
            e.wait_ge(bank_free["act"], emptied(GROUP_OF[(S_GATE - 1, 0)])[1])

            def gate_tile(i):
                return (T0 if i < 4 else T1)[:, 2 * (i % 4):2 * (i % 4) + 2, :]

            def merge_parts(first, n0):
                def run(i):
                    e.wait_ge(merged, n0 + i + 1)
                    e.activation(pairs[0][0][:, 2 * i:2 * i + 2, :], T0[:, 2 * i:2 * i + 2, :], ACT.Copy,
                                 scale=0.5).then_inc(m_hi, 1)
                return run

            mp = merge_parts(S_PA, 0)
            for s in range(S_GATE, FFN1):
                for step in steps_at(s):
                    att(step)
                pre(s + 3)
                if s < S_PR:
                    i = s - S_GATE
                    e.wait_ge(bank_free["dve"], emptied(GROUP_OF[(s, 0)])[1])
                    e.activation(gate_tile(i), gate_tile(i), ACT.Tanh, scale=0.5).then_inc(gate_t, 1)
                if S_PA <= s < S_OUT:
                    mp(s - S_PA)

            def ffn(which, base, n0, func, norm_args):
                norm(*norm_args)
                g_up = GROUP_OF[(base, 0)]
                free0 = emptied(g_up)[1]

                def post(j, pre_a, pre_b, pre_c):
                    pre_a()
                    pre_b()
                    if which == 1:
                        e.wait_ge(f_conv, j + 1)
                    else:
                        e.wait_ge(bank_free["dve"], j * 2 + (free0 + 1))
                    buf = cv if which == 1 else gt
                    e.activation(buf, buf, func).then_inc(f_glu, 1)
                    pre_c()
                    e.wait_ge(f_act, j + (n0 + 1))
                    if not (isinstance(j, int) and j == 0):
                        e.wait_ge(down_used, j + n0)
                    e.activation(acthi, actf, ACT.Copy).then_inc(f_hi, 1)

                roots(which * 2 - 1, False)
                post(0, lambda: pre(base + 3), lambda: pre(base + 4), lambda: None)

                def hi_at(j, off):
                    used = (down_used, j + n0) if off == 4 else (group_done, j * 2 + (g_up + off - 1))
                    hi((base + off) % RING, j * 32 + 32 * ((base + off) // RING + 1), used)

                with e.Fori(1, STEPS - 1) as j:
                    post(j, lambda: hi_at(j, 2), lambda: hi_at(j, 3), lambda: hi_at(j, 4))
                last = base + 3 * (STEPS - 1) - 1
                post(STEPS - 1, lambda: pre(last + 3), lambda: pre(last + 4), lambda: pre(last + 5))
                pre(base + 3 * STEPS + 2)

            ffn(1, FFN1, 0, ACT.Gelu_apprx_tanh, (1, 2, G2, pairs[2][0], False))

            norm(2, 0, MIXG, pairs[0][0], True)
            roots(2, True)
            e.wait_ge(rstd_ready, 3)
            for s in range(S2_SEQ, S2_GA):
                pre(s + 3)
                g = GROUP_OF[(s, 0)]
                i = s - S2_SEQ
                width = min(WIDE, SEQ_COLS - WIDE * i)
                e.wait_ge(group_done, g + 1)
                for h in range(HALVES):
                    ins = e.activation(u2[:, h, WIDE * i:WIDE * i + width], ps[g % 2][:, 256 * h:256 * h + width],
                                       ACT.Copy, scale=rstd_sq[:, h:h + 1])
                free_bank(ins)
            e.wait_ge(bank_free["act"], U2_FREE[5])
            for h in range(HALVES):
                link(e.activation(junk[:, 0:QLAT], u2[:, h, OFF_QL:OFF_QL + QLAT], ACT.Square,
                                  accum_out=ss2[:, 0, h:h + 1]))
                link(e.activation(junk[:, 0:KVLAT], u2[:, h, OFF_KVL:OFF_KVL + KVLAT], ACT.Square,
                                  accum_out=ss2[:, 1, h:h + 1]))
            e.activation(r2[:, 0, :], ss2[:, 0, :], ACT.Sqrt, bias=epst[:, :], scale=1.0 / QLAT)
            e.activation(r2[:, 1, :], ss2[:, 1, :], ACT.Sqrt, bias=epst[:, :], scale=1.0 / KVLAT).then_inc(cq_ss, 1)
            e.wait_ge(cq_r, 1)
            for h in range(HALVES):
                e.activation(u2[:, h, OFF_QL:OFF_QL + QLAT], u2[:, h, OFF_QL:OFF_QL + QLAT], ACT.Copy,
                             scale=ss2[:, 0, h:h + 1])
                ins = e.activation(u2[:, h, OFF_KVL:OFF_KVL + KVLAT], u2[:, h, OFF_KVL:OFF_KVL + KVLAT], ACT.Copy,
                                   scale=ss2[:, 1, h:h + 1])
            ins.then_inc(cq_s, 1)
            mp2 = merge_parts(S2_OMLA, 4)
            for s in range(S2_GA, FFN2):
                for step in steps_at(s):
                    att(step)
                if s != S2_UKV:
                    pre(s + 3)
                if s < S2_UQ or S2_GB <= s < S2_OSWA:
                    i = s - S2_GA if s < S2_UQ else s - S2_GB + 4
                    e.wait_ge(bank_free["dve"], emptied(GROUP_OF[(s, 0)])[1])
                    e.activation(gate_tile(i), gate_tile(i), ACT.Tanh, scale=0.5).then_inc(gate_t, 1)
                if s == S2_GA:
                    for r in range(3):
                        e.wait_ge(cq_T, r + 1)
                        for c in ((0, 1), (2, 3), (4,))[r]:
                            e.activation(pairs[1][0][:, c, :], (PSA, PSB, PSA)[r][:, SEQ * (c % 2):SEQ * (c % 2) + SEQ],
                                         ACT.Copy, scale=pcol[:, QLG + c:QLG + c + 1]).then_inc(cq_hi, 1)
                if S2_UQ <= s < S2_UKV:
                    for h in range(HALVES):
                        g = GROUP_OF[(s, h)]
                        e.wait_ge(group_done, g + 1)
                        i = s - S2_UQ
                        free_bank(e.activation(qbf[:, h, QLAT * i:QLAT * i + QLAT], ps[g % 2][:, 0:QLAT], ACT.Copy))
                if s == S2_UKV:
                    for i in range(4):
                        g = GROUP_OF[(s, i)]
                        h, c = divmod(i, 2)
                        e.wait_ge(group_done, g + 1)
                        src = ps[g % 2][:, :].rearrange("p (n d) -> p n d", n=4)
                        e.activation(kf[:, h, 4 * c:4 * c + 4, 0:NOPE], src[:, :, 0:NOPE], ACT.Copy)
                        free_bank(e.activation(
                            vb[:, h, 4 * VD * c:4 * VD * c + 4 * VD].rearrange("p (n d) -> p n d", n=4),
                            src[:, :, NOPE:P], ACT.Copy))
                    pre(s + 3)
                if S2_OMLA <= s < S2_OUT:
                    for i in range(2):
                        mp2(2 * (s - S2_OMLA) + i)
            ffn(2, FFN2, STEPS, ACT.Silu, (3, 2, FFNG, pairs[2][0], False))
            for h in range(HALVES):
                e.wait_ge(fin_ready, h + 1)
                e.activation(VV[:, 0:D], outp[:, h, :], ACT.Square, accum_out=fin[:, h:h + 1]).then_inc(fin_ss, 1)
                e.wait_ge(fin_ss, h + 1)
            e.activation(fin[:, 2:4], fin[:, 0:2], ACT.Sqrt, bias=epst[:, :], scale=1.0 / D).then_inc(fin_root, 1)

        @block.vector
        def _(e):
            count = [0]

            def link(ins):
                count[0] += 1
                ins.then_inc(dve_step, 1)
                e.wait_ge(dve_step, count[0])

            def lo(s, slot):
                e.wait_ge(hi_ready, s + 1)
                e.tensor_tensor(wlo[slot][:, :], raw[slot][:, :], whi[slot][:, :].bitcast(f32),
                                ALU.subtract).then_inc(lo_ready, 1)

            def pre(s):
                if s < SLABS:
                    lo(s, s % RING)

            def bc2(ap, n):
                return ap.unsqueeze(1).to_broadcast([P, n, SEQ])

            def norm(n, g0, lo_dst, hi_src):
                for c in range(KD):
                    e.wait_ge(*x_value(n, c))
                    e.wait_ge(h_hi, KD * n + c + 1)
                    e.scalar_tensor_tensor(lo_dst[:, c, :], X[:, c, :], pcol[:, g0 + c:g0 + c + 1],
                                           hi_src[:, c, :].bitcast(f32), ALU.mult, ALU.subtract).then_inc(h_lo, 1)

            def inv(n, seq):
                e.wait_ge(rms_root, n + 1)
                if seq:
                    e.reciprocal(rstd_sq[:, :], root2[:, :])
                e.reciprocal(rstd_bc[:, :], root[:, :]).then_inc(rstd_ready, 1)
                e.wait_ge(rstd_ready, n + 1)

            def normed(g, dst):
                e.wait_ge(group_done, g + 1)
                e.tensor_tensor(dst, ps[g % 2][:, :].rearrange("p (m n) -> p m n", m=2), bc2(rstd_bc[:, :], 2),
                                ALU.mult).then_inc(bank_free["dve"], 1)

            def att(step):
                kind_base = 0 if step < 100 else 100
                u = unit_of(step - LAG_S) if step - LAG_S >= kind_base else None
                ul = unit_of(step - LAG_PV) if step - LAG_PV >= kind_base else None
                if u is not None:
                    e.wait_ge(aS, u + 1)
                    if u >= 2:
                        e.wait_ge(aE, u - 1)
                    link(e.tensor_tensor(sm[:, u % 2, :], PSS[:, 0:3 * P],
                                         masks[:, 1 if 8 <= u < 16 else 0, :], ALU.add))
                    e.reduce_max(mx[:, u % 2, 0:1], sm[:, u % 2, 0:P], AX)
                    link(e.reduce_max(mx[:, u % 2, 1:2], sm[:, u % 2, P:3 * P], AX))
                    if u < 8:
                        e.tensor_tensor(nb[:, u % 3, :], mx[:, u % 2, :], cq[:, 1, :, u], ALU.mult).then_inc(aM, 1)
                    elif u < 16:
                        hd = swa_head(u)
                        e.tensor_scalar(nb[:, u % 3, :], mx[:, u % 2, :], -(64 ** -0.5), sinks[:, 1, hd:hd + 1],
                                        ALU.mult, ALU.min).then_inc(aM, 1)
                    else:
                        e.tensor_scalar(nb[:, u % 3, :], mx[:, u % 2, :], -(MLA_D ** -0.5), None,
                                        ALU.mult).then_inc(aM, 1)
                if ul is not None:
                    e.wait_ge(aH, ul + 1)
                    rows, chunk = yb_place(ul)
                    e.tensor_tensor(pairs[2][1][rows, chunk, :], PSPV[rows, 0:SEQ],
                                    pairs[2][0][rows, chunk, :].bitcast(f32), ALU.subtract).then_inc(aL, 1)
                if u is not None:
                    e.wait_ge(aE, u + 1)
                    if 8 <= u < 16:
                        link(e.tensor_tensor(sums[:, u % 3, :], sums[:, u % 3, :], esink[:, u % 3, :], ALU.add))
                    link(e.reciprocal(rinv[:, u % 2, :], sums[:, u % 3, :]))
                    e.tensor_scalar(pr[:, u % 3, 0:P], pr[:, u % 3, 0:P], rinv[:, u % 2, 0:1], None, ALU.mult)
                    e.tensor_scalar(pr[:, u % 3, P:3 * P], pr[:, u % 3, P:3 * P], rinv[:, u % 2, 1:2], None,
                                    ALU.mult).then_inc(aN, 1)

            e.memset(epst[:, :], EPS)
            e.memset(xrp[:, :, 0:KW - 1], 0.0)
            e.memset(ones[:, :], 1.0).then_inc(consts, 1)
            for b in range(4):
                e.wait_ge(xT_done, b + 1)
                e.tensor_copy(X[:, 2 * b:2 * b + 2, :],
                              ps[2 + b][:, :].rearrange("p (m n) -> p m n", m=2)).then_inc(x_ready, 1)
            e.wait_ge(par_ready, 1)
            e.wait_ge(x_ready, 4)
            e.tensor_scalar(halfb[:, :], pcol[:, BR:BR + 16], 0.5, None, ALU.mult)
            e.tensor_tensor(qkg[:, :], pcol[:, QG:QG + 1], pcol[:, KG:KG + 1], ALU.mult)
            link(e.tensor_scalar(sp[:, 2, :], pcol[:, LAM:LAM + KD], -1.0, None, ALU.mult))
            link(e.tensor_tensor(sp[:, 0, :], sp[:, 2, :], pcol[:, LAM:LAM + KD], ALU.max))
            e.tensor_scalar(sp[:, 3, :], sp[:, 2, :], 0.0, None, ALU.max).then_inc(sp_in, 1)
            pre(0)
            norm(0, G1, pairs[0][1], pairs[0][0])
            e.wait_ge(sp_exp, 1)
            link(e.tensor_scalar(sp[:, 4, :], sp[:, 1, :], 2.0, None, ALU.add))
            link(e.reciprocal(sp[:, 5, :], sp[:, 4, :]))
            link(e.tensor_tensor(sp[:, 4, :], sp[:, 1, :], sp[:, 5, :], ALU.mult))
            link(e.tensor_tensor(sp[:, 5, :], sp[:, 4, :], sp[:, 4, :], ALU.mult))
            link(e.tensor_scalar(sp[:, 6, :], sp[:, 5, :], 1.0 / 17, 1.0 / 15, ALU.mult, ALU.add))
            for odd in (13, 11, 9, 7, 5, 3, 1):
                link(e.tensor_tensor(sp[:, 6, :], sp[:, 6, :], sp[:, 5, :], ALU.mult))
                link(e.tensor_scalar(sp[:, 6, :], sp[:, 6, :], 1.0 / odd, None, ALU.add))
            link(e.tensor_tensor(sp[:, 6, :], sp[:, 6, :], sp[:, 4, :], ALU.mult))
            link(e.scalar_tensor_tensor(sp[:, 6, :], sp[:, 6, :], 2.0, sp[:, 3, :], ALU.mult, ALU.add))
            e.tensor_scalar(sp[:, 7, :], sp[:, 6, :], 2.0, None, ALU.mult).then_inc(sp_ready, 1)
            pre(1)
            pre(2)
            inv(0, True)

            def conv(src, dst, taps, width, col, bias_col):
                link(e.tensor_scalar(dst, src[:, 0:SEQ], taps(0), bias_col, ALU.mult, ALU.add))
                for k in range(1, width):
                    ins = e.scalar_tensor_tensor(dst, src[:, k:k + SEQ], taps(k), dst, ALU.mult, ALU.add)
                    if k < width - 1:
                        link(ins)
                return ins

            for s in range(S_XR, S_G):
                pre(s + 3)
                normed(GROUP_OF[(s, 0)], xrp[:, :, KW - 1:])
                e.wait_ge(bank_free["dve"], s + 1)
                for m in range(2):
                    c = 2 * s + m
                    ins = conv(xrp[:, m, :], xa[:, c, :], lambda k: pcol[:, CONVW + KD * k + c:CONVW + KD * k + c + 1],
                               KW, pcol, pcol[:, CONVB + c:CONVB + c + 1])
                    if m == 0:
                        link(ins)
                ins.then_inc(xa_ready, 1)
                e.wait_ge(xa_hi, s + 1)
                e.tensor_tensor(pairs[1][1][:, 2 * s:2 * s + 2, :], xa[:, 2 * s:2 * s + 2, :],
                                pairs[1][0][:, 2 * s:2 * s + 2, :].bitcast(f32), ALU.subtract).then_inc(xa_lo, 1)
            for s in range(S_G, S_RI):
                pre(s + 3)
                i = s - S_G
                normed(GROUP_OF[(s, 0)], gg[:, 2 * i:2 * i + 2, :])
            pre(S_RI + 3)

            def rnn_chunk(m):
                if m < KD:
                    e.wait_ge(t_ready, m + 1)
                    e.wait_ge(sqt_ready, m + 1)
                    if m == 0:
                        e.wait_ge(g_ready, 4)
                    w, a, ya = rnn_t[:, 0, :], rnn_t[:, 1, :], rnn_t[:, 2 + m % 2, :]
                    if m >= 2:
                        e.wait_ge(ya_hi, m - 1)
                    link(e.tensor_scalar(a, T0[:, m, :], 1.0, None, ALU.add))
                    link(e.reciprocal(w, a))
                    link(e.tensor_scalar(a, T0[:, m, :], -1.0, 1.0, ALU.mult, ALU.add))
                    link(e.tensor_tensor(a, a, w, ALU.mult))
                    z = T1[:, m, :]
                    link(e.scalar_tensor_tensor(z, z, 1.0, xa[:, m, :], ALU.add, ALU.mult))
                    link(e.tensor_tensor(z, z, w, ALU.mult))
                    link(e.tensor_tensor(z, z, rnn_sq[:, m % 2, :], ALU.mult))
                    link(e.tensor_tensor_scan(w, a, z, 0.0, ALU.mult, ALU.add))
                    e.tensor_tensor(ya, w, gg[:, m, :], ALU.mult).then_inc(ya_ready, 1)
                if m >= 1:
                    e.wait_ge(ya_hi, m)
                    e.tensor_tensor(pairs[1][1][:, m - 1, :], rnn_t[:, 2 + (m - 1) % 2, :],
                                    pairs[1][0][:, m - 1, :].bitcast(f32), ALU.subtract).then_inc(ya_lo, 1)

            for s in range(S_Q, S_GATE):
                pre(s + 3)
                if s - S_Q <= KD:
                    rnn_chunk(s - S_Q)
                if s == S_V:
                    e.wait_ge(qk_ss, 1)
                    link(e.reciprocal(ssqk[:, :, :, :], rqk[:, :, :, :]))
                    e.tensor_scalar(cq[:, 0], ssqk[:, 0], P ** -0.5, None, ALU.mult)
                    e.tensor_scalar(cq[:, 1], ssqk[:, 0], -(P ** -0.5), None, ALU.mult)
                    for h in range(HALVES):
                        kk = k_s[:, h, :].rearrange("p (n d) -> p n d", n=HEADS)
                        ins = e.tensor_tensor(kk, kk, ssqk[:, 1, h, :].unsqueeze(2).to_broadcast([P, HEADS, P]),
                                              ALU.mult)
                    ins.then_inc(qk_scaled, 1)

            def gate_tile(i):
                return (T0 if i < 4 else T1)[:, 2 * (i % 4):2 * (i % 4) + 2, :]

            def gate(s, i, n0):
                g = GROUP_OF[(s, 0)]
                normed(g, gate_tile(i))

            def branch(g, tiles, dst):
                e.wait_ge(group_done, g + 1)
                e.scalar_tensor_tensor(dst[:, tiles, :], dst[:, tiles, :], 1.0,
                                       ps[g % 2][:, :].rearrange("p (m n) -> p m n", m=2),
                                       ALU.add, ALU.mult).then_inc(bank_free["dve"], 1)
                e.wait_ge(bank_free["dve"], emptied(g)[1])

            def merge(i, n0):
                tiles = slice(2 * i, 2 * i + 2)
                e.tensor_tensor(T0[:, tiles, :], T0[:, tiles, :], T1[:, tiles, :], ALU.add).then_inc(merged, 1)
                e.wait_ge(m_hi, n0 + i + 1)
                e.scalar_tensor_tensor(pairs[0][1][:, tiles, :], T0[:, tiles, :], 0.5,
                                       pairs[0][0][:, tiles, :].bitcast(f32), ALU.mult, ALU.subtract).then_inc(m_lo, 1)

            def residual(s, i):
                g = GROUP_OF[(s, 0)]
                e.wait_ge(group_done, g + 1)
                e.tensor_tensor(X[:, 2 * i:2 * i + 2, :], ps[g % 2][:, :].rearrange("p (m n) -> p m n", m=2),
                                X[:, 2 * i:2 * i + 2, :], ALU.add).then_inc(bank_free["dve"], 1)

            e.wait_ge(sink_T, 1)
            link(e.tensor_copy(sinks[:, 0, :], PSB[:, 8:8 + HEADS]))
            e.tensor_scalar(sinks[:, 1, :], sinks[:, 0, :], -1.0, None, ALU.mult).then_inc(sink_ready, 1)
            for s in range(S_GATE, FFN1):
                for step in steps_at(s):
                    att(step)
                pre(s + 3)
                if s < S_PR:
                    gate(s, s - S_GATE, 0)
                if S_PR <= s < S_PA:
                    i = s - S_PR
                    e.wait_ge(gate_t, 4)
                    branch(GROUP_OF[(s, 0)], slice(2 * i, 2 * i + 2), T0)
                if S_PA <= s < S_OUT:
                    i = s - S_PA
                    e.wait_ge(gate_t, 8)
                    branch(GROUP_OF[(s, 0)], slice(2 * i, 2 * i + 2), T1)
                    merge(i, 0)
                if S_OUT <= s < FFN1:
                    residual(s, s - S_OUT)

            def ffn(which, base, n0, n, g0):
                norm(n, g0, pairs[2][1], pairs[2][0])
                g_up = GROUP_OF[(base, 0)]
                free0 = emptied(g_up)[1]
                if which == 1:
                    e.memset(upn[:, :, 0:FKW - 1], 0.0)
                chain = dve_loop[which - 1]
                LINKS = 5
                state = [0]

                def llink(j, ins):
                    state[0] += 1
                    ins.then_inc(chain, 1)
                    e.wait_ge(chain, j * LINKS + state[0])

                def post(j, pre_a, pre_b, pre_c):
                    state[0] = 0
                    pre_a()
                    bank_u, bank_g = ps[g_up % 2], ps[(g_up + 1) % 2]
                    e.wait_ge(group_done, j * 2 + (g_up + 1))
                    dst = upn[:, :, FKW - 1:] if which == 1 else cv
                    e.tensor_tensor(dst, bank_u[:, :].rearrange("p (m n) -> p m n", m=2), bc2(rstd_bc[:, :], 2),
                                    ALU.mult).then_inc(bank_free["dve"], 1)
                    e.wait_ge(bank_free["dve"], j * 2 + free0)
                    if which == 1:
                        for m in range(2):
                            def col(k):
                                c = j * 2 + (k * FT + m)
                                return fcol[:, bass.ds(c, 1)]
                            llink(j, e.tensor_scalar(cv[:, m, :], upn[:, m, 0:SEQ], col(0), col(FKW), ALU.mult, ALU.add))
                            llink(j, e.scalar_tensor_tensor(cv[:, m, :], upn[:, m, 1:1 + SEQ], col(1), cv[:, m, :],
                                                            ALU.mult, ALU.add))
                            ins = e.scalar_tensor_tensor(cv[:, m, :], upn[:, m, 2:2 + SEQ], col(2), cv[:, m, :],
                                                         ALU.mult, ALU.add)
                            if m == 0:
                                llink(j, ins)
                        ins.then_inc(f_conv, 1)
                    pre_b()
                    e.wait_ge(group_done, j * 2 + (g_up + 2))
                    e.tensor_tensor(gt, bank_g[:, :].rearrange("p (m n) -> p m n", m=2), bc2(rstd_bc[:, :], 2),
                                    ALU.mult).then_inc(bank_free["dve"], 1)
                    e.wait_ge(bank_free["dve"], j * 2 + (free0 + 1))
                    e.wait_ge(f_glu, j + (n0 + 1))
                    e.tensor_tensor(actf, cv, gt, ALU.mult).then_inc(f_act, 1)
                    pre_c()
                    e.wait_ge(f_hi, j + (n0 + 1))
                    e.tensor_tensor(actlo, actf, acthi.bitcast(f32), ALU.subtract).then_inc(f_lo, 1)
                    assert state[0] == (LINKS if which == 1 else 0)

                inv(n, False)
                post(0, lambda: pre(base + 3), lambda: pre(base + 4), lambda: None)
                with e.Fori(1, STEPS - 1) as j:
                    s = j * 3 + (base - 1)
                    post(j, lambda: lo(s + 3, (base + 2) % RING), lambda: lo(s + 4, (base + 3) % RING),
                         lambda: lo(s + 5, (base + 4) % RING))
                last = base + 3 * (STEPS - 1) - 1
                post(STEPS - 1, lambda: pre(last + 3), lambda: pre(last + 4), lambda: pre(last + 5))
                pre(base + 3 * STEPS + 2)

            ffn(1, FFN1, 0, 1, G2)
            e.wait_ge(down_used, STEPS)
            for b in range(4):
                e.tensor_copy(X[:, 2 * b:2 * b + 2, :],
                              ps[2 + b][:, :].rearrange("p (m n) -> p m n", m=2)).then_inc(x_ready, 1)
            norm(2, MIXG, pairs[0][1], pairs[0][0])
            inv(2, True)

            def rotate(src1, src2, dst1, dst2, cos, sin, n, w, done=None):
                def t3(i):
                    return rope_t[:, i, 0:n * w].rearrange("p (n w) -> p n w", n=n)
                c = cos.unsqueeze(1).to_broadcast([P, n, w])
                s_ = sin.unsqueeze(1).to_broadcast([P, n, w])
                e.tensor_tensor(t3(0), src1, c, ALU.mult)
                e.tensor_tensor(t3(1), src2, s_, ALU.mult)
                e.tensor_tensor(t3(2), src2, c, ALU.mult)
                link(e.tensor_tensor(t3(3), src1, s_, ALU.mult))
                link(e.tensor_tensor(dst1, t3(0), t3(1), ALU.subtract))
                ins = e.tensor_tensor(dst2, t3(2), t3(3), ALU.add)
                if done:
                    ins.then_inc(done, 1)
                    e.wait_ge(done, 1)
                else:
                    link(ins)

            e.wait_ge(in_misc, 16 * 6)
            for s in range(S2_SEQ, S2_GA):
                pre(s + 3)
                i = s - S2_SEQ
                if i in (2, 3):
                    h = i - 2
                    e.wait_ge(bank_free["act"], U2_FREE[1])
                    for a in range(2):
                        src = u2[:, h, 256 * a:256 * a + 256].rearrange("p (n d) -> p n d", n=4)
                        dst = q_r[:, h, :].rearrange("p (n b d) -> p b n d", b=2, d=64)[:, a]
                        rotate(src[:, :, 0:32], src[:, :, 32:64], dst[:, :, 0:32], dst[:, :, 32:64],
                               ropeA[:, 0, h, :], ropeA[:, 1, h, :], 4, 32)
                if i in (4, 5):
                    h = i - 4
                    e.wait_ge(bank_free["act"], U2_FREE[2])
                    src = u2[:, h, OFF_KA:OFF_KA + P].rearrange("p (n d) -> p n d", n=2)
                    dst = k_r[:, h, :].rearrange("p (n d) -> p n d", n=2)
                    rotate(src[:, :, 0:32], src[:, :, 32:64], dst[:, :, 0:32], dst[:, :, 32:64],
                           ropeA[:, 0, h, :], ropeA[:, 1, h, :], 2, 32, rope_q if h else None)
            e.wait_ge(cq_ss, 1)
            e.reciprocal(ss2[:, :, :], r2[:, :, :]).then_inc(cq_r, 1)
            e.wait_ge(bank_free["act"], U2_FREE[5])
            for h in range(HALVES):
                src = u2[:, h, OFF_KR:OFF_KR + ROPE].unsqueeze(1)
                dst = krr[:, h, :].unsqueeze(1)
                rotate(src[:, :, 0:16], src[:, :, 16:32], dst[:, :, 0:16], dst[:, :, 16:32],
                       ropeB[:, 0, h, :], ropeB[:, 1, h, :], 1, 16)
                ins = e.tensor_copy(kf[:, h, :, NOPE:MLA_D],
                                    krr[:, h, :].unsqueeze(1).to_broadcast([P, HEADS, ROPE]))
            ins.then_inc(rope_k, 1)
            for s in range(S2_GA, FFN2):
                for step in steps_at(s):
                    att(step)
                pre(s + 3)
                if s < S2_UQ or S2_GB <= s < S2_OSWA:
                    i = s - S2_GA if s < S2_UQ else s - S2_GB + 4
                    gate(s, i, 8)
                if S2_OSWA <= s < S2_OMLA:
                    e.wait_ge(gate_t, 12)
                    for i in range(2):
                        c = 4 * (s - S2_OSWA) + 2 * i
                        branch(GROUP_OF[(s, i)], slice(c, c + 2), T0)
                if S2_OMLA <= s < S2_OUT:
                    e.wait_ge(gate_t, 16)
                    for i in range(2):
                        c = 2 * (s - S2_OMLA) + i
                        branch(GROUP_OF[(s, i)], slice(2 * c, 2 * c + 2), T1)
                        tiles = slice(2 * c, 2 * c + 2)
                        e.tensor_tensor(T0[:, tiles, :], T0[:, tiles, :], T1[:, tiles, :], ALU.add).then_inc(merged, 1)
                        e.wait_ge(m_hi, 4 + c + 1)
                        e.scalar_tensor_tensor(pairs[0][1][:, tiles, :], T0[:, tiles, :], 0.5,
                                               pairs[0][0][:, tiles, :].bitcast(f32), ALU.mult,
                                               ALU.subtract).then_inc(m_lo, 1)
                if S2_OUT <= s < FFN2:
                    residual(s, s - S2_OUT)
                if s == S2_GA:
                    for r in range(3):
                        for c in ((0, 1), (2, 3), (4,))[r]:
                            e.wait_ge(cq_hi, (2, 4, 5)[r])
                            e.scalar_tensor_tensor(pairs[1][1][:, c, :],
                                                   (PSA, PSB, PSA)[r][:, SEQ * (c % 2):SEQ * (c % 2) + SEQ],
                                                   pcol[:, QLG + c:QLG + c + 1],
                                                   pairs[1][0][:, c, :].bitcast(f32), ALU.mult,
                                                   ALU.subtract).then_inc(cq_lo, 1)
                if s == S2_UKV:
                    e.wait_ge(bank_free["act"], emptied(GROUP_OF[(S2_UKV - 1, 1)])[1])
                    for h in range(HALVES):
                        src = qb[:, h]
                        rotate(src[:, :, 64:80], src[:, :, 80:96], src[:, :, 64:80], src[:, :, 80:96],
                               ropeB[:, 0, h, :], ropeB[:, 1, h, :], 8, 16, mla_ready if h else None)
            ffn(2, FFN2, STEPS, 3, FFNG)
            e.wait_ge(down_used, 2 * STEPS)
            for h in range(HALVES):
                e.tensor_copy(outp[:, h, 0:512], ps[2 + 2 * h][:, :])
                e.tensor_copy(outp[:, h, 512:D], ps[3 + 2 * h][:, :]).then_inc(fin_ready, 1)
            e.wait_ge(fin_T, 1)
            e.tensor_copy(fing[:, 0:512], ps[0][:, :])
            link(e.tensor_copy(fing[:, 512:D], ps[1][:, :]))
            e.wait_ge(fin_root, 1)
            link(e.reciprocal(fin[:, 0:2], fin[:, 2:4]))
            for h in range(HALVES):
                e.scalar_tensor_tensor(outp[:, h, :], outp[:, h, :], fin[:, h:h + 1], fing, ALU.mult,
                                       ALU.mult).then_inc(y_ready, 1)

        @block.tensor
        def _(e):
            def three(out, lhs, rhs, first, last):
                e.matmul(out, lhs[0], rhs[0], start=first, stop=False, skip_group_check=True)
                e.matmul(out, lhs[0], rhs[1], start=False, stop=False, skip_group_check=True)
                return e.matmul(out, lhs[1], rhs[0], start=False, stop=last, skip_group_check=True)

            def bank_ready(g):
                if g >= 2:
                    who, n = emptied(g - 2)
                    e.wait_ge(bank_free[who], n)

            def weights(slot, k, cols, width):
                return tuple(w[slot][:, width * k:width * (k + 1)][:, cols] for w in (whi, wlo))

            def feature_tiles(out, slot, kk, width, act, tiles, k0=0, segment=None):
                for n, (c, o) in enumerate(tiles):
                    for k in range(kk):
                        if segment:
                            segment(n, k)
                        ins = three(out[:, o:o + SEQ], weights(slot, k, slice(c, c + P), width),
                                    (act[0][:, k0 + k, :], act[1][:, k0 + k, :]), n == 0 and k == 0, k == kk - 1)
                return ins

            def positions(out, slot, kk, width, act, cols, halves_, k0=0):
                for n, (h, o) in enumerate(halves_):
                    for k in range(kk):
                        ins = three(out[:, o:o + cols.stop - cols.start],
                                    tuple(a[:, k0 + k, P * h:P * h + P] for a in act),
                                    weights(slot, k, cols, width), n == 0 and k == 0, k == kk - 1)
                return ins

            def sums(n, seq):
                e.wait_ge(sq_ready, 2 * n + 2)
                e.wait_ge(consts, 1)
                if seq:
                    for h in range(HALVES):
                        for c in range(KD):
                            e.matmul(PSB[:, h:h + 1], SQ[:, c, P * h:P * h + P], ones[:, 0:1],
                                     start=(c == 0 and h == 0), stop=(c == KD - 1), skip_group_check=True)
                for c in range(KD):
                    ins = e.matmul(PSA[:, 0:SEQ], ones[:, :], SQ[:, c, :], start=(c == 0), stop=(c == KD - 1))
                ins.then_inc(ssum, 1)

            def att(step):
                kind_base = 0 if step < 100 else 100
                u = unit_of(step)
                if u is not None and not (8 <= u < 16 and u % 2):
                    n_t = t_count(u)
                    if n_t >= 2:
                        e.wait_ge(aTe, n_t - 1)
                    if u == 0:
                        e.wait_ge(qk_scaled, 1)
                    if u == 8:
                        e.wait_ge(rope_q, 1)
                    if u == 16:
                        e.wait_ge(mla_ready, 1)
                        e.wait_ge(rope_k, 1)
                        e.wait_ge(bank_free["act"], emptied(GROUP_OF[(S2_UKV, 3)])[1])
                    for h in range(HALVES):
                        for i in range(2):
                            if u < 8:
                                src = (q_s, k_s)[i][:, h, P * u:P * u + P]
                            elif u < 16:
                                c = (u - 8) // 2
                                src = q_r[:, h, P * c:P * c + P] if i == 0 else k_r[:, h, :]
                            else:
                                src = (qb, kf)[i][:, h, u - 16, :]
                            d = MLA_D if u >= 16 else P
                            ins = e.transpose(PST[0:d, SEQ * i + P * h:SEQ * i + P * h + P], src, ident[:, :])
                    ins.then_inc(aT, 1)
                u = unit_of(step - LAG_S) if step - LAG_S >= kind_base else None
                if u is not None:
                    e.wait_ge(aTe, t_count(u))
                    if u >= 1:
                        e.wait_ge(aM, u)
                    b = tbuf(u)
                    rows = slice(0, P) if u < 8 else slice(64 * (u % 2), 64 * (u % 2) + 64) if u < 16 \
                        else slice(0, MLA_D)
                    e.matmul(PSS[:, 0:P], qT[rows, b, 0:P], kT[rows, b, 0:P], start=True, stop=True)
                    e.matmul(PSS[:, P:3 * P], qT[rows, b, P:SEQ], kT[rows, b, :], start=True,
                             stop=True).then_inc(aS, 1)
                u = unit_of(step - LAG_PT) if step - LAG_PT >= kind_base else None
                if u is not None:
                    e.wait_ge(aN, u + 1)
                    if u >= 1:
                        e.wait_ge(aPTe, u)
                    for i in range(3):
                        ins = e.transpose(PSPT[:, P * i:P * i + P], pr[:, u % 3, P * i:P * i + P], ident[:, :])
                    ins.then_inc(aPT, 1)
                u = unit_of(step - LAG_PV) if step - LAG_PV >= kind_base else None
                if u is not None:
                    e.wait_ge(aPTe, u + 1)
                    if u >= 1:
                        e.wait_ge(aL, u)
                    if u < 8:
                        v = [v_s[:, h, P * u:P * u + P] for h in range(2)]
                    elif u < 16:
                        v = [u2[:, h, OFF_VA:OFF_VA + P] for h in range(2)]
                    else:
                        c = (u - 16) // 2
                        v = [vb[:, h, P * c:P * c + P] for h in range(2)]
                    e.matmul(PSPV[:, 0:SEQ], v[0], pT[:, u % 2, 0:SEQ], start=True, stop=False,
                             skip_group_check=True)
                    e.matmul(PSPV[:, P:SEQ], v[1], pT[:, u % 2, SEQ:3 * P], start=False, stop=True,
                             skip_group_check=True).then_inc(aPV, 1)

            e.wait_ge(in_x, 32)
            for k in range(KD):
                for h in range(HALVES):
                    o = SEQ * (k % 2) + P * h
                    ins = e.transpose(ps[2 + k // 2][:, o:o + P], xpos[:, h, P * k:P * k + P], ident[:, :])
                if k % 2:
                    ins.then_inc(xT_done, 1)
            e.wait_ge(in_par, 16 * 15)
            e.transpose(PSA[:, 0:PROWS], prow[0:PROWS, :], ident[0:PROWS, 0:PROWS])
            e.transpose(PSB[:, 0:FROWS], frow[0:FROWS, :], ident[0:FROWS, 0:FROWS]).then_inc(par_T, 1)
            e.wait_ge(par_ready, 1)
            sums(0, True)
            e.wait_ge(h_lo, KD)

            def slab(s, act, layout="feature"):
                e.wait_ge(lo_ready, s + 1)
                slot = s % RING
                kind = PLAN[s][1]
                n = sum(1 for x in GROUPS if x[0] == s)
                for i in range(n):
                    g = GROUP_OF[(s, i)]
                    bank_ready(g)
                    out = ps[g % 2]
                    steps = steps_at(s)

                    def segment(tile, k, steps=steps, i=i):
                        if k == 0 and i == 0 and n == 1:
                            if len(steps) == 1 and tile == 0:
                                att(steps[0])
                            if len(steps) == 2:
                                att(steps[tile])
                        if n == 2 and len(steps) == 2 and k == 0 and tile == 0:
                            att(steps[i])

                    if kind == "blocks":
                        for m in range(2):
                            blk = 2 * (i % 4) + m
                            c = 1024 * (i // 4) + P * blk
                            ins = three(out[:, SEQ * m:SEQ * m + SEQ], tuple(w[slot][:, c:c + P] for w in (whi, wlo)),
                                        (act[0][:, blk, :], act[1][:, blk, :]), m == 0, True)
                    elif layout == "feature" and kind == "cols":
                        ins = feature_tiles(out, slot, KD, WIDE, act, [(0, 0), (P, SEQ)], segment=segment)
                    elif layout == "feature":
                        k0 = 4 if s >= S2_OMLA else 0
                        ins = feature_tiles(out, slot, 4, 512, act, [(2 * P * i, 0), (2 * P * i + P, SEQ)], k0=k0,
                                            segment=segment)
                    elif kind == "cols":
                        width = min(WIDE, t[PLAN[s][0]].shape[2] - PLAN[s][2])
                        if s == S2_GA - 1:
                            width = SEQ_COLS - PLAN[s][2]
                        ins = positions(out, slot, KD, WIDE, act, slice(0, width), [(0, 0), (1, 256)])
                    elif kind == "rows3":
                        ins = positions(out, slot, 3, QLAT, act, slice(0, QLAT), [(i, 0)])
                    else:
                        h, c = divmod(i, 2)
                        ins = positions(out, slot, 2, 1024, act, slice(512 * c, 512 * c + 512), [(h, 0)], k0=3)
                    ins.then_inc(group_done, 1)

            for s in range(S_XR, FFN1):
                if s == S_RI:
                    e.wait_ge(xa_lo, 4)
                if s == S_V:
                    e.wait_ge(in_misc, 16 * 6)
                    e.wait_ge(rstd_ready, 1)
                    e.matmul(PSB[:, 8:8 + HEADS], ones[0:1, :], rowt[:, :], start=True, stop=True).then_inc(sink_T, 1)
                if s == S_PR:
                    e.wait_ge(ya_lo, KD)
                if s == S_PA:
                    e.wait_ge(aL, 8)
                if s == S_OUT:
                    e.wait_ge(m_lo, 4)
                act = pairs[1] if s == S_RI or S_PR <= s < S_PA else pairs[2] if S_PA <= s < S_OUT else pairs[0]
                slab(s, act, "position" if S_Q <= s < S_GATE else "feature")

            def ffn(which, base, n, n0):
                e.wait_ge(h_lo, KD * n + KD)
                act = pairs[2]
                g_up = GROUP_OF[(base, 0)]
                free0 = emptied(g_up)[1]
                if which == 1:
                    for c in range(KD):
                        e.matmul(ps[2 + c // 2][:, SEQ * (c % 2):SEQ * (c % 2) + SEQ], ident[:, :], X[:, c, :],
                                 start=(c % 2 == 0), stop=False, skip_group_check=True)
                else:
                    for h in range(HALVES):
                        for c in range(KD):
                            e.matmul(ps[2 + 2 * h + c // 4][:, P * (c % 4):P * (c % 4) + P],
                                     X[:, c, P * h:P * h + P], ident[:, :], start=(c % 4 == 0), stop=False,
                                     skip_group_check=True)

                def wide(j, s, slot, i, free):
                    e.wait_ge(lo_ready, s + 1)
                    free()
                    feature_tiles(ps[(g_up + i) % 2], slot, KD, WIDE, act, [(0, 0), (P, SEQ)]).then_inc(group_done, 1)

                def down(j, s, slot):
                    e.wait_ge(lo_ready, s + 1)
                    e.wait_ge(f_lo, j + (n0 + 1))
                    if which == 1:
                        for k in range(2):
                            for c in range(KD):
                                ins = three(ps[2 + c // 2][:, SEQ * (c % 2):SEQ * (c % 2) + SEQ],
                                            weights(slot, k, slice(P * c, P * c + P), D),
                                            (acthi[:, k, :], actlo[:, k, :]), False, False)
                    else:
                        for k in range(2):
                            for h in range(HALVES):
                                for c in range(2):
                                    ins = three(ps[2 + 2 * h + c][:, :],
                                                (acthi[:, k, P * h:P * h + P], actlo[:, k, P * h:P * h + P]),
                                                weights(slot, k, slice(512 * c, 512 * c + 512), D), False, False)
                    ins.then_inc(down_used, 1)

                for i in range(2):
                    g = g_up + i
                    wide(0, base + i, (base + i) % RING, i, lambda: bank_ready(g))
                    if i == 0:
                        sums(n, False)
                with e.Fori(1, STEPS) as j:
                    s = j * 3 + (base - 1)
                    for i in range(2):
                        wide(j, s + i, (base + 2 + i) % RING, i,
                             lambda: e.wait_ge(bank_free["dve"], (j - 1) * 2 + (free0 + i)))
                    down(j - 1, s + 2, (base + 4) % RING)
                last = base + 3 * STEPS - 1
                down(STEPS - 1, last, last % RING)

            ffn(1, FFN1, 1, 0)
            sums(2, True)
            e.wait_ge(h_lo, 3 * KD)
            for s in range(S2_SEQ, FFN2):
                if s == S2_GA + 1:
                    e.wait_ge(cq_s, 1)
                    for r in range(3):
                        if r == 2:
                            e.wait_ge(cq_lo, 2)
                        for c in ((0, 1), (2, 3), (4,))[r]:
                            for h in range(HALVES):
                                o = SEQ * (c % 2) + P * h
                                ins = e.transpose((PSA, PSB, PSA)[r][:, o:o + P],
                                                  u2[:, h, OFF_QL + P * c:OFF_QL + P * c + P], ident[:, :])
                        ins.then_inc(cq_T, 1)
                if s == S2_UQ:
                    e.wait_ge(cq_lo, 5)
                if s == S2_OSWA:
                    e.wait_ge(aL, 16)
                if s == S2_OMLA:
                    e.wait_ge(aL, 24)
                if s == S2_OUT:
                    e.wait_ge(m_lo, 8)
                act = pairs[1] if S2_UQ <= s <= S2_UKV else pairs[2] if S2_OSWA <= s < S2_OUT else pairs[0]
                slab(s, act, "position" if s < S2_GA or S2_UQ <= s <= S2_UKV else "feature")
            ffn(2, FFN2, 3, STEPS)
            e.wait_ge(in_x, 48)
            for c in range(2):
                ins = e.matmul(ps[c][:, :], ones[0:1, :], frow_g[:, 512 * c:512 * c + 512], start=True, stop=True)
            ins.then_inc(fin_T, 1)


def t_count(u):
    return u + 1 if u < 8 else 8 + (u - 8) // 2 + 1 if u < 16 else 12 + u - 16 + 1


def tbuf(u):
    return (t_count(u) - 1) % 2


def last_reader_of_tbuf(u):
    n = t_count(u) - 2
    return max(v for v in range(24) if t_count(v) == n) + 1


def swa_head(u):
    return (u - 8) // 2 + 4 * ((u - 8) % 2)


def yb_place(u):
    if u < 8:
        return slice(0, P), u
    b = u % 2
    return slice(64 * b, 64 * b + 64), (u - 8) // 2


_INS = ['x', 'norm1_g', 'w_in', 'conv_w', 'conv_b', 'w_r', 'b_r', 'w_i', 'b_i', 'lru_lambda', 'q_norm_g',
        'k_norm_g', 'w_proj_rnn', 'w_proj_attn', 'w_out', 'norm2_g', 'w_up', 'w_gate', 'ffn_conv_w',
        'ffn_conv_b', 'w_down', 'mix_norm_g_2', 'w_in_2', 'swa_sinks_2', 'q_norm_g_2', 'w_uq_2',
        'kv_norm_g_2', 'w_ukv_2', 'w_o_swa_2', 'w_o_mla_2', 'w_out_2', 'ffn_norm_g_2', 'w_gate_2',
        'w_up_2', 'w_down_2', 'final_norm_g_2']


def constants():
    q = np.arange(P)[:, None]
    k = np.arange(P)[None, :]
    causal = np.where(k <= q, 0.0, NEG)
    before = np.where(k > q, 0.0, NEG)
    masks = np.stack([np.concatenate([causal, 0 * causal, causal], 1),
                      np.concatenate([causal, before, causal], 1)], 1).astype(np.float32)

    def rope(dim):
        inv = np.float32(10000.0) ** (-np.arange(0, dim, 2, dtype=np.float32) / np.float32(dim))
        ang = np.arange(SEQ, dtype=np.float32)[:, None] * inv.astype(np.float32)[None, :]
        return np.stack([np.cos(ang), np.sin(ang)]).astype(np.float32)
    return {"ident": np.eye(P, dtype=np.float32), "masks": masks, "rope_a": rope(64), "rope_b": rope(32)}


def kernel(**inputs):
    import concourse.bacc as _bacc
    from concourse.bass_utils import run_bass_kernel_spmd as _run

    nc = _bacc.Bacc("TRN2", target_bir_lowering=False, num_devices=1)
    arrays, t = {}, {}
    given = {n: np.ascontiguousarray(inputs[n]) for n in _INS}
    given.update(constants())
    for name, a in given.items():
        arrays[f"in_{name}"] = a
        t[name] = nc.dram_tensor(f"in_{name}", a.shape, mybir.dt.from_np(a.dtype), kind="ExternalInput").ap()
    t["final_norm_g"] = t["final_norm_g_2"]
    t["out"] = nc.dram_tensor("out", (1, SEQ, D), mybir.dt.float32, kind="ExternalOutput").ap()
    program(nc, t)
    r = _run(nc, [arrays], core_ids=[0])
    return r.results[0]["out"]
```

```python
import numpy as np
import concourse.bass as bass
from concourse import mybir
from contextlib import ExitStack

P = 128
SEQ = 256
HALVES = SEQ // P
D = 1024
KD = D // P
FF = 2816
FT = FF // P
HEADS = 8
SLAB = 2048
WIDE = SLAB // KD
RING = 3
EPS = 1e-6
NEG = -1e30
KW = 4
FKW = 3
D_IN2 = 3488
SEQ_COLS = 1440
QLAT, KVLAT = 384, 256
OFF_KA, OFF_VA, OFF_QL, OFF_KVL, OFF_KR = 512, 640, 768, 1152, 1408
MLA_D, NOPE, ROPE, VD = 96, 64, 32, 64

G1, CONVW, CONVB, BR, BI, LAM, G2, MIXG, FFNG, QLG, KVLG, QG, KG = (
    0, 8, 40, 48, 56, 64, 72, 80, 88, 96, 99, 101, 102)
PROWS = 103
FROWS = FKW * FT + FT


def slab_plan():
    plan = [("w_in", "cols", WIDE * i) for i in range(8)]
    plan += [("w_ri", "blocks", 0)]
    plan += [("w_in", "cols", WIDE * i) for i in range(8, 28)]
    plan += [(w, "cols", WIDE * i) for w in ("w_proj_rnn", "w_proj_attn", "w_out") for i in range(4)]
    ffn1 = len(plan)
    plan += [("ffn1", "loop", i) for i in range(3 * (FF // WIDE))]
    plan += [("w_in_2", "cols", WIDE * i) for i in range(6)]
    plan += [("w_in_2", "cols", SEQ_COLS + WIDE * i) for i in range(2)]
    plan += [("w_uq_2", "rows3", 0), ("w_uq_2", "rows3", QLAT), ("w_ukv_2", "rows2", 0)]
    plan += [("w_in_2", "cols", SEQ_COLS + WIDE * i) for i in range(2, 8)]
    plan += [("w_o_swa_2", "swa", 512 * i) for i in range(2)]
    plan += [("w_o_mla_2", "rows4", 512 * i) for i in range(2)]
    plan += [("w_out_2", "cols", WIDE * i) for i in range(4)]
    ffn2 = len(plan)
    plan += [("ffn2", "loop", i) for i in range(3 * (FF // WIDE))]
    return plan, ffn1, ffn2


PLAN, FFN1, FFN2 = slab_plan()
SLABS = len(PLAN)
STEPS = FF // WIDE
S_XR, S_G, S_RI, S_Q, S_K, S_V, S_GATE, S_PR, S_PA, S_OUT = 0, 4, 8, 9, 13, 17, 21, 29, 33, 37
S2_SEQ, S2_GA, S2_UQ, S2_UKV, S2_GB = FFN1 + 33, FFN1 + 39, FFN1 + 41, FFN1 + 43, FFN1 + 44
S2_OSWA, S2_OMLA, S2_OUT = FFN1 + 50, FFN1 + 52, FFN1 + 54


def group_plan():
    groups = []
    for s, (_, kind, _) in enumerate(PLAN):
        if kind == "loop":
            if s in (FFN1, FFN2):
                groups += [(s, i, "dve") for i in range(2 * STEPS)]
        elif kind == "blocks":
            groups += [(s, i, "act") for i in range(8)]
        elif S_Q <= s < S_GATE or S2_SEQ <= s < S2_GA:
            groups.append((s, 0, "act"))
        elif S2_UQ <= s < S2_UKV:
            groups += [(s, i, "act") for i in range(2)]
        elif s == S2_UKV:
            groups += [(s, i, "act") for i in range(4)]
        elif S2_OSWA <= s < S2_OUT:
            groups += [(s, i, "dve") for i in range(2)]
        else:
            groups.append((s, 0, "dve"))
    return groups


GROUPS = group_plan()
GROUP_OF = {(s, i): g for g, (s, i, _) in enumerate(GROUPS)}


def emptied(g):
    who = GROUPS[g][2]
    return who, sum(1 for x in GROUPS[:g + 1] if x[2] == who)


LAG_S, LAG_PT, LAG_PV = 1, 3, 4


def steps_at(s):
    if S_GATE <= s < S_PR + LAG_PV:
        return [s - S_GATE]
    if S2_GA <= s < S2_OMLA:
        first = sum(STEPS_AT[:s - S2_GA])
        return [100 + first + i for i in range(STEPS_AT[s - S2_GA])]
    return []


STEPS_AT = [1, 2, 1, 1, 1, 2, 2, 2, 1, 2, 1, 2, 2]


def gate_of(s):
    if S2_GA <= s < S2_UQ:
        return s - S2_GA
    if S2_GB <= s < S2_OSWA:
        return s - S2_GB + S2_UQ - S2_GA
    return None


def unit_of(step):
    if 0 <= step < HEADS:
        return step
    if 100 <= step < 100 + 2 * HEADS:
        return step - 100 + HEADS
    return None


def program(nc, t):
    f32, f32r = mybir.dt.float32, mybir.dt.float32r
    ALU, ACT, AX = mybir.AluOpType, mybir.ActivationFunctionType, mybir.AxisListType.X
    with ExitStack() as ctx:
        def sb(name, shape, dt=f32):
            return ctx.enter_context(nc.sbuf_tensor(name, shape, dt))

        def sem(name):
            return ctx.enter_context(nc.semaphore(name))

        raw = [sb(f"raw{i}", [P, SLAB]) for i in range(RING)]
        whi = [sb(f"whi{i}", [P, SLAB], f32r) for i in range(RING)]
        wlo = [sb(f"wlo{i}", [P, SLAB], f32r) for i in range(RING)]
        pairs = [(sb(f"ahi{i}", [P, KD, SEQ], f32r), sb(f"alo{i}", [P, KD, SEQ], f32r)) for i in range(3)]
        X = sb("x_res", [P, KD, SEQ])
        XA = sb("xa", [P, SLAB])
        GG = sb("gg", [P, SLAB])
        VV = sb("vv", [P, SLAB])
        T0 = sb("gate0", [P, KD, SEQ])
        T1 = sb("gate1", [P, KD, SEQ])
        QK = sb("qk", [P, 2 * SLAB])
        qkT = sb("qkT", [P, 2, 2, SEQ])
        qT, kT = qkT[:, :, 0, :], qkT[:, :, 1, :]
        sm = sb("sm", [P, 2, 3 * P])
        pr = sb("pr", [P, 3, 3 * P])
        pT = sb("pT", [P, 2, 3 * P])
        masks = sb("masks", [P, 2, 3 * P])
        ident = sb("ident", [P, P])
        ones = sb("ones", [P, P])
        pcol = sb("pcol", [P, PROWS])
        fcol = sb("fcol", [P, FROWS])
        halfb = sb("halfb", [P, 16])
        sp = sb("sp", [P, 8, KD])
        qkg = sb("qkg", [P, 1])
        epst = sb("epst", [P, 1])
        ropeA = sb("ropeA", [P, 2, HALVES, 32])
        ropeB = sb("ropeB", [P, 2, HALVES, 16])
        krr = sb("krr", [P, HALVES, ROPE])
        sinks = sb("sinks", [P, 2, HEADS])
        rowt = sb("rowt", [1, HEADS])
        root = sb("root", [P, SEQ])
        root2 = sb("root2", [P, 2])
        rstd_bc = sb("rstd_bc", [P, SEQ])
        rstd_sq = sb("rstd_sq", [P, 2])
        ssqk = sb("ssqk", [P, 2, HALVES, HEADS])
        rqk = sb("rqk", [P, 2, HALVES, HEADS])
        cq = sb("cq", [P, 2, HALVES, HEADS])
        ss2 = sb("ss2", [P, 2, 2])
        r2 = sb("r2", [P, 2, 2])
        mx = sb("mx", [P, 2, 2])
        nb = sb("nb", [P, 3, 2])
        sums = sb("sums", [P, 3, 2])
        esink = sb("esink", [P, 3, 2])
        rinv = sb("rinv", [P, 2, 2])
        junk = pT[:, 0, :]
        fin = sb("fin", [P, 4])
        fin2 = sb("fin2", [P, 4])
        finr = sb("finr", [P, 2])

        xpos = GG[:, :].rearrange("p (h d) -> p h d", h=HALVES)
        prow = QK[:, 0:P]
        frow = QK[:, P:2 * P]
        SQ = VV[:, :].rearrange("p (k n) -> p k n", k=KD)
        xrp = QK[:, 1024:1024 + 2 * (SEQ + KW - 1)].rearrange("p (m n) -> p m n", m=2)
        xa = XA[:, :].rearrange("p (k n) -> p k n", k=KD)
        gg = GG[:, :].rearrange("p (k n) -> p k n", k=KD)
        q_s = QK[:, 0:SLAB].rearrange("p (h d) -> p h d", h=HALVES)
        k_s = QK[:, SLAB:2 * SLAB].rearrange("p (h d) -> p h d", h=HALVES)
        v_s = VV[:, :].rearrange("p (h d) -> p h d", h=HALVES)
        rnn_t = pr[:, :, :].rearrange("p a n -> p (a n)")[:, 0:4 * SEQ].rearrange("p (a n) -> p a n", a=4)
        rnn_sq = sm[:, :, :].rearrange("p a n -> p (a n)")[:, 0:2 * SEQ].rearrange("p (a n) -> p a n", a=2)
        rope_t = T1[:, 0:4, :]
        u2 = QK[:, 0:HALVES * SEQ_COLS].rearrange("p (h d) -> p h d", h=HALVES)
        vb = QK[:, HALVES * SEQ_COLS:HALVES * SEQ_COLS + HALVES * HEADS * VD].rearrange(
            "p (h d) -> p h d", h=HALVES)
        q_r = VV[:, 0:1024].rearrange("p (h d) -> p h d", h=HALVES)
        k_r = VV[:, 1024:1280].rearrange("p (h d) -> p h d", h=HALVES)
        qb = XA[:, 0:HALVES * HEADS * MLA_D].rearrange("p (h n d) -> p h n d", h=HALVES, n=HEADS)
        qbf = XA[:, 0:HALVES * HEADS * MLA_D].rearrange("p (h d) -> p h d", h=HALVES)
        kf = GG[:, 0:HALVES * HEADS * MLA_D].rearrange("p (h n d) -> p h n d", h=HALVES, n=HEADS)
        upn = QK[:, 0:2 * (SEQ + FKW - 1)].rearrange("p (m n) -> p m n", m=2)
        cv = QK[:, 1024:1536].rearrange("p (m n) -> p m n", m=2)
        gt = QK[:, 1536:2048].rearrange("p (m n) -> p m n", m=2)
        actf = QK[:, 2048:2560].rearrange("p (m n) -> p m n", m=2)
        acthi, actlo = pairs[1][0][:, 0:2, :], pairs[1][1][:, 0:2, :]
        fing = T0[:, 0:4, :].rearrange("p k n -> p (k n)")
        frow_g = QK[0:1, 3072:4096]
        outp = GG[:, :].rearrange("p (h d) -> p h d", h=HALVES)

        ps = [ctx.enter_context(nc.psum_tensor(f"ps{i}", [P, 512], f32)) for i in range(8)]
        PST, PSS, PSPT, PSPV, PSA, PSB = ps[2], ps[3], ps[4], ps[5], ps[6], ps[7]

        in_x, in_par, in_misc, out_done = sem("in_x"), sem("in_par"), sem("in_misc"), sem("out_done")
        raw_in = [sem(f"raw_in{i}") for i in range(RING)]
        hi_ready, lo_ready, down_used = sem("hi_ready"), sem("lo_ready"), sem("down_used")
        group_done = sem("group_done")
        bank_free = {"act": sem("bank_free_act"), "dve": sem("bank_free_dve")}
        act_step, dve_step = sem("act_step"), sem("dve_step")
        dve_loop = [sem("dve_loop0"), sem("dve_loop1")]
        par_T, par_ready, sp_exp, consts = sem("par_T"), sem("par_ready"), sem("sp_exp"), sem("consts")
        sp_in, sp_ready = sem("sp_in"), sem("sp_ready")
        xT_done, x_ready = sem("xT_done"), sem("x_ready")
        h_hi, h_lo, sq_ready, ssum, rms_root, rstd_ready, rms_root2, rstd2_ready = (sem(n) for n in (
            "h_hi", "h_lo", "sq_ready", "ssum", "rms_root", "rstd_ready", "rms_root2", "rstd2_ready"))
        xa_ready, xa_hi, xa_lo = sem("xa_ready"), sem("xa_hi"), sem("xa_lo")
        g_ready = sem("g_ready")
        t_ready, sqt_ready, ya_ready, ya_hi, ya_lo = (
            sem(n) for n in ("t_ready", "sqt_ready", "ya_ready", "ya_hi", "ya_lo"))
        qk_ss, qk_scaled, v_ready = sem("qk_ss"), sem("qk_scaled"), sem("v_ready")
        gate_t = sem("gate_t")
        aT, aTe, aS, aM, aE, aN, aPT, aPTe, aPV, aH, aL = (sem(n) for n in (
            "att_T", "att_T_out", "att_S", "att_max", "att_exp", "att_norm", "att_PT", "att_PT_out",
            "att_PV", "yb_hi", "yb_lo"))
        merged, m_hi, m_lo = sem("merged"), sem("m_hi"), sem("m_lo")
        rope_q, cq_ss, cq_r, cq_s, cq_T, cq_hi, cq_lo = (sem(n) for n in (
            "rope_q", "cq_ss", "cq_r", "cq_scaled", "cq_T", "cq_hi", "cq_lo"))
        qb_ready, kv_ready, mla_ready, rope_k = sem("qb_ready"), sem("kv_ready"), sem("mla_ready"), sem("rope_k")
        sink_T, sink_ready = sem("sink_T"), sem("sink_ready")
        f_conv, f_glu, f_act, f_hi, f_lo = (sem(n) for n in ("f_conv", "f_glu", "f_act", "f_hi", "f_lo"))
        down_bank, fin_T, fin_Te, fin_root, y_ready = (
            sem(n) for n in ("down_bank", "fin_T", "fin_T_out", "fin_root", "y_ready"))
        block = ctx.enter_context(nc.Block())

        U2_FREE = [emptied(GROUP_OF[(s, 0)])[1] for s in range(S2_SEQ, S2_GA)]

        CQ_ROUND = ((0, 1), (2, 3), (4,))

        def used_value(s):
            base = FFN2 if s >= FFN2 else FFN1
            if base <= s < base + 3 * STEPS:
                i = s - base
                n0 = 0 if base == FFN1 else STEPS
                if i < 2:
                    return group_done, GROUP_OF[(base, 0)] + i + 1
                j, kind = divmod(i - 2, 3)
                if i == 3 * STEPS - 1 or kind == 2:
                    if i == 3 * STEPS - 1:
                        return down_bank, 4 if n0 == 0 else 6
                    return down_used, n0 // STEPS * (STEPS - 1) + j + 1
                return group_done, GROUP_OF[(base, 0)] + 2 * (j + 1) + kind + 1
            return group_done, max(g for (x, _), g in GROUP_OF.items() if x == s) + 1

        def x_value(n, c):
            if n % 2 == 0:
                return x_ready, 2 * n + c // 2 + 1
            return bank_free["dve"], emptied(GROUP_OF[((S_OUT if n == 1 else S2_OUT) + c // 2, 0)])[1]

        def raw_value(s):
            return 32 * (s // RING + 1)

        @block.sync
        def _(sp_eng):
            e = sp_eng
            e.dma_start(xpos, t["x"][0].rearrange("(h p) d -> p h d", p=P)).then_inc(in_x, 16)
            e.dma_start(ident[:, :], t["ident"]).then_inc(in_x, 16)

            def halves(slot, src_of, view):
                for a in range(2):
                    e.dma_start(view[64 * a:64 * a + 64], src_of(a)).then_inc(raw_in[slot], 16)

            def load(s):
                name, kind, arg = PLAN[s]
                slot = s % RING
                if s >= RING:
                    e.wait_ge(lo_ready, s - RING + 1)
                r = raw[slot]
                if kind == "blocks":
                    for i, w in enumerate(("w_r", "w_i")):
                        e.dma_start(r[:, 1024 * i:1024 * i + 1024].rearrange("p (n d) -> p n d", n=8),
                                    t[w][0].rearrange("n c d -> c n d")).then_inc(raw_in[slot], 16)
                    return
                w = t[name][0]
                if kind == "cols":
                    width = min(WIDE, w.shape[1] - arg)
                    view = r[:, :].rearrange("p (k n) -> p k n", k=KD)[:, :, 0:width]
                    src = w.rearrange("(k a p) n -> a p k n", a=2, p=64)
                    halves(slot, lambda a: src[a][:, :, arg:arg + width], view)
                elif kind == "swa":
                    view = r[:, :].rearrange("p (k n) -> p k n", k=4)
                    src = w.rearrange("(a k p) n -> a p k n", a=2, p=64)
                    halves(slot, lambda a: src[a][:, :, arg:arg + 512], view)
                else:
                    k, width = {"rows4": (4, 512), "rows3": (3, QLAT), "rows2": (2, 1024)}[kind]
                    view = r[:, 0:k * width].rearrange("p (k n) -> p k n", k=k)
                    src = w.rearrange("(k a p) n -> a p k n", a=2, p=64)
                    halves(slot, lambda a: src[a][:, :, arg:arg + width], view)

            def load_cols(s, slot, name, j, free=True):
                if free:
                    e.wait_ge(lo_ready, s - RING + 1)
                src = t[name][0].rearrange("(k a p) n -> a p k n", a=2, p=64)
                view = raw[slot][:, :].rearrange("p (k n) -> p k n", k=KD)
                halves(slot, lambda a: src[a][:, :, bass.ts(j, WIDE)], view)

            def load_down(s, slot, name, j):
                e.wait_ge(lo_ready, s - RING + 1)
                src = t[name][0].rearrange("(j k a p) n -> a p j k n", k=2, a=2, p=64)
                view = raw[slot][:, :].rearrange("p (k n) -> p k n", k=2)
                halves(slot, lambda a: src[a][:, j], view)

            def ffn(base, up, gate, down):
                load_cols(base, base % RING, up, 0)
                load_cols(base + 1, (base + 1) % RING, gate, 0)
                with e.Fori(1, STEPS) as j:
                    s = j * 3 + (base - 1)
                    load_cols(s, (base + 2) % RING, up, j)
                    load_cols(s + 1, base % RING, gate, j)
                    load_down(s + 2, (base + 1) % RING, down, j - 1)
                load_down(base + 3 * STEPS - 1, (base + 3 * STEPS - 1) % RING, down, STEPS - 1)

            load(0)
            load(1)
            load(2)
            e.dma_start(masks[:, :, :], t["masks"]).then_inc(in_misc, 16)
            for c in range(2):
                e.dma_start(ropeA[:, c], t["rope_a"][c].rearrange("(h p) d -> p h d", p=P)).then_inc(in_misc, 16)
                e.dma_start(ropeB[:, c], t["rope_b"][c].rearrange("(h p) d -> p h d", p=P)).then_inc(in_misc, 16)
            e.dma_start(rowt[:, :], t["swa_sinks_2"]).then_inc(in_misc, 16)
            for s in range(RING, FFN1):
                load(s)
            ffn(FFN1, "w_up", "w_gate", "w_down")
            for s in range(S2_SEQ, FFN2):
                load(s)
            e.wait_ge(aPV, 24)
            e.dma_start(frow_g, t["final_norm_g"].rearrange("(a n) -> a n", a=1)).then_inc(in_x, 16)
            ffn(FFN2, "w_up_2", "w_gate_2", "w_down_2")
            for h in range(HALVES):
                e.wait_ge(y_ready, h + 1)
                e.dma_start(t["out"][0][P * h:P * h + P, :], outp[:, h, :]).then_inc(out_done, 16)
            e.wait_ge(out_done, 16 * HALVES)

        @block.scalar
        def _(e):
            count = [0]

            def link(ins):
                count[0] += 1
                ins.then_inc(act_step, 1)
                e.wait_ge(act_step, count[0])

            def hi(slot, raw_v, used):
                e.wait_ge(raw_in[slot], raw_v)
                if used:
                    e.wait_ge(*used)
                e.activation(whi[slot][:, :], raw[slot][:, :], ACT.Copy).then_inc(hi_ready, 1)

            def pre(s):
                if s < SLABS:
                    hi(s % RING, raw_value(s), used_value(s - RING) if s >= RING else None)

            def free_bank(ins):
                ins.then_inc(bank_free["act"], 1)

            def norm_hi(n, g0, h_dst, chunks):
                for c in chunks:
                    e.wait_ge(*x_value(n, c))
                    e.activation(h_dst[:, c, :], X[:, c, :], ACT.Copy,
                                 scale=pcol[:, g0 + c:g0 + c + 1]).then_inc(h_hi, 1)

            def squares(n, i):
                e.activation(SQ[:, 2 * i:2 * i + 2, :], X[:, 2 * i:2 * i + 2, :], ACT.Square).then_inc(sq_ready, 1)

            def roots(n, seq):
                e.wait_ge(ssum, n + 1)
                if seq:
                    e.activation(root2[:, :], PSB[:, 0:2], ACT.Sqrt, bias=epst[:, :], scale=1.0 / D).then_inc(rms_root2, 1)
                e.activation(root[:, :], PSA[:, 0:SEQ], ACT.Sqrt, bias=epst[:, :], scale=1.0 / D).then_inc(rms_root, 1)

            def att(step):
                kind_base = 0 if step < 100 else 100
                u = unit_of(step)
                if u is not None and not (8 <= u < 16 and u % 2):
                    n_t = t_count(u)
                    b = tbuf(u)
                    e.wait_ge(aT, n_t)
                    if n_t > 2:
                        e.wait_ge(aS, last_reader_of_tbuf(u))
                    d = MLA_D if u >= 16 else P
                    if u < 8:
                        e.activation(qT[:, b, :], PST[:, 0:SEQ], ACT.Copy)
                        e.activation(kT[:, b, :], PST[:, SEQ:2 * SEQ], ACT.Copy, scale=qkg[:, :]).then_inc(aTe, 1)
                    else:
                        e.activation(qkT[0:d, b, :, :], PST[0:d, :].rearrange("p (i n) -> p i n", i=2),
                                     ACT.Copy).then_inc(aTe, 1)
                u = unit_of(step - LAG_PT) if step - LAG_PT >= kind_base else None
                if u is not None:
                    e.wait_ge(aPT, u + 1)
                    if u >= 2:
                        e.wait_ge(aPV, u - 1)
                    e.activation(pT[:, u % 2, :], PSPT[:, 0:3 * P], ACT.Copy).then_inc(aPTe, 1)
                u = unit_of(step - LAG_PV) if step - LAG_PV >= kind_base else None
                if u is not None:
                    e.wait_ge(aPV, u + 1)
                    rows, chunk = yb_place(u)
                    e.activation(pairs[2][0][rows, chunk, :], PSPV[rows, 0:SEQ], ACT.Copy).then_inc(aH, 1)
                u = unit_of(step - LAG_S) if step - LAG_S >= kind_base else None
                if u is not None:
                    e.wait_ge(aM, u + 1)
                    if u >= 3:
                        e.wait_ge(aPT, u - 2)
                    for h in range(HALVES):
                        cols = slice(0, P) if h == 0 else slice(P, 3 * P)
                        if u < 8:
                            scale = cq[:, 0, h, u:u + 1]
                        else:
                            scale = (64 ** -0.5) if u < 16 else MLA_D ** -0.5
                        ins = e.activation(pr[:, u % 3, cols], sm[:, u % 2, cols], ACT.Exp,
                                           bias=nb[:, u % 3, h:h + 1], scale=scale,
                                           accum_out=sums[:, u % 3, h:h + 1])
                    if 8 <= u < 16:
                        hd = swa_head(u)
                        ins = e.activation(esink[:, u % 3, :], nb[:, u % 3, :], ACT.Exp,
                                           bias=sinks[:, 0, hd:hd + 1])
                    ins.then_inc(aE, 1)

            rows = [(G1, "norm1_g", 8), (CONVB, "conv_b", 8), (BR, "b_r", 8),
                    (BI, "b_i", 8), (LAM, "lru_lambda", 8), (G2, "norm2_g", 8), (MIXG, "mix_norm_g_2", 8),
                    (FFNG, "ffn_norm_g_2", 8), (QLG, "q_norm_g_2", 3), (KVLG, "kv_norm_g_2", 2),
                    (QG, "q_norm_g", 1), (KG, "k_norm_g", 1)]
            for r0, name, n in rows:
                src = t[name][0] if name in ("b_r", "b_i") else t[name][0].rearrange("(k p) -> k p", p=P)
                e.dma_start(prow[r0:r0 + n, :], src).then_inc(in_par, 16)
            e.dma_start(prow[CONVW:CONVW + KW * KD, :],
                        t["conv_w"][0].rearrange("w (k p) -> (w k) p", p=P)).then_inc(in_par, 16)
            e.dma_start(frow[0:FKW * FT, :],
                        t["ffn_conv_w"][0].rearrange("w (k p) -> (w k) p", p=P)).then_inc(in_par, 16)
            e.dma_start(frow[FKW * FT:FROWS, :],
                        t["ffn_conv_b"][0].rearrange("(k p) -> k p", p=P)).then_inc(in_par, 16)
            e.wait_ge(par_T, 1)
            e.wait_ge(consts, 1)
            e.activation(pcol[:, :], PSA[:, 0:PROWS], ACT.Copy)
            e.activation(fcol[:, :], PSB[:, 0:FROWS], ACT.Copy).then_inc(par_ready, 1)
            e.wait_ge(par_ready, 1)
            norm_hi(0, G1, pairs[0][0], range(4))
            pre(0)
            norm_hi(0, G1, pairs[0][0], range(4, KD))
            for i in range(4):
                squares(0, i)
            e.wait_ge(sp_in, 1)
            e.activation(sp[:, 1, :], sp[:, 0, :], ACT.Exp, scale=-1.0).then_inc(sp_exp, 1)
            pre(1)
            pre(2)
            for s in range(S_XR, S_G):
                if s == S_XR:
                    roots(0, True)
                pre(s + 3)
                e.wait_ge(xa_ready, s + 1)
                e.activation(pairs[1][0][:, 2 * s:2 * s + 2, :], xa[:, 2 * s:2 * s + 2, :], ACT.Copy).then_inc(xa_hi, 1)
            for s in range(S_G, S_RI):
                pre(s + 3)
                i = s - S_G
                e.wait_ge(bank_free["dve"], s + 1)
                e.activation(gg[:, 2 * i:2 * i + 2, :], gg[:, 2 * i:2 * i + 2, :], ACT.Gelu_apprx_tanh).then_inc(g_ready, 1)
            for i in range(8):
                g = GROUP_OF[(S_RI, i)]
                e.wait_ge(group_done, g + 1)
                for m in range(2):
                    blk = 2 * (i % 4) + m
                    dst = (T0 if i < 4 else T1)[:, blk, :]
                    ins = e.activation(dst, ps[g % 2][:, SEQ * m:SEQ * m + SEQ], ACT.Tanh, scale=0.5,
                                       bias=halfb[:, 8 * (i // 4) + blk:8 * (i // 4) + blk + 1])
                free_bank(ins)
            e.wait_ge(bank_free["act"], 8)
            e.wait_ge(sp_ready, 1)
            pre(S_RI + 3)
            for m in range(KD):
                e.activation(T0[:, m, :], T0[:, m, :], ACT.Tanh, scale=sp[:, 7, m:m + 1],
                             bias=sp[:, 7, m:m + 1]).then_inc(t_ready, 1)
            e.wait_ge(t_ready, KD)

            e.wait_ge(rstd2_ready, 1)

            def evac_qkv(s, dst, i):
                g = GROUP_OF[(s, 0)]
                e.wait_ge(group_done, g + 1)
                for h in range(HALVES):
                    ins = e.activation(dst[:, h, WIDE * i:WIDE * i + WIDE], ps[g % 2][:, 256 * h:256 * h + 256],
                                       ACT.Copy, scale=rstd_sq[:, h:h + 1])
                free_bank(ins)
                e.wait_ge(bank_free["act"], emptied(g)[1])

            def rnn_chunk(m):
                if m >= 2:
                    e.wait_ge(ya_ready, m - 1)
                e.activation(rnn_sq[:, m % 2, :], T0[:, m, :], ACT.Sqrt).then_inc(sqt_ready, 1)

            for s in range(S_Q, S_V):
                pre(s + 3)
                which, i = divmod(s - S_Q, 4)
                dst = (q_s, k_s)[which]
                evac_qkv(s, dst, i)
                for h in range(HALVES):
                    for hd in (2 * i, 2 * i + 1):
                        e.activation(junk[:, 0:P], dst[:, h, P * hd:P * hd + P], ACT.Square,
                                     accum_out=ssqk[:, which, h, hd:hd + 1]).then_inc(act_step, 1)
                        count[0] += 1
                        e.wait_ge(act_step, count[0])
                rnn_chunk(s - S_Q)
            e.activation(rqk[:, :, :, :], ssqk[:, :, :, :], ACT.Sqrt, bias=epst[:, :], scale=1.0 / P).then_inc(qk_ss, 1)
            for s in range(S_V, S_GATE):
                pre(s + 3)
                evac_qkv(s, v_s, s - S_V)
            e.wait_ge(bank_free["act"], emptied(GROUP_OF[(S_GATE - 1, 0)])[1])

            def gate_tile(i):
                return (T0 if i < 4 else T1)[:, 2 * (i % 4):2 * (i % 4) + 2, :]

            def merge_parts(first, n0):
                def run(i):
                    e.wait_ge(merged, n0 + i + 1)
                    e.activation(pairs[0][0][:, 2 * i:2 * i + 2, :], T0[:, 2 * i:2 * i + 2, :], ACT.Copy,
                                 scale=0.5).then_inc(m_hi, 1)
                return run

            e.wait_ge(ya_lo, KD)
            mp = merge_parts(S_PA, 0)
            for s in range(S_GATE, FFN1):
                for step in steps_at(s):
                    att(step)
                if S_PA <= s < S_OUT:
                    mp(s - S_PA)
                if s >= S_OUT:
                    i = s - S_OUT
                    norm_hi(1, G2, pairs[2][0], (2 * i, 2 * i + 1))
                pre(s + 3)
                if s < S_PR:
                    i = s - S_GATE
                    e.wait_ge(bank_free["dve"], emptied(GROUP_OF[(s, 0)])[1])
                    e.activation(gate_tile(i), gate_tile(i), ACT.Tanh, scale=0.5).then_inc(gate_t, 1)
                if s >= S_OUT:
                    squares(1, s - S_OUT)

            def ffn(which, base, n0, func):
                g_up = GROUP_OF[(base, 0)]
                free0 = emptied(g_up)[1]

                def post(j, pre_a, pre_b, pre_c):
                    pre_a()
                    pre_b()
                    if which == 1:
                        e.wait_ge(f_conv, j + 1)
                    else:
                        e.wait_ge(bank_free["dve"], j * 2 + (free0 + 1))
                    buf = cv if which == 1 else gt
                    e.activation(buf, buf, func).then_inc(f_glu, 1)
                    pre_c()
                    e.wait_ge(f_act, j + (n0 + 1))
                    if not (isinstance(j, int) and j == 0):
                        e.wait_ge(down_used, j + n0 // STEPS * (STEPS - 1))
                    e.activation(acthi, actf, ACT.Copy).then_inc(f_hi, 1)

                roots(which * 2 - 1, False)
                post(0, lambda: pre(base + 3), lambda: pre(base + 4), lambda: None)

                def hi_at(j, off):
                    used = (down_used, j + n0 // STEPS * (STEPS - 1)) if off == 4 else (group_done, j * 2 + (g_up + off - 1))
                    hi((base + off) % RING, j * 32 + 32 * ((base + off) // RING + 1), used)

                with e.Fori(1, STEPS - 1) as j:
                    post(j, lambda: hi_at(j, 2), lambda: hi_at(j, 3), lambda: hi_at(j, 4))
                last = base + 3 * (STEPS - 1) - 1
                post(STEPS - 1, lambda: pre(last + 3), lambda: pre(last + 4), lambda: pre(last + 5))

            ffn(1, FFN1, 0, ACT.Gelu_apprx_tanh)

            norm_hi(2, MIXG, pairs[0][0], range(KD))
            pre(S2_SEQ + 2)
            for i in range(4):
                squares(2, i)
            for s in range(S2_SEQ, S2_GA):
                if s == S2_SEQ:
                    roots(2, True)
                    e.wait_ge(rstd2_ready, 2)
                pre(s + 3)
                g = GROUP_OF[(s, 0)]
                i = s - S2_SEQ
                width = min(WIDE, SEQ_COLS - WIDE * i)
                e.wait_ge(group_done, g + 1)
                for h in range(HALVES):
                    ins = e.activation(u2[:, h, WIDE * i:WIDE * i + width], ps[g % 2][:, 256 * h:256 * h + width],
                                       ACT.Copy, scale=rstd_sq[:, h:h + 1])
                free_bank(ins)
            e.wait_ge(bank_free["act"], U2_FREE[5])
            for h in range(HALVES):
                link(e.activation(junk[:, 0:QLAT], u2[:, h, OFF_QL:OFF_QL + QLAT], ACT.Square,
                                  accum_out=ss2[:, 0, h:h + 1]))
                link(e.activation(junk[:, 0:KVLAT], u2[:, h, OFF_KVL:OFF_KVL + KVLAT], ACT.Square,
                                  accum_out=ss2[:, 1, h:h + 1]))
            e.activation(r2[:, 0, :], ss2[:, 0, :], ACT.Sqrt, bias=epst[:, :], scale=1.0 / QLAT)
            e.activation(r2[:, 1, :], ss2[:, 1, :], ACT.Sqrt, bias=epst[:, :], scale=1.0 / KVLAT).then_inc(cq_ss, 1)
            e.wait_ge(cq_r, 1)
            for h in range(HALVES):
                e.activation(u2[:, h, OFF_QL:OFF_QL + QLAT], u2[:, h, OFF_QL:OFF_QL + QLAT], ACT.Copy,
                             scale=ss2[:, 0, h:h + 1])
                ins = e.activation(u2[:, h, OFF_KVL:OFF_KVL + KVLAT], u2[:, h, OFF_KVL:OFF_KVL + KVLAT], ACT.Copy,
                                   scale=ss2[:, 1, h:h + 1])
            ins.then_inc(cq_s, 1)
            mp2 = merge_parts(S2_OMLA, 4)

            def cq_parts(r):
                e.wait_ge(cq_T, r + 1)
                for c in CQ_ROUND[r]:
                    e.activation(pairs[1][0][:, c, :], (PSA, PSB, PSA)[r][:, SEQ * (c % 2):SEQ * (c % 2) + SEQ],
                                 ACT.Copy, scale=pcol[:, QLG + c:QLG + c + 1]).then_inc(cq_hi, 1)

            for s in range(S2_GA, FFN2):
                for step in steps_at(s):
                    att(step)
                if S2_OMLA <= s < S2_OUT:
                    for i in range(2):
                        mp2(2 * (s - S2_OMLA) + i)
                if s >= S2_OUT:
                    i = s - S2_OUT
                    norm_hi(3, FFNG, pairs[2][0], (2 * i, 2 * i + 1))
                if s != S2_UKV:
                    pre(s + 3)
                if s >= S2_OUT:
                    squares(3, s - S2_OUT)
                if gate_of(s) is not None:
                    i = gate_of(s)
                    e.wait_ge(bank_free["dve"], emptied(GROUP_OF[(s, 0)])[1])
                    e.activation(gate_tile(i), gate_tile(i), ACT.Tanh, scale=0.5).then_inc(gate_t, 1)
                if s == S2_GA + 1:
                    cq_parts(0)
                    cq_parts(1)
                if S2_UQ <= s < S2_UKV:
                    for h in range(HALVES):
                        g = GROUP_OF[(s, h)]
                        e.wait_ge(group_done, g + 1)
                        i = s - S2_UQ
                        free_bank(e.activation(qbf[:, h, QLAT * i:QLAT * i + QLAT], ps[g % 2][:, 0:QLAT], ACT.Copy))
                if s == S2_UQ:
                    cq_parts(2)
                if s == S2_UKV:
                    for i in range(4):
                        g = GROUP_OF[(s, i)]
                        h, c = divmod(i, 2)
                        e.wait_ge(group_done, g + 1)
                        src = ps[g % 2][:, :].rearrange("p (n d) -> p n d", n=4)
                        e.activation(kf[:, h, 4 * c:4 * c + 4, 0:NOPE], src[:, :, 0:NOPE], ACT.Copy)
                        free_bank(e.activation(
                            vb[:, h, 4 * VD * c:4 * VD * c + 4 * VD].rearrange("p (n d) -> p n d", n=4),
                            src[:, :, NOPE:P], ACT.Copy))
                    pre(s + 3)
            ffn(2, FFN2, STEPS, ACT.Silu)
            for h in range(HALVES):
                e.wait_ge(down_bank, 4 + h + 1)
                for c in range(2):
                    ins = e.activation(VV[:, 0:512], ps[2 + 2 * h + c][:, :], ACT.Square,
                                       accum_out=fin[:, 2 * h + c:2 * h + c + 1])
                    link(ins)
                link(e.activation(fin2[:, h:h + 1], fin[:, 2 * h:2 * h + 1], ACT.Identity,
                                  bias=fin[:, 2 * h + 1:2 * h + 2]))
                e.activation(fin2[:, 2 + h:3 + h], fin2[:, h:h + 1], ACT.Sqrt, bias=epst[:, :],
                             scale=1.0 / D).then_inc(fin_root, 1)

        @block.vector
        def _(e):
            count = [0]

            def link(ins):
                count[0] += 1
                ins.then_inc(dve_step, 1)
                e.wait_ge(dve_step, count[0])

            def lo(s, slot):
                e.wait_ge(hi_ready, s + 1)
                e.tensor_tensor(wlo[slot][:, :], raw[slot][:, :], whi[slot][:, :].bitcast(f32),
                                ALU.subtract).then_inc(lo_ready, 1)

            def pre(s):
                if s < SLABS:
                    lo(s, s % RING)

            def bc2(ap, n):
                return ap.unsqueeze(1).to_broadcast([P, n, SEQ])

            def norm_lo(n, g0, lo_dst, hi_src, chunks):
                for c in chunks:
                    e.wait_ge(*x_value(n, c))
                    e.wait_ge(h_hi, KD * n + c + 1)
                    e.scalar_tensor_tensor(lo_dst[:, c, :], X[:, c, :], pcol[:, g0 + c:g0 + c + 1],
                                           hi_src[:, c, :].bitcast(f32), ALU.mult, ALU.subtract).then_inc(h_lo, 1)

            def inv(n, seq):
                if seq:
                    e.wait_ge(rms_root2, n // 2 + 1)
                    e.reciprocal(rstd_sq[:, :], root2[:, :]).then_inc(rstd2_ready, 1)
                e.wait_ge(rms_root, n + 1)
                e.reciprocal(rstd_bc[:, :], root[:, :]).then_inc(rstd_ready, 1)
                e.wait_ge(rstd_ready, n + 1)

            def normed(g, dst):
                e.wait_ge(group_done, g + 1)
                e.tensor_tensor(dst, ps[g % 2][:, :].rearrange("p (m n) -> p m n", m=2), bc2(rstd_bc[:, :], 2),
                                ALU.mult).then_inc(bank_free["dve"], 1)

            def att(step):
                kind_base = 0 if step < 100 else 100
                u = unit_of(step - LAG_S) if step - LAG_S >= kind_base else None
                ul = unit_of(step - LAG_PV) if step - LAG_PV >= kind_base else None
                if u is not None:
                    e.wait_ge(aS, u + 1)
                    if u >= 2:
                        e.wait_ge(aE, u - 1)
                    link(e.tensor_tensor(sm[:, u % 2, :], PSS[:, 0:3 * P],
                                         masks[:, 1 if 8 <= u < 16 else 0, :], ALU.add))
                    e.reduce_max(mx[:, u % 2, 0:1], sm[:, u % 2, 0:P], AX)
                    link(e.reduce_max(mx[:, u % 2, 1:2], sm[:, u % 2, P:3 * P], AX))
                    if u < 8:
                        e.tensor_tensor(nb[:, u % 3, :], mx[:, u % 2, :], cq[:, 1, :, u], ALU.mult).then_inc(aM, 1)
                    elif u < 16:
                        hd = swa_head(u)
                        e.tensor_scalar(nb[:, u % 3, :], mx[:, u % 2, :], -(64 ** -0.5), sinks[:, 1, hd:hd + 1],
                                        ALU.mult, ALU.min).then_inc(aM, 1)
                    else:
                        e.tensor_scalar(nb[:, u % 3, :], mx[:, u % 2, :], -(MLA_D ** -0.5), None,
                                        ALU.mult).then_inc(aM, 1)
                if ul is not None:
                    e.wait_ge(aH, ul + 1)
                    rows, chunk = yb_place(ul)
                    e.tensor_tensor(pairs[2][1][rows, chunk, :], PSPV[rows, 0:SEQ],
                                    pairs[2][0][rows, chunk, :].bitcast(f32), ALU.subtract).then_inc(aL, 1)
                if u is not None:
                    e.wait_ge(aE, u + 1)
                    if 8 <= u < 16:
                        link(e.tensor_tensor(sums[:, u % 3, :], sums[:, u % 3, :], esink[:, u % 3, :], ALU.add))
                    link(e.reciprocal(rinv[:, u % 2, :], sums[:, u % 3, :]))
                    e.tensor_scalar(pr[:, u % 3, 0:P], pr[:, u % 3, 0:P], rinv[:, u % 2, 0:1], None, ALU.mult)
                    e.tensor_scalar(pr[:, u % 3, P:3 * P], pr[:, u % 3, P:3 * P], rinv[:, u % 2, 1:2], None,
                                    ALU.mult).then_inc(aN, 1)

            e.memset(epst[:, :], EPS)
            e.memset(xrp[:, :, 0:KW - 1], 0.0)
            e.memset(ones[:, :], 1.0).then_inc(consts, 1)
            for b in range(4):
                e.wait_ge(xT_done, b + 1)
                e.tensor_copy(X[:, 2 * b:2 * b + 2, :],
                              ps[2 + b][:, :].rearrange("p (m n) -> p m n", m=2)).then_inc(x_ready, 1)
            e.wait_ge(par_ready, 1)
            e.wait_ge(x_ready, 4)
            e.tensor_scalar(halfb[:, :], pcol[:, BR:BR + 16], 0.5, None, ALU.mult)
            e.tensor_tensor(qkg[:, :], pcol[:, QG:QG + 1], pcol[:, KG:KG + 1], ALU.mult)
            link(e.tensor_scalar(sp[:, 2, :], pcol[:, LAM:LAM + KD], -1.0, None, ALU.mult))
            link(e.tensor_tensor(sp[:, 0, :], sp[:, 2, :], pcol[:, LAM:LAM + KD], ALU.max))
            e.tensor_scalar(sp[:, 3, :], sp[:, 2, :], 0.0, None, ALU.max).then_inc(sp_in, 1)
            norm_lo(0, G1, pairs[0][1], pairs[0][0], range(4))
            pre(0)
            norm_lo(0, G1, pairs[0][1], pairs[0][0], range(4, KD))
            pre(1)
            e.wait_ge(sp_exp, 1)
            link(e.tensor_scalar(sp[:, 4, :], sp[:, 1, :], 2.0, None, ALU.add))
            link(e.reciprocal(sp[:, 5, :], sp[:, 4, :]))
            link(e.tensor_tensor(sp[:, 4, :], sp[:, 1, :], sp[:, 5, :], ALU.mult))
            link(e.tensor_tensor(sp[:, 5, :], sp[:, 4, :], sp[:, 4, :], ALU.mult))
            link(e.tensor_scalar(sp[:, 6, :], sp[:, 5, :], 1.0 / 17, 1.0 / 15, ALU.mult, ALU.add))
            for odd in (13, 11, 9, 7, 5, 3, 1):
                link(e.tensor_tensor(sp[:, 6, :], sp[:, 6, :], sp[:, 5, :], ALU.mult))
                link(e.tensor_scalar(sp[:, 6, :], sp[:, 6, :], 1.0 / odd, None, ALU.add))
            link(e.tensor_tensor(sp[:, 6, :], sp[:, 6, :], sp[:, 4, :], ALU.mult))
            link(e.scalar_tensor_tensor(sp[:, 6, :], sp[:, 6, :], 2.0, sp[:, 3, :], ALU.mult, ALU.add))
            e.tensor_scalar(sp[:, 7, :], sp[:, 6, :], 2.0, None, ALU.mult).then_inc(sp_ready, 1)
            pre(2)
            inv(0, True)

            def conv(src, dst, taps, width, col, bias_col):
                link(e.tensor_scalar(dst, src[:, 0:SEQ], taps(0), bias_col, ALU.mult, ALU.add))
                for k in range(1, width):
                    ins = e.scalar_tensor_tensor(dst, src[:, k:k + SEQ], taps(k), dst, ALU.mult, ALU.add)
                    if k < width - 1:
                        link(ins)
                return ins

            for s in range(S_XR, S_G):
                if s:
                    e.wait_ge(xa_ready, s)
                normed(GROUP_OF[(s, 0)], xrp[:, :, KW - 1:])
                e.wait_ge(bank_free["dve"], s + 1)
                for m in range(2):
                    c = 2 * s + m
                    ins = conv(xrp[:, m, :], xa[:, c, :], lambda k: pcol[:, CONVW + KD * k + c:CONVW + KD * k + c + 1],
                               KW, pcol, pcol[:, CONVB + c:CONVB + c + 1])
                    if m == 0:
                        link(ins)
                ins.then_inc(xa_ready, 1)
                pre(s + 3)
            for s in range(S_G, S_RI):
                i = s - S_G
                normed(GROUP_OF[(s, 0)], gg[:, 2 * i:2 * i + 2, :])
                pre(s + 3)
            pre(S_RI + 3)

            def rnn_chunk(m):
                if True:
                    e.wait_ge(t_ready, m + 1)
                    e.wait_ge(sqt_ready, m + 1)
                    if m == 0:
                        e.wait_ge(g_ready, 4)
                    w, a, ya = rnn_t[:, 0, :], rnn_t[:, 1, :], rnn_t[:, 2 + m % 2, :]
                    if m >= 2:
                        e.wait_ge(ya_lo, m - 1)
                    link(e.tensor_scalar(a, T0[:, m, :], 1.0, None, ALU.add))
                    link(e.reciprocal(w, a))
                    link(e.tensor_scalar(a, T0[:, m, :], -1.0, 1.0, ALU.mult, ALU.add))
                    link(e.tensor_tensor(a, a, w, ALU.mult))
                    z = T1[:, m, :]
                    link(e.scalar_tensor_tensor(z, z, 1.0, xa[:, m, :], ALU.add, ALU.mult))
                    link(e.tensor_tensor(z, z, w, ALU.mult))
                    link(e.tensor_tensor(z, z, rnn_sq[:, m % 2, :], ALU.mult))
                    link(e.tensor_tensor_scan(w, a, z, 0.0, ALU.mult, ALU.add))
                    e.tensor_tensor(ya, w, gg[:, m, :], ALU.mult).then_inc(ya_ready, 1)

            for s in range(S_Q, S_GATE):
                pre(s + 3)
                if s - S_Q < KD:
                    rnn_chunk(s - S_Q)
                if s == S_V:
                    e.wait_ge(qk_ss, 1)
                    link(e.reciprocal(ssqk[:, :, :, :], rqk[:, :, :, :]))
                    e.tensor_scalar(cq[:, 0], ssqk[:, 0], P ** -0.5, None, ALU.mult)
                    e.tensor_scalar(cq[:, 1], ssqk[:, 0], -(P ** -0.5), None, ALU.mult)
                    for h in range(HALVES):
                        kk = k_s[:, h, :].rearrange("p (n d) -> p n d", n=HEADS)
                        ins = e.tensor_tensor(kk, kk, ssqk[:, 1, h, :].unsqueeze(2).to_broadcast([P, HEADS, P]),
                                              ALU.mult)
                    ins.then_inc(qk_scaled, 1)

            def gate_tile(i):
                return (T0 if i < 4 else T1)[:, 2 * (i % 4):2 * (i % 4) + 2, :]

            def gate(s, i):
                normed(GROUP_OF[(s, 0)], gate_tile(i))

            def branch(g, tiles, dst):
                e.wait_ge(group_done, g + 1)
                e.scalar_tensor_tensor(dst[:, tiles, :], dst[:, tiles, :], 1.0,
                                       ps[g % 2][:, :].rearrange("p (m n) -> p m n", m=2),
                                       ALU.add, ALU.mult).then_inc(bank_free["dve"], 1)
                e.wait_ge(bank_free["dve"], emptied(g)[1])

            def merge(i, n0):
                tiles = slice(2 * i, 2 * i + 2)
                e.tensor_tensor(T0[:, tiles, :], T0[:, tiles, :], T1[:, tiles, :], ALU.add).then_inc(merged, 1)
                e.wait_ge(m_hi, n0 + i + 1)
                e.scalar_tensor_tensor(pairs[0][1][:, tiles, :], T0[:, tiles, :], 0.5,
                                       pairs[0][0][:, tiles, :].bitcast(f32), ALU.mult, ALU.subtract).then_inc(m_lo, 1)

            def residual(s, i):
                g = GROUP_OF[(s, 0)]
                e.wait_ge(group_done, g + 1)
                e.tensor_tensor(X[:, 2 * i:2 * i + 2, :], ps[g % 2][:, :].rearrange("p (m n) -> p m n", m=2),
                                X[:, 2 * i:2 * i + 2, :], ALU.add).then_inc(bank_free["dve"], 1)

            e.wait_ge(sink_T, 1)
            link(e.tensor_copy(sinks[:, 0, :], PSB[:, 8:8 + HEADS]))
            e.tensor_scalar(sinks[:, 1, :], sinks[:, 0, :], -1.0, None, ALU.mult).then_inc(sink_ready, 1)
            for s in range(S_GATE, FFN1):
                for step in steps_at(s):
                    att(step)
                if s < S_PR:
                    gate(s, s - S_GATE)
                if S_PR <= s < S_PA:
                    i = s - S_PR
                    e.wait_ge(gate_t, 4)
                    branch(GROUP_OF[(s, 0)], slice(2 * i, 2 * i + 2), T0)
                if S_PA <= s < S_OUT:
                    i = s - S_PA
                    e.wait_ge(gate_t, 8)
                    branch(GROUP_OF[(s, 0)], slice(2 * i, 2 * i + 2), T1)
                    merge(i, 0)
                if S_OUT <= s < FFN1:
                    i = s - S_OUT
                    residual(s, i)
                    norm_lo(1, G2, pairs[2][1], pairs[2][0], (2 * i, 2 * i + 1))
                pre(s + 3)

            def ffn(which, base, n0, n):
                g_up = GROUP_OF[(base, 0)]
                free0 = emptied(g_up)[1]
                if which == 1:
                    e.memset(upn[:, :, 0:FKW - 1], 0.0)
                chain = dve_loop[which - 1]
                LINKS = 5
                state = [0]

                def llink(j, ins):
                    state[0] += 1
                    ins.then_inc(chain, 1)
                    e.wait_ge(chain, j * LINKS + state[0])

                def post(j, pre_a, pre_b, pre_c):
                    state[0] = 0
                    pre_a()
                    bank_u, bank_g = ps[g_up % 2], ps[(g_up + 1) % 2]
                    e.wait_ge(group_done, j * 2 + (g_up + 1))
                    dst = upn[:, :, FKW - 1:] if which == 1 else cv
                    e.tensor_tensor(dst, bank_u[:, :].rearrange("p (m n) -> p m n", m=2), bc2(rstd_bc[:, :], 2),
                                    ALU.mult).then_inc(bank_free["dve"], 1)
                    e.wait_ge(bank_free["dve"], j * 2 + free0)
                    if which == 1:
                        for m in range(2):
                            def col(k):
                                c = j * 2 + (k * FT + m)
                                return fcol[:, bass.ds(c, 1)]
                            llink(j, e.tensor_scalar(cv[:, m, :], upn[:, m, 0:SEQ], col(0), col(FKW), ALU.mult, ALU.add))
                            llink(j, e.scalar_tensor_tensor(cv[:, m, :], upn[:, m, 1:1 + SEQ], col(1), cv[:, m, :],
                                                            ALU.mult, ALU.add))
                            ins = e.scalar_tensor_tensor(cv[:, m, :], upn[:, m, 2:2 + SEQ], col(2), cv[:, m, :],
                                                         ALU.mult, ALU.add)
                            if m == 0:
                                llink(j, ins)
                        ins.then_inc(f_conv, 1)
                    pre_b()
                    e.wait_ge(group_done, j * 2 + (g_up + 2))
                    e.tensor_tensor(gt, bank_g[:, :].rearrange("p (m n) -> p m n", m=2), bc2(rstd_bc[:, :], 2),
                                    ALU.mult).then_inc(bank_free["dve"], 1)
                    e.wait_ge(bank_free["dve"], j * 2 + (free0 + 1))
                    e.wait_ge(f_glu, j + (n0 + 1))
                    e.tensor_tensor(actf, cv, gt, ALU.mult).then_inc(f_act, 1)
                    pre_c()
                    e.wait_ge(f_hi, j + (n0 + 1))
                    e.tensor_tensor(actlo, actf, acthi.bitcast(f32), ALU.subtract).then_inc(f_lo, 1)
                    assert state[0] == (LINKS if which == 1 else 0)

                inv(n, False)
                post(0, lambda: pre(base + 3), lambda: pre(base + 4), lambda: None)
                with e.Fori(1, STEPS - 1) as j:
                    s = j * 3 + (base - 1)
                    post(j, lambda: lo(s + 3, (base + 2) % RING), lambda: lo(s + 4, (base + 3) % RING),
                         lambda: lo(s + 5, (base + 4) % RING))
                last = base + 3 * (STEPS - 1) - 1
                post(STEPS - 1, lambda: pre(last + 3), lambda: pre(last + 4), lambda: pre(last + 5))

            ffn(1, FFN1, 0, 1)
            for b in range(4):
                e.wait_ge(down_bank, b + 1)
                e.tensor_copy(X[:, 2 * b:2 * b + 2, :],
                              ps[2 + b][:, :].rearrange("p (m n) -> p m n", m=2)).then_inc(x_ready, 1)
                if b:
                    norm_lo(2, MIXG, pairs[0][1], pairs[0][0], (2 * b - 2, 2 * b - 1))
            norm_lo(2, MIXG, pairs[0][1], pairs[0][0], (6, 7))
            pre(S2_SEQ + 2)
            inv(2, True)

            def rotate(src1, src2, dst1, dst2, cos, sin, n, w, done=None):
                def t3(i):
                    return rope_t[:, i, 0:n * w].rearrange("p (n w) -> p n w", n=n)
                c = cos.unsqueeze(1).to_broadcast([P, n, w])
                s_ = sin.unsqueeze(1).to_broadcast([P, n, w])
                e.tensor_tensor(t3(0), src1, c, ALU.mult)
                e.tensor_tensor(t3(1), src2, s_, ALU.mult)
                e.tensor_tensor(t3(2), src2, c, ALU.mult)
                link(e.tensor_tensor(t3(3), src1, s_, ALU.mult))
                link(e.tensor_tensor(dst1, t3(0), t3(1), ALU.subtract))
                ins = e.tensor_tensor(dst2, t3(2), t3(3), ALU.add)
                if done:
                    ins.then_inc(done, 1)
                    e.wait_ge(done, 1)
                else:
                    link(ins)

            e.wait_ge(in_misc, 16 * 6)
            for s in range(S2_SEQ, S2_GA):
                pre(s + 3)
                i = s - S2_SEQ
                if i in (2, 3):
                    h = i - 2
                    e.wait_ge(bank_free["act"], U2_FREE[1])
                    for a in range(2):
                        src = u2[:, h, 256 * a:256 * a + 256].rearrange("p (n d) -> p n d", n=4)
                        dst = q_r[:, h, :].rearrange("p (n b d) -> p b n d", b=2, d=64)[:, a]
                        rotate(src[:, :, 0:32], src[:, :, 32:64], dst[:, :, 0:32], dst[:, :, 32:64],
                               ropeA[:, 0, h, :], ropeA[:, 1, h, :], 4, 32)
                if i in (4, 5):
                    h = i - 4
                    e.wait_ge(bank_free["act"], U2_FREE[2])
                    src = u2[:, h, OFF_KA:OFF_KA + P].rearrange("p (n d) -> p n d", n=2)
                    dst = k_r[:, h, :].rearrange("p (n d) -> p n d", n=2)
                    rotate(src[:, :, 0:32], src[:, :, 32:64], dst[:, :, 0:32], dst[:, :, 32:64],
                           ropeA[:, 0, h, :], ropeA[:, 1, h, :], 2, 32, rope_q if h else None)
            e.wait_ge(cq_ss, 1)
            e.reciprocal(ss2[:, :, :], r2[:, :, :]).then_inc(cq_r, 1)
            e.wait_ge(bank_free["act"], U2_FREE[5])
            for h in range(HALVES):
                src = u2[:, h, OFF_KR:OFF_KR + ROPE].unsqueeze(1)
                dst = krr[:, h, :].unsqueeze(1)
                rotate(src[:, :, 0:16], src[:, :, 16:32], dst[:, :, 0:16], dst[:, :, 16:32],
                       ropeB[:, 0, h, :], ropeB[:, 1, h, :], 1, 16)
                ins = e.tensor_copy(kf[:, h, :, NOPE:MLA_D],
                                    krr[:, h, :].unsqueeze(1).to_broadcast([P, HEADS, ROPE]))
            ins.then_inc(rope_k, 1)

            def cq_parts(r):
                e.wait_ge(cq_hi, (2, 4, 5)[r])
                for c in CQ_ROUND[r]:
                    e.scalar_tensor_tensor(pairs[1][1][:, c, :],
                                           (PSA, PSB, PSA)[r][:, SEQ * (c % 2):SEQ * (c % 2) + SEQ],
                                           pcol[:, QLG + c:QLG + c + 1],
                                           pairs[1][0][:, c, :].bitcast(f32), ALU.mult,
                                           ALU.subtract).then_inc(cq_lo, 1)

            for s in range(S2_GA, FFN2):
                for step in steps_at(s):
                    att(step)
                if gate_of(s) is not None:
                    gate(s, gate_of(s))
                if S2_OSWA <= s < S2_OMLA:
                    e.wait_ge(gate_t, 12)
                    for i in range(2):
                        c = 4 * (s - S2_OSWA) + 2 * i
                        branch(GROUP_OF[(s, i)], slice(c, c + 2), T0)
                if S2_OMLA <= s < S2_OUT:
                    e.wait_ge(gate_t, 16)
                    for i in range(2):
                        c = 2 * (s - S2_OMLA) + i
                        branch(GROUP_OF[(s, i)], slice(2 * c, 2 * c + 2), T1)
                        tiles = slice(2 * c, 2 * c + 2)
                        e.tensor_tensor(T0[:, tiles, :], T0[:, tiles, :], T1[:, tiles, :], ALU.add).then_inc(merged, 1)
                        e.wait_ge(m_hi, 4 + c + 1)
                        e.scalar_tensor_tensor(pairs[0][1][:, tiles, :], T0[:, tiles, :], 0.5,
                                               pairs[0][0][:, tiles, :].bitcast(f32), ALU.mult,
                                               ALU.subtract).then_inc(m_lo, 1)
                if S2_OUT <= s < FFN2:
                    i = s - S2_OUT
                    residual(s, i)
                    norm_lo(3, FFNG, pairs[2][1], pairs[2][0], (2 * i, 2 * i + 1))
                pre(s + 3)
                if s == S2_GA + 1:
                    cq_parts(0)
                    cq_parts(1)
                if s == S2_UQ:
                    cq_parts(2)
                if s == S2_UKV:
                    e.wait_ge(bank_free["act"], emptied(GROUP_OF[(S2_UKV - 1, 1)])[1])
                    for h in range(HALVES):
                        src = qb[:, h]
                        rotate(src[:, :, 64:80], src[:, :, 80:96], src[:, :, 64:80], src[:, :, 80:96],
                               ropeB[:, 0, h, :], ropeB[:, 1, h, :], 8, 16, mla_ready if h else None)
            ffn(2, FFN2, STEPS, 3)
            e.wait_ge(fin_T, 1)
            e.tensor_copy(fing[:, 0:512], ps[0][:, :])
            e.tensor_copy(fing[:, 512:D], ps[1][:, :]).then_inc(fin_Te, 1)
            e.wait_ge(fin_Te, 1)
            for h in range(HALVES):
                e.wait_ge(fin_root, h + 1)
                link(e.reciprocal(finr[:, h:h + 1], fin2[:, 2 + h:3 + h]))
                for c in range(2):
                    cols = slice(512 * c, 512 * c + 512)
                    ins = e.scalar_tensor_tensor(outp[:, h, cols], ps[2 + 2 * h + c][:, :], finr[:, h:h + 1],
                                                 fing[:, cols], ALU.mult, ALU.mult)
                ins.then_inc(y_ready, 1)

        @block.gpsimd
        def _(e):
            for s in range(S_XR, S_G):
                e.wait_ge(xa_hi, s + 1)
                e.tensor_tensor(pairs[1][1][:, 2 * s:2 * s + 2, :], xa[:, 2 * s:2 * s + 2, :],
                                pairs[1][0][:, 2 * s:2 * s + 2, :].bitcast(f32), ALU.subtract).then_inc(xa_lo, 1)
            e.wait_ge(group_done, GROUP_OF[(S_RI, 7)] + 1)
            for m in range(KD):
                ya = rnn_t[:, 2 + m % 2, :]
                e.wait_ge(ya_ready, m + 1)
                e.tensor_copy(pairs[1][0][:, m, :], ya).then_inc(ya_hi, 1)
                e.wait_ge(ya_hi, m + 1)
                e.tensor_tensor(pairs[1][1][:, m, :], ya, pairs[1][0][:, m, :].bitcast(f32),
                                ALU.subtract).then_inc(ya_lo, 1)

        @block.tensor
        def _(e):
            def three(out, lhs, rhs, first, last):
                e.matmul(out, lhs[0], rhs[0], start=first, stop=False, skip_group_check=True)
                e.matmul(out, lhs[0], rhs[1], start=False, stop=False, skip_group_check=True)
                return e.matmul(out, lhs[1], rhs[0], start=False, stop=last, skip_group_check=True)

            def bank_ready(g):
                if g >= 2:
                    who, n = emptied(g - 2)
                    e.wait_ge(bank_free[who], n)

            def weights(slot, k, cols, width):
                return tuple(w[slot][:, width * k:width * (k + 1)][:, cols] for w in (whi, wlo))

            def always(k):
                pass

            def feature_tiles(out, slot, kk, width, act, tiles, k0=0, ready=always):
                for k in range(kk):
                    ready(k)
                    for n, (c, o) in enumerate(tiles):
                        ins = three(out[:, o:o + SEQ], weights(slot, k, slice(c, c + P), width),
                                    (act[0][:, k0 + k, :], act[1][:, k0 + k, :]), n == 0 and k == 0, k == kk - 1)
                return ins

            def positions(out, slot, kk, width, act, cols, halves_, k0=0, ready=always):
                for k in range(kk):
                    ready(k)
                    for n, (h, o) in enumerate(halves_):
                        ins = three(out[:, o:o + cols.stop - cols.start],
                                    tuple(a[:, k0 + k, P * h:P * h + P] for a in act),
                                    weights(slot, k, cols, width), n == 0 and k == 0, k == kk - 1)
                return ins

            def sums(n, seq):
                e.wait_ge(sq_ready, 4 * n + 4)
                e.wait_ge(consts, 1)
                if seq:
                    for h in range(HALVES):
                        for c in range(KD):
                            e.matmul(PSB[:, h:h + 1], SQ[:, c, P * h:P * h + P], ones[:, 0:1],
                                     start=(c == 0 and h == 0), stop=(c == KD - 1), skip_group_check=True)
                for c in range(KD):
                    ins = e.matmul(PSA[:, 0:SEQ], ones[:, :], SQ[:, c, :], start=(c == 0), stop=(c == KD - 1))
                ins.then_inc(ssum, 1)

            def att(step):
                kind_base = 0 if step < 100 else 100
                u = unit_of(step)
                if u is not None and not (8 <= u < 16 and u % 2):
                    n_t = t_count(u)
                    if n_t >= 2:
                        e.wait_ge(aTe, n_t - 1)
                    if u == 0:
                        e.wait_ge(qk_scaled, 1)
                    if u == 8:
                        e.wait_ge(rope_q, 1)
                    if u == 16:
                        e.wait_ge(mla_ready, 1)
                        e.wait_ge(rope_k, 1)
                        e.wait_ge(bank_free["act"], emptied(GROUP_OF[(S2_UKV, 3)])[1])
                    for h in range(HALVES):
                        for i in range(2):
                            if u < 8:
                                src = (q_s, k_s)[i][:, h, P * u:P * u + P]
                            elif u < 16:
                                c = (u - 8) // 2
                                src = q_r[:, h, P * c:P * c + P] if i == 0 else k_r[:, h, :]
                            else:
                                src = (qb, kf)[i][:, h, u - 16, :]
                            d = MLA_D if u >= 16 else P
                            ins = e.transpose(PST[0:d, SEQ * i + P * h:SEQ * i + P * h + P], src, ident[:, :])
                    ins.then_inc(aT, 1)
                u = unit_of(step - LAG_S) if step - LAG_S >= kind_base else None
                if u is not None:
                    e.wait_ge(aTe, t_count(u))
                    if u >= 1:
                        e.wait_ge(aM, u)
                    b = tbuf(u)
                    rows = slice(0, P) if u < 8 else slice(64 * (u % 2), 64 * (u % 2) + 64) if u < 16 \
                        else slice(0, MLA_D)
                    e.matmul(PSS[:, 0:P], qT[rows, b, 0:P], kT[rows, b, 0:P], start=True, stop=True)
                    e.matmul(PSS[:, P:3 * P], qT[rows, b, P:SEQ], kT[rows, b, :], start=True,
                             stop=True).then_inc(aS, 1)
                u = unit_of(step - LAG_PT) if step - LAG_PT >= kind_base else None
                if u is not None:
                    e.wait_ge(aN, u + 1)
                    if u >= 1:
                        e.wait_ge(aPTe, u)
                    for i in range(3):
                        ins = e.transpose(PSPT[:, P * i:P * i + P], pr[:, u % 3, P * i:P * i + P], ident[:, :])
                    ins.then_inc(aPT, 1)
                u = unit_of(step - LAG_PV) if step - LAG_PV >= kind_base else None
                if u is not None:
                    e.wait_ge(aPTe, u + 1)
                    if u >= 1:
                        e.wait_ge(aL, u)
                    if u < 8:
                        v = [v_s[:, h, P * u:P * u + P] for h in range(2)]
                    elif u < 16:
                        v = [u2[:, h, OFF_VA:OFF_VA + P] for h in range(2)]
                    else:
                        c = (u - 16) // 2
                        v = [vb[:, h, P * c:P * c + P] for h in range(2)]
                    e.matmul(PSPV[:, 0:SEQ], v[0], pT[:, u % 2, 0:SEQ], start=True, stop=False,
                             skip_group_check=True)
                    e.matmul(PSPV[:, P:SEQ], v[1], pT[:, u % 2, SEQ:3 * P], start=False, stop=True,
                             skip_group_check=True).then_inc(aPV, 1)

            e.wait_ge(in_x, 32)
            for k in range(KD):
                for h in range(HALVES):
                    o = SEQ * (k % 2) + P * h
                    ins = e.transpose(ps[2 + k // 2][:, o:o + P], xpos[:, h, P * k:P * k + P], ident[:, :])
                if k % 2:
                    ins.then_inc(xT_done, 1)
            e.wait_ge(in_par, 16 * 15)
            e.transpose(PSA[:, 0:PROWS], prow[0:PROWS, :], ident[0:PROWS, 0:PROWS])
            e.transpose(PSB[:, 0:FROWS], frow[0:FROWS, :], ident[0:FROWS, 0:FROWS]).then_inc(par_T, 1)

            def slab(s, act, layout="feature", ready=always, hook=None):
                e.wait_ge(lo_ready, s + 1)
                slot = s % RING
                kind = PLAN[s][1]
                n = sum(1 for x in GROUPS if x[0] == s)
                for i in range(n):
                    g = GROUP_OF[(s, i)]
                    bank_ready(g)
                    out = ps[g % 2]
                    steps = steps_at(s)

                    def at(k, steps=steps, i=i):
                        places = [(0, 0), (0, 4) if n == 1 else (1, 0)]
                        for place, step in zip(places, steps):
                            if place == (i, k):
                                att(step)
                        if hook and (i, k) == (0, 6):
                            hook()
                        ready(k)

                    if kind == "blocks":
                        for m in range(2):
                            blk = 2 * (i % 4) + m
                            c = 1024 * (i // 4) + P * blk
                            ins = three(out[:, SEQ * m:SEQ * m + SEQ], tuple(w[slot][:, c:c + P] for w in (whi, wlo)),
                                        (act[0][:, blk, :], act[1][:, blk, :]), m == 0, True)
                    elif layout == "feature" and kind == "cols":
                        ins = feature_tiles(out, slot, KD, WIDE, act, [(0, 0), (P, SEQ)], ready=at)
                    elif layout == "feature":
                        k0 = 4 if s >= S2_OMLA else 0
                        ins = feature_tiles(out, slot, 4, 512, act, [(2 * P * i, 0), (2 * P * i + P, SEQ)], k0=k0,
                                            ready=at)
                    elif kind == "cols":
                        width = min(WIDE, t[PLAN[s][0]].shape[2] - PLAN[s][2])
                        if s == S2_GA - 1:
                            width = SEQ_COLS - PLAN[s][2]
                        ins = positions(out, slot, KD, WIDE, act, slice(0, width), [(0, 0), (1, 256)],
                                        ready=at)
                    elif kind == "rows3":
                        ins = positions(out, slot, 3, QLAT, act, slice(0, QLAT), [(i, 0)], ready=at)
                    else:
                        h, c = divmod(i, 2)
                        ins = positions(out, slot, 2, 1024, act, slice(512 * c, 512 * c + 512), [(h, 0)], k0=3,
                                        ready=at)
                    ins.then_inc(group_done, 1)

            for s in range(S_XR, FFN1):
                if s == S_RI:
                    e.wait_ge(xa_lo, 4)
                if s == S_V:
                    e.wait_ge(in_misc, 16 * 6)
                    e.wait_ge(rstd_ready, 1)
                    e.matmul(PSB[:, 8:8 + HEADS], ones[0:1, :], rowt[:, :], start=True, stop=True).then_inc(sink_T, 1)
                ready = {
                    S_XR: lambda k: e.wait_ge(h_lo, k + 1),
                    S_PR: lambda k: e.wait_ge(ya_lo, k + 1),
                    S_PA: lambda k: e.wait_ge(aL, k + 1),
                    S_OUT: lambda k: e.wait_ge(m_lo, k // 2 + 1),
                }.get(s, always)
                act = pairs[1] if s == S_RI or S_PR <= s < S_PA else pairs[2] if S_PA <= s < S_OUT else pairs[0]
                slab(s, act, "position" if S_Q <= s < S_GATE else "feature", ready)
                if s == S_XR:
                    sums(0, True)

            def ffn(which, base, n, n0):
                act = pairs[2]
                g_up = GROUP_OF[(base, 0)]
                free0 = emptied(g_up)[1]
                def residual():
                    if which == 1:
                        for c in range(KD):
                            e.matmul(ps[2 + c // 2][:, SEQ * (c % 2):SEQ * (c % 2) + SEQ], ident[:, :], X[:, c, :],
                                     start=(c % 2 == 0), stop=False, skip_group_check=True)
                    else:
                        for h in range(HALVES):
                            for c in range(KD):
                                e.matmul(ps[2 + 2 * h + c // 4][:, P * (c % 4):P * (c % 4) + P],
                                         X[:, c, P * h:P * h + P], ident[:, :], start=(c % 4 == 0), stop=False,
                                         skip_group_check=True)

                def wide(j, s, slot, i, free, ready=always):
                    e.wait_ge(lo_ready, s + 1)
                    free()
                    feature_tiles(ps[(g_up + i) % 2], slot, KD, WIDE, act, [(0, 0), (P, SEQ)],
                                  ready=ready).then_inc(group_done, 1)

                def down(j, s, slot, last=False):
                    e.wait_ge(lo_ready, s + 1)
                    e.wait_ge(f_lo, j + (n0 + 1))
                    if which == 1:
                        for c in range(KD):
                            for k in range(2):
                                ins = three(ps[2 + c // 2][:, SEQ * (c % 2):SEQ * (c % 2) + SEQ],
                                            weights(slot, k, slice(P * c, P * c + P), D),
                                            (acthi[:, k, :], actlo[:, k, :]), False, False)
                            if last and c % 2 and c < KD - 1:
                                ins.then_inc(down_bank, 1)
                    else:
                        for h in range(HALVES):
                            if last and h:
                                ins.then_inc(down_bank, 1)
                            for k in range(2):
                                for c in range(2):
                                    ins = three(ps[2 + 2 * h + c][:, :],
                                                (acthi[:, k, P * h:P * h + P], actlo[:, k, P * h:P * h + P]),
                                                weights(slot, k, slice(512 * c, 512 * c + 512), D), False, False)
                    ins.then_inc(down_bank if last else down_used, 1)

                for i in range(2):
                    g = g_up + i
                    wide(0, base + i, (base + i) % RING, i, lambda: bank_ready(g),
                         (lambda k: e.wait_ge(h_lo, KD * n + k + 1)) if i == 0 else always)
                    if i == 0:
                        sums(n, False)
                        residual()
                with e.Fori(1, STEPS) as j:
                    s = j * 3 + (base - 1)
                    for i in range(2):
                        wide(j, s + i, (base + 2 + i) % RING, i,
                             lambda: e.wait_ge(bank_free["dve"], (j - 1) * 2 + (free0 + i)))
                    down(j - 1, s + 2, (base + 4) % RING)
                last = base + 3 * STEPS - 1
                down(STEPS - 1, last, last % RING, True)

            ffn(1, FFN1, 1, 0)

            def cq_transposes(r):
                e.wait_ge(cq_s, 1)
                if r == 2:
                    e.wait_ge(cq_lo, 2)
                for c in CQ_ROUND[r]:
                    for h in range(HALVES):
                        o = SEQ * (c % 2) + P * h
                        ins = e.transpose((PSA, PSB, PSA)[r][:, o:o + P],
                                          u2[:, h, OFF_QL + P * c:OFF_QL + P * c + P], ident[:, :])
                ins.then_inc(cq_T, 1)

            for s in range(S2_SEQ, FFN2):
                if s == S2_UQ + 1:
                    cq_transposes(2)
                ready = {
                    S2_SEQ: lambda k: e.wait_ge(h_lo, 2 * KD + k + 1),
                    S2_UQ: lambda k: e.wait_ge(cq_lo, k + 1),
                    S2_UKV: lambda k: e.wait_ge(cq_lo, 3 + k + 1),
                    S2_OSWA: lambda k: e.wait_ge(aL, 8 + 2 * k + 2),
                    S2_OMLA: lambda k: e.wait_ge(aL, 16 + 2 * k + 2),
                    S2_OUT: lambda k: e.wait_ge(m_lo, 4 + k // 2 + 1),
                }.get(s, always)
                hook = (lambda: (cq_transposes(0), cq_transposes(1))) if s == S2_GA + 1 else None
                act = pairs[1] if S2_UQ <= s <= S2_UKV else pairs[2] if S2_OSWA <= s < S2_OUT else pairs[0]
                slab(s, act, "position" if s < S2_GA or S2_UQ <= s <= S2_UKV else "feature", ready, hook)
                if s == S2_SEQ:
                    sums(2, True)
            ffn(2, FFN2, 3, STEPS)
            e.wait_ge(in_x, 48)
            e.wait_ge(bank_free["dve"], emptied(GROUP_OF[(FFN2, 2 * STEPS - 1)])[1])
            for c in range(2):
                ins = e.matmul(ps[c][:, :], ones[0:1, :], frow_g[:, 512 * c:512 * c + 512], start=True, stop=True)
            ins.then_inc(fin_T, 1)


def t_count(u):
    return u + 1 if u < 8 else 8 + (u - 8) // 2 + 1 if u < 16 else 12 + u - 16 + 1


def tbuf(u):
    return (t_count(u) - 1) % 2


def last_reader_of_tbuf(u):
    n = t_count(u) - 2
    return max(v for v in range(24) if t_count(v) == n) + 1


def swa_head(u):
    return (u - 8) // 2 + 4 * ((u - 8) % 2)


def yb_place(u):
    if u < 8:
        return slice(0, P), u
    b = u % 2
    return slice(64 * b, 64 * b + 64), (u - 8) // 2


_INS = ['x', 'norm1_g', 'w_in', 'conv_w', 'conv_b', 'w_r', 'b_r', 'w_i', 'b_i', 'lru_lambda', 'q_norm_g',
        'k_norm_g', 'w_proj_rnn', 'w_proj_attn', 'w_out', 'norm2_g', 'w_up', 'w_gate', 'ffn_conv_w',
        'ffn_conv_b', 'w_down', 'mix_norm_g_2', 'w_in_2', 'swa_sinks_2', 'q_norm_g_2', 'w_uq_2',
        'kv_norm_g_2', 'w_ukv_2', 'w_o_swa_2', 'w_o_mla_2', 'w_out_2', 'ffn_norm_g_2', 'w_gate_2',
        'w_up_2', 'w_down_2', 'final_norm_g_2']


def constants():
    q = np.arange(P)[:, None]
    k = np.arange(P)[None, :]
    causal = np.where(k <= q, 0.0, NEG)
    before = np.where(k > q, 0.0, NEG)
    masks = np.stack([np.concatenate([causal, 0 * causal, causal], 1),
                      np.concatenate([causal, before, causal], 1)], 1).astype(np.float32)

    def rope(dim):
        inv = np.float32(10000.0) ** (-np.arange(0, dim, 2, dtype=np.float32) / np.float32(dim))
        ang = np.arange(SEQ, dtype=np.float32)[:, None] * inv.astype(np.float32)[None, :]
        return np.stack([np.cos(ang), np.sin(ang)]).astype(np.float32)
    return {"ident": np.eye(P, dtype=np.float32), "masks": masks, "rope_a": rope(64), "rope_b": rope(32)}


def kernel(**inputs):
    import concourse.bacc as _bacc
    from concourse.bass_utils import run_bass_kernel_spmd as _run

    nc = _bacc.Bacc("TRN2", target_bir_lowering=False, num_devices=1)
    arrays, t = {}, {}
    given = {n: np.ascontiguousarray(inputs[n]) for n in _INS}
    given.update(constants())
    for name, a in given.items():
        arrays[f"in_{name}"] = a
        t[name] = nc.dram_tensor(f"in_{name}", a.shape, mybir.dt.from_np(a.dtype), kind="ExternalInput").ap()
    t["final_norm_g"] = t["final_norm_g_2"]
    t["out"] = nc.dram_tensor("out", (1, SEQ, D), mybir.dt.float32, kind="ExternalOutput").ap()
    program(nc, t)
    r = _run(nc, [arrays], core_ids=[0])
    return r.results[0]["out"]
```

```python
import numpy as np
import concourse.bass as bass
from concourse import mybir
from contextlib import ExitStack

P = 128
SEQ = 256
HALVES = SEQ // P
D = 1024
KD = D // P
FF = 2816
FT = FF // P
HEADS = 8
SLAB = 2048
WIDE = SLAB // KD
RING = 3
EPS = 1e-6
NEG = -1e30
KW = 4
FKW = 3
D_IN2 = 3488
SEQ_COLS = 1440
QLAT, KVLAT = 384, 256
OFF_KA, OFF_VA, OFF_QL, OFF_KVL, OFF_KR = 512, 640, 768, 1152, 1408
MLA_D, NOPE, ROPE, VD = 96, 64, 32, 64

PARAMS = ("norm1_g", "conv_w", "conv_b", "b_r", "b_i", "lru_lambda", "norm2_g", "mix_norm_g_2", "ffn_norm_g_2",
          "q_norm_g_2", "kv_norm_g_2", "q_norm_g", "k_norm_g", "ffn_conv_w", "ffn_conv_b")
PCOLS = (KD, KW * KD, KD, KD, KD, KD, KD, KD, KD, QLAT // P, KVLAT // P, 1, 1, FKW * FT, FT)
G1, CONVW, CONVB, BR, BI, LAM, G2, MIXG, FFNG, QLG, KVLG, QG, KG, FCONV, _ = (
    sum(PCOLS[:i]) for i in range(len(PCOLS)))


def slab_plan():
    plan = [("w_in", "cols", WIDE * i) for i in range(8)]
    plan += [("w_ri", "blocks", 0)]
    plan += [("w_in", "cols", WIDE * i) for i in range(8, 28)]
    plan += [(w, "cols", WIDE * i) for w in ("w_proj_rnn", "w_proj_attn", "w_out") for i in range(4)]
    ffn1 = len(plan)
    plan += [("ffn1", "loop", i) for i in range(3 * (FF // WIDE))]
    plan += [("w_in_2", "cols", WIDE * i) for i in range(6)]
    plan += [("w_in_2", "cols", SEQ_COLS + WIDE * i) for i in range(4)]
    plan += [("w_uq_2", "rows3", 0), ("w_uq_2", "rows3", QLAT), ("w_ukv_2", "rows2", 0)]
    plan += [("w_in_2", "cols", SEQ_COLS + WIDE * i) for i in range(4, 8)]
    plan += [("w_o_swa_2", "swa", 512 * i) for i in range(2)]
    plan += [("w_o_mla_2", "rows4", 512 * i) for i in range(2)]
    plan += [("w_out_2", "cols", WIDE * i) for i in range(4)]
    ffn2 = len(plan)
    plan += [("ffn2", "loop", i) for i in range(3 * (FF // WIDE))]
    return plan, ffn1, ffn2


PLAN, FFN1, FFN2 = slab_plan()
SLABS = len(PLAN)
STEPS = FF // WIDE
S_XR, S_G, S_RI, S_Q, S_K, S_V, S_GATE, S_PR, S_PA, S_OUT = 0, 4, 8, 9, 13, 17, 21, 29, 33, 37
S_RNN = S_Q + 3
S2_SEQ, S2_GA, S2_UQ, S2_UKV, S2_GB = FFN1 + 33, FFN1 + 39, FFN1 + 43, FFN1 + 45, FFN1 + 46
S2_OSWA, S2_OMLA, S2_OUT = FFN1 + 50, FFN1 + 52, FFN1 + 54


def group_plan():
    groups = []
    for s, (_, kind, _) in enumerate(PLAN):
        if kind == "loop":
            if s in (FFN1, FFN2):
                groups += [(s, i, "dve") for i in range(2 * STEPS)]
        elif kind == "blocks":
            groups += [(s, i, "act") for i in range(8)]
        elif S_Q <= s < S_GATE or S2_SEQ <= s < S2_GA:
            groups.append((s, 0, "act"))
        elif S2_UQ <= s < S2_UKV:
            groups += [(s, i, "act") for i in range(2)]
        elif s == S2_UKV:
            groups += [(s, i, ("dve", "act")[i % 2]) for i in range(4)]
        elif S2_OSWA <= s < S2_OUT:
            groups += [(s, i, "dve") for i in range(2)]
        else:
            groups.append((s, 0, "dve"))
    return groups


GROUPS = group_plan()
GROUP_OF = {(s, i): g for g, (s, i, _) in enumerate(GROUPS)}


def emptied(g):
    who = GROUPS[g][2]
    return who, sum(1 for x in GROUPS[:g + 1] if x[2] == who)


LAG_S, LAG_E, LAG_N, LAG_PT, LAG_PV = 1, 2, 3, 4, 5


def steps_at(s):
    if S_GATE <= s < S_PR + LAG_PV:
        return [s - S_GATE]
    if S2_GA <= s <= S2_OMLA:
        first = sum(STEPS_AT[:s - S2_GA])
        return [100 + first + i for i in range(STEPS_AT[s - S2_GA])]
    return []


STEPS_AT = [0, 2, 2, 1, 1, 1, 1, 2, 2, 2, 2, 2, 2, 1]


def early_att(s):
    return S_GATE < s < S_PA or S2_GA < s < S2_OUT


def late_cut(s):
    return S2_UQ <= s <= S2_UKV


def gate_of(s):
    if S2_GA <= s < S2_UQ:
        return s - S2_GA
    if S2_GB <= s < S2_OSWA:
        return s - S2_GB + S2_UQ - S2_GA
    return None


def unit_of(step):
    if 0 <= step < HEADS:
        return step
    if 100 <= step < 100 + 2 * HEADS:
        return step - 100 + HEADS
    return None


def program(nc, t):
    f32, f32r = mybir.dt.float32, mybir.dt.float32r
    ALU, ACT, AX = mybir.AluOpType, mybir.ActivationFunctionType, mybir.AxisListType.X
    with ExitStack() as ctx:
        def sb(name, shape, dt=f32):
            return ctx.enter_context(nc.sbuf_tensor(name, shape, dt))

        def sem(name):
            return ctx.enter_context(nc.semaphore(name))

        raw = [sb(f"raw{i}", [P, SLAB]) for i in range(RING)]
        whi = [sb(f"whi{i}", [P, SLAB], f32r) for i in range(RING)]
        wlo = [sb(f"wlo{i}", [P, SLAB], f32r) for i in range(RING)]
        pairs = [(sb(f"ahi{i}", [P, KD, SEQ], f32r), sb(f"alo{i}", [P, KD, SEQ], f32r)) for i in range(3)]
        X = sb("x_res", [P, KD, SEQ])
        XA = sb("xa", [P, SLAB])
        GG = sb("gg", [P, SLAB])
        VV = sb("vv", [P, SLAB])
        T0 = sb("gate0", [P, KD, SEQ])
        T1 = sb("gate1", [P, KD, SEQ])
        QK = sb("qk", [P, 2 * SLAB])
        qkT = sb("qkT", [P, 2, 2, SEQ])
        qT, kT = qkT[:, :, 0, :], qkT[:, :, 1, :]
        sm = sb("sm", [P, 2, 3 * P])
        pr = sb("pr", [P, 3, 3 * P])
        pT = sb("pT", [P, 2, 3 * P])
        masks = sb("masks", [P, 2, 3 * P])
        ident = sb("ident", [P, P])
        ones = sb("ones", [P, P])
        par = sb("params", [P, sum(PCOLS)])
        halfb = sb("halfb", [P, 16])
        sp = sb("sp", [P, 8, KD])
        qkg = sb("qkg", [P, 1])
        epst = sb("epst", [P, 1])
        ropeA = sb("ropeA", [P, 2, HALVES, 32])
        ropeB = sb("ropeB", [P, 2, HALVES, 16])
        krr = sb("krr", [P, HALVES, ROPE])
        sinks = sb("sinks", [P, 2, HEADS])
        rowt = sb("rowt", [1, HEADS])
        root = sb("root", [P, SEQ])
        root2 = sb("root2", [P, 2])
        rstd_bc = sb("rstd_bc", [P, SEQ])
        rstd_sq = sb("rstd_sq", [P, 2])
        ssqk = sb("ssqk", [P, 2, HALVES, HEADS])
        rqk = sb("rqk", [P, 2, HALVES, HEADS])
        cq = sb("cq", [P, 2, HALVES, HEADS])
        ss2 = sb("ss2", [P, 2, 2])
        r2 = sb("r2", [P, 2, 2])
        mx = sb("mx", [P, 2, 2])
        nb = sb("nb", [P, 3, 2])
        sums = sb("sums", [P, 3, 2])
        esink = sb("esink", [P, 3, 2])
        rinv = sb("rinv", [P, 2, 2])
        junk = pT[:, 0, :]
        fin = sb("fin", [P, 4])
        fin2 = sb("fin2", [P, 4])
        finr = sb("finr", [P, 2])

        pcol, fcol = par[:, 0:FCONV], par[:, FCONV:]
        SQ = VV[:, :].rearrange("p (k n) -> p k n", k=KD)
        xrp = QK[:, 0:4 * (SEQ + KW - 1)].rearrange("p (b m n) -> p b m n", b=2, m=2)
        decay = VV[:, :].rearrange("p (k n) -> p k n", k=KD)
        xa = XA[:, :].rearrange("p (k n) -> p k n", k=KD)
        gg = GG[:, :].rearrange("p (k n) -> p k n", k=KD)
        q_s = QK[:, 0:SLAB].rearrange("p (h d) -> p h d", h=HALVES)
        k_s = QK[:, SLAB:2 * SLAB].rearrange("p (h d) -> p h d", h=HALVES)
        v_s = VV[:, :].rearrange("p (h d) -> p h d", h=HALVES)
        rnn_t = pr[:, :, :].rearrange("p a n -> p (a n)")[:, 0:4 * SEQ].rearrange("p (a n) -> p a n", a=4)
        rnn_sq = sm[:, :, :].rearrange("p a n -> p (a n)")[:, 0:2 * SEQ].rearrange("p (a n) -> p a n", a=2)
        rope_t = T1[:, 0:4, :]
        def kv_parts(bank, h, c):
            src = bank[:, :].rearrange("p (n d) -> p n d", n=4)
            return ((kf[:, h, 4 * c:4 * c + 4, 0:NOPE], src[:, :, 0:NOPE]),
                    (vb[:, h, 4 * VD * c:4 * VD * c + 4 * VD].rearrange("p (n d) -> p n d", n=4), src[:, :, NOPE:P]))

        u2 = QK[:, 0:HALVES * SEQ_COLS].rearrange("p (h d) -> p h d", h=HALVES)
        vb = QK[:, HALVES * SEQ_COLS:HALVES * SEQ_COLS + HALVES * HEADS * VD].rearrange(
            "p (h d) -> p h d", h=HALVES)
        q_r = VV[:, 0:1024].rearrange("p (h d) -> p h d", h=HALVES)
        k_r = VV[:, 1024:1280].rearrange("p (h d) -> p h d", h=HALVES)
        qb = XA[:, 0:HALVES * HEADS * MLA_D].rearrange("p (h n d) -> p h n d", h=HALVES, n=HEADS)
        qbf = XA[:, 0:HALVES * HEADS * MLA_D].rearrange("p (h d) -> p h d", h=HALVES)
        kf = GG[:, 0:HALVES * HEADS * MLA_D].rearrange("p (h n d) -> p h n d", h=HALVES, n=HEADS)
        upn = QK[:, 0:2 * (SEQ + FKW - 1)].rearrange("p (m n) -> p m n", m=2)
        cv = QK[:, 1024:1536].rearrange("p (m n) -> p m n", m=2)
        gt = QK[:, 1536:2048].rearrange("p (m n) -> p m n", m=2)
        actf = QK[:, 2048:2560].rearrange("p (m n) -> p m n", m=2)
        act_parts = [tuple(a[:, 2 * i:2 * i + 2, :] for a in pairs[1]) for i in range(2)]
        fing = T0[:, 0:4, :].rearrange("p k n -> p (k n)")
        frow_g = QK[0:1, 3072:4096]
        outp = GG[:, :].rearrange("p (h d) -> p h d", h=HALVES)

        ps = [ctx.enter_context(nc.psum_tensor(f"ps{i}", [P, 512], f32)) for i in range(8)]
        PST, PSS, PSPT, PSPV, PSA, PSB = ps[2], (ps[3], ps[7]), (ps[4], ps[6]), ps[5], ps[6], ps[7]

        in_x = [sem("in_x0"), sem("in_x1")]
        in_par, in_misc, in_fing, out_done = sem("in_par"), sem("in_misc"), sem("in_fing"), sem("out_done")
        raw_in = [sem(f"raw_in{i}") for i in range(RING)]
        hi_ready, lo_ready, down_used = sem("hi_ready"), sem("lo_ready"), sem("down_used")
        group_done = sem("group_done")
        bank_free = {"act": sem("bank_free_act"), "dve": sem("bank_free_dve")}
        act_step, dve_step, pool_step = sem("act_step"), sem("dve_step"), sem("pool_step")
        dve_loop = [sem("dve_loop0"), sem("dve_loop1")]
        sp_exp, consts, tap0 = sem("sp_exp"), sem("consts"), sem("conv_tap0")
        sp_in, sp_ready = sem("sp_in"), sem("sp_ready")
        x_ready, first_hi, first_lo = sem("x_ready"), sem("first_hi"), sem("first_lo")
        h_hi, h_lo, sq_ready, ssum, rms_root, rstd_ready, rms_root2, rstd2_ready = (sem(n) for n in (
            "h_hi", "h_lo", "sq_ready", "ssum", "rms_root", "rstd_ready", "rms_root2", "rstd2_ready"))
        folded, sq_fold = sem("folded"), sem("sq_fold")
        xa_ready, xa_hi, xa_lo = sem("xa_ready"), sem("xa_hi"), sem("xa_lo")
        g_ready = sem("g_ready")
        t_ready, sqt_ready, ya_ready, ya_hi, ya_lo = (
            sem(n) for n in ("t_ready", "sqt_ready", "ya_ready", "ya_hi", "ya_lo"))
        qk_ss, qk_scaled, v_ready = sem("qk_ss"), sem("qk_scaled"), sem("v_ready")
        gate_t = sem("gate_t")
        aT, aTe, aS, aM, aE, aN, aPT, aPTe, aPV, aH, aL = (sem(n) for n in (
            "att_T", "att_T_out", "att_S", "att_max", "att_exp", "att_norm", "att_PT", "att_PT_out",
            "att_PV", "yb_hi", "yb_lo"))
        merged, m_hi, m_lo, m_lo_pool = sem("merged"), sem("m_hi"), sem("m_lo"), sem("m_lo_pool")
        rope_q, cq_ss, cq_r, cq_s, cq_T, cq_hi, cq_lo = (sem(n) for n in (
            "rope_q", "cq_ss", "cq_r", "cq_scaled", "cq_T", "cq_hi", "cq_lo"))
        qb_ready, kv_ready, mla_ready, rope_k = sem("qb_ready"), sem("kv_ready"), sem("mla_ready"), sem("rope_k")
        sink_T, sink_ready = sem("sink_T"), sem("sink_ready")
        f_conv, f_glu, f_act, f_hi, f_lo = (sem(n) for n in ("f_conv", "f_glu", "f_act", "f_hi", "f_lo"))
        down_bank, fin_T, fin_Te, fin_root, y_ready = (
            sem(n) for n in ("down_bank", "fin_T", "fin_T_out", "fin_root", "y_ready"))
        block = ctx.enter_context(nc.Block())

        U2_FREE = [emptied(GROUP_OF[(s, 0)])[1] for s in range(S2_SEQ, S2_GA)]

        POOL_MERGES = 2
        CQ_ROUND = ((0, 1), (2, 3), (4,))

        def used_value(s):
            base = FFN2 if s >= FFN2 else FFN1
            if base <= s < base + 3 * STEPS:
                i = s - base
                n0 = 0 if base == FFN1 else STEPS
                if i < 2:
                    return group_done, GROUP_OF[(base, 0)] + i + 1
                j, kind = divmod(i - 2, 3)
                if i == 3 * STEPS - 1 or kind == 2:
                    if i == 3 * STEPS - 1:
                        return down_bank, 4 if n0 == 0 else 6
                    return down_used, n0 // STEPS * (STEPS - 1) + j + 1
                return group_done, GROUP_OF[(base, 0)] + 2 * (j + 1) + kind + 1
            return group_done, max(g for (x, _), g in GROUP_OF.items() if x == s) + 1

        def x_value(n, c):
            if n == 0:
                return in_x[c // 4], 16
            if n == 2:
                return x_ready, c // 2 + 1
            return bank_free["dve"], emptied(GROUP_OF[((S_OUT if n == 1 else S2_OUT) + c // 2, 0)])[1]

        def raw_value(s):
            return 32 * (s // RING + 1)

        @block.sync
        def _(sp_eng):
            e = sp_eng

            def halves(slot, src_of, view):
                for a in range(2):
                    e.dma_start(view[64 * a:64 * a + 64], src_of(a)).then_inc(raw_in[slot], 16)

            def load(s):
                name, kind, arg = PLAN[s]
                slot = s % RING
                if s >= RING:
                    e.wait_ge(lo_ready, s - RING + 1)
                r = raw[slot]
                if kind == "blocks":
                    for i, w in enumerate(("w_r", "w_i")):
                        e.dma_start(r[:, 1024 * i:1024 * i + 1024].rearrange("p (n d) -> p n d", n=8),
                                    t[w][0].rearrange("n c d -> c n d")).then_inc(raw_in[slot], 16)
                    return
                w = t[name][0]
                if kind == "cols":
                    width = min(WIDE, w.shape[1] - arg)
                    view = r[:, :].rearrange("p (k n) -> p k n", k=KD)[:, :, 0:width]
                    src = w.rearrange("(k a p) n -> a p k n", a=2, p=64)
                    halves(slot, lambda a: src[a][:, :, arg:arg + width], view)
                elif kind == "swa":
                    view = r[:, :].rearrange("p (k n) -> p k n", k=4)
                    src = w.rearrange("(a k p) n -> a p k n", a=2, p=64)
                    halves(slot, lambda a: src[a][:, :, arg:arg + 512], view)
                else:
                    k, width = {"rows4": (4, 512), "rows3": (3, QLAT), "rows2": (2, 1024)}[kind]
                    view = r[:, 0:k * width].rearrange("p (k n) -> p k n", k=k)
                    src = w.rearrange("(k a p) n -> a p k n", a=2, p=64)
                    halves(slot, lambda a: src[a][:, :, arg:arg + width], view)

            def load_cols(s, slot, name, j, free=True):
                if free:
                    e.wait_ge(lo_ready, s - RING + 1)
                src = t[name][0].rearrange("(k a p) n -> a p k n", a=2, p=64)
                view = raw[slot][:, :].rearrange("p (k n) -> p k n", k=KD)
                halves(slot, lambda a: src[a][:, :, bass.ts(j, WIDE)], view)

            def load_down(s, slot, name, j):
                e.wait_ge(lo_ready, s - RING + 1)
                src = t[name][0].rearrange("(j k a p) n -> a p j k n", k=2, a=2, p=64)
                view = raw[slot][:, :].rearrange("p (k n) -> p k n", k=2)
                halves(slot, lambda a: src[a][:, j], view)

            def ffn(base, up, gate, down):
                load_cols(base, base % RING, up, 0)
                load_cols(base + 1, (base + 1) % RING, gate, 0)
                with e.Fori(1, STEPS) as j:
                    s = j * 3 + (base - 1)
                    load_cols(s, (base + 2) % RING, up, j)
                    load_cols(s + 1, base % RING, gate, j)
                    load_down(s + 2, (base + 1) % RING, down, j - 1)
                load_down(base + 3 * STEPS - 1, (base + 3 * STEPS - 1) % RING, down, STEPS - 1)

            load(0)
            for i in range(2):
                e.dma_start(X[:, 4 * i:4 * i + 4, :], t["xT"][:, 4 * i:4 * i + 4, :]).then_inc(in_x[i], 16)
            load(1)
            load(2)
            e.dma_start(ident[:, :], t["ident"]).then_inc(in_misc, 16)
            e.dma_start(masks[:, :, :], t["masks"]).then_inc(in_misc, 16)
            for c in range(2):
                e.dma_start(ropeA[:, c], t["rope_a"][c].rearrange("(h p) d -> p h d", p=P)).then_inc(in_misc, 16)
                e.dma_start(ropeB[:, c], t["rope_b"][c].rearrange("(h p) d -> p h d", p=P)).then_inc(in_misc, 16)
            e.dma_start(rowt[:, :], t["swa_sinks_2"]).then_inc(in_misc, 16)
            for s in range(RING, FFN1):
                load(s)
            ffn(FFN1, "w_up", "w_gate", "w_down")
            for s in range(S2_SEQ, FFN2):
                load(s)
            e.wait_ge(aPV, 24)
            e.dma_start(frow_g, t["final_norm_g"].rearrange("(a n) -> a n", a=1)).then_inc(in_fing, 16)
            ffn(FFN2, "w_up_2", "w_gate_2", "w_down_2")
            for i in range(2 * HALVES):
                h, cols = i // 2, slice(512 * (i % 2), 512 * (i % 2) + 512)
                e.wait_ge(y_ready, i + 1)
                e.dma_start(t["out"][0][P * h:P * h + P, cols], outp[:, h, cols]).then_inc(out_done, 16)
            e.wait_ge(out_done, 16 * 2 * HALVES)

        @block.scalar
        def _(e):
            count = [0]

            def link(ins):
                count[0] += 1
                ins.then_inc(act_step, 1)
                e.wait_ge(act_step, count[0])

            def hi(slot, raw_v, used):
                e.wait_ge(raw_in[slot], raw_v)
                if used:
                    e.wait_ge(*used)
                e.activation(whi[slot][:, :], raw[slot][:, :], ACT.Copy).then_inc(hi_ready, 1)

            def pre(s):
                if s < SLABS:
                    hi(s % RING, raw_value(s), used_value(s - RING) if s >= RING else None)

            def free_bank(ins):
                ins.then_inc(bank_free["act"], 1)

            def norm_hi(n, gains, h_dst, chunks):
                for c in chunks:
                    e.wait_ge(*x_value(n, c))
                    e.activation(h_dst[:, c, :], X[:, c, :], ACT.Copy, scale=gains[:, c:c + 1]).then_inc(h_hi, 1)

            def squares(n, i):
                e.activation(SQ[:, 2 * i:2 * i + 2, :], X[:, 2 * i:2 * i + 2, :], ACT.Square).then_inc(sq_ready, 1)

            def roots(n, seq):
                e.wait_ge(ssum, n + 1)
                if seq:
                    e.activation(root2[:, :], PSB[:, 0:2], ACT.Sqrt, bias=epst[:, :], scale=1.0 / D).then_inc(rms_root2, 1)
                e.activation(root[:, :], PSA[:, 0:SEQ], ACT.Sqrt, bias=epst[:, :], scale=1.0 / D).then_inc(rms_root, 1)

            def att(step):
                kind_base = 0 if step < 100 else 100
                u = unit_of(step)
                if u is not None and not (8 <= u < 16 and u % 2):
                    n_t = t_count(u)
                    b = tbuf(u)
                    e.wait_ge(aT, n_t)
                    if n_t > 2:
                        e.wait_ge(aS, last_reader_of_tbuf(u))
                    d = MLA_D if u >= 16 else P
                    if u < 8:
                        e.activation(qT[:, b, :], PST[:, 0:SEQ], ACT.Copy)
                        e.activation(kT[:, b, :], PST[:, SEQ:2 * SEQ], ACT.Copy, scale=qkg[:, :]).then_inc(aTe, 1)
                    else:
                        e.activation(qkT[0:d, b, :, :], PST[0:d, :].rearrange("p (i n) -> p i n", i=2),
                                     ACT.Copy).then_inc(aTe, 1)
                u = unit_of(step - LAG_PT) if step - LAG_PT >= kind_base else None
                if u is not None:
                    e.wait_ge(aPT, u + 1)
                    if u >= 2:
                        e.wait_ge(aPV, u - 1)
                    e.activation(pT[:, u % 2, :], PSPT[u % 2][:, 0:3 * P], ACT.Copy).then_inc(aPTe, 1)
                u = unit_of(step - LAG_PV) if step - LAG_PV >= kind_base else None
                if u is not None:
                    e.wait_ge(aPV, u + 1)
                    rows, chunk = yb_place(u)
                    e.activation(pairs[2][0][rows, chunk, :], PSPV[rows, 0:SEQ], ACT.Copy).then_inc(aH, 1)
                u = unit_of(step - LAG_E) if step - LAG_E >= kind_base else None
                if u is not None:
                    e.wait_ge(aM, u + 1)
                    if u >= 3:
                        e.wait_ge(aPT, u - 2)
                    for h in range(HALVES):
                        cols = slice(0, P) if h == 0 else slice(P, 3 * P)
                        if u < 8:
                            scale = cq[:, 0, h, u:u + 1]
                        else:
                            scale = (64 ** -0.5) if u < 16 else MLA_D ** -0.5
                        ins = e.activation(pr[:, u % 3, cols], sm[:, u % 2, cols], ACT.Exp,
                                           bias=nb[:, u % 3, h:h + 1], scale=scale,
                                           accum_out=sums[:, u % 3, h:h + 1])
                    if 8 <= u < 16:
                        hd = swa_head(u)
                        ins = e.activation(esink[:, u % 3, :], nb[:, u % 3, :], ACT.Exp,
                                           bias=sinks[:, 0, hd:hd + 1])
                    ins.then_inc(aE, 1)

            e.dma_start(par[:, :], t["params"]).then_inc(in_par, 16)
            e.wait_ge(raw_in[0], raw_value(0))
            e.activation(whi[0][:, 0:SLAB // 2], raw[0][:, 0:SLAB // 2], ACT.Copy).then_inc(first_hi, 1)
            e.activation(whi[0][:, SLAB // 2:], raw[0][:, SLAB // 2:], ACT.Copy).then_inc(hi_ready, 1)
            e.wait_ge(in_par, 16)
            norm_hi(0, pcol[:, G1:G1 + KD], pairs[0][0], range(KD))
            for i in range(4):
                squares(0, i)
            pre(1)
            e.wait_ge(sp_in, 1)
            e.activation(sp[:, 1, :], sp[:, 0, :], ACT.Exp, scale=-1.0).then_inc(sp_exp, 1)
            pre(2)

            def xa_parts(s):
                e.wait_ge(xa_ready, s + 1)
                e.activation(pairs[1][0][:, 2 * s:2 * s + 2, :], xa[:, 2 * s:2 * s + 2, :], ACT.Copy).then_inc(xa_hi, 1)

            for s in range(S_XR, S_G):
                if s == S_XR:
                    roots(0, True)
                pre(s + 3)
                e.wait_ge(bank_free["dve"], s + 1)
                for m in range(2):
                    c = 2 * s + m
                    ins = e.activation(xa[:, c, :], xrp[:, s % 2, m, 0:SEQ], ACT.Identity,
                                       scale=pcol[:, CONVW + c:CONVW + c + 1], bias=pcol[:, CONVB + c:CONVB + c + 1])
                ins.then_inc(tap0, 1)
                if s:
                    xa_parts(s - 1)
            for s in range(S_G, S_RI):
                if s < S_RI - 1:
                    pre(s + 3)
                i = s - S_G
                if i == 0:
                    xa_parts(S_G - 1)
                e.wait_ge(bank_free["dve"], s + 1)
                e.activation(gg[:, 2 * i:2 * i + 2, :], gg[:, 2 * i:2 * i + 2, :], ACT.Gelu_apprx_tanh).then_inc(g_ready, 1)
            for i in range(8):
                g = GROUP_OF[(S_RI, i)]
                e.wait_ge(group_done, g + 1)
                for m in range(2):
                    blk = 2 * (i % 4) + m
                    dst = (T0 if i < 4 else T1)[:, blk, :]
                    ins = e.activation(dst, ps[g % 2][:, SEQ * m:SEQ * m + SEQ], ACT.Tanh, scale=0.5,
                                       bias=halfb[:, 8 * (i // 4) + blk:8 * (i // 4) + blk + 1])
                free_bank(ins)
            e.wait_ge(bank_free["act"], 8)
            e.wait_ge(sp_ready, 1)
            pre(S_RI + 2)
            pre(S_RI + 3)

            def decays(chunks):
                for m in chunks:
                    e.activation(decay[:, m, :], T0[:, m, :], ACT.Exp, scale=sp[:, 2, m:m + 1], bias=sp[:, 2, m:m + 1])
                    e.activation(T0[:, m, :], T0[:, m, :], ACT.Tanh, scale=sp[:, 7, m:m + 1],
                                 bias=sp[:, 7, m:m + 1]).then_inc(t_ready, 1)

            def evac_qkv(s, dst, i):
                g = GROUP_OF[(s, 0)]
                e.wait_ge(group_done, g + 1)
                for h in range(HALVES):
                    ins = e.activation(dst[:, h, WIDE * i:WIDE * i + WIDE], ps[g % 2][:, 256 * h:256 * h + 256],
                                       ACT.Copy, scale=rstd_sq[:, h:h + 1])
                free_bank(ins)
                e.wait_ge(bank_free["act"], emptied(g)[1])

            def rnn_chunk(m):
                if m >= 2:
                    e.wait_ge(ya_ready, m - 1)
                e.activation(rnn_sq[:, m % 2, :], T0[:, m, :], ACT.Sqrt).then_inc(sqt_ready, 1)

            decays(range(2))
            e.wait_ge(rstd2_ready, 1)
            for s in range(S_Q, S_V):
                pre(s + 3)
                which, i = divmod(s - S_Q, 4)
                dst = (q_s, k_s)[which]
                evac_qkv(s, dst, i)
                for h in range(HALVES):
                    for hd in (2 * i, 2 * i + 1):
                        e.activation(junk[:, 0:P], dst[:, h, P * hd:P * hd + P], ACT.Square,
                                     accum_out=ssqk[:, which, h, hd:hd + 1]).then_inc(act_step, 1)
                        count[0] += 1
                        e.wait_ge(act_step, count[0])
                if s < S_RNN:
                    decays(range(2 + 2 * i, 4 + 2 * i))
                else:
                    e.wait_ge(t_ready, KD)
                    rnn_chunk(s - S_RNN)
            e.activation(rqk[:, :, :, :], ssqk[:, :, :, :], ACT.Sqrt, bias=epst[:, :], scale=1.0 / P).then_inc(qk_ss, 1)
            for s in range(S_V, S_GATE):
                pre(s + 3)
                e.wait_ge(ya_ready, 4 + s - S_V + 1)
                evac_qkv(s, v_s, s - S_V)
                if s - S_RNN < KD:
                    rnn_chunk(s - S_RNN)
            e.wait_ge(bank_free["act"], emptied(GROUP_OF[(S_GATE - 1, 0)])[1])

            def gate_tile(i):
                return (T0 if i < 4 else T1)[:, 2 * (i % 4):2 * (i % 4) + 2, :]

            def merge_parts(first, n0):
                def run(i):
                    e.wait_ge(merged, n0 + i + 1)
                    e.activation(pairs[0][0][:, 2 * i:2 * i + 2, :], T0[:, 2 * i:2 * i + 2, :],
                                 ACT.Copy).then_inc(m_hi, 1)
                return run

            e.wait_ge(ya_lo, KD)
            mp = merge_parts(S_PA, 0)
            for s in range(S_GATE, FFN1):
                for step in steps_at(s):
                    att(step)
                if early_att(s):
                    pre(s + 2)
                last = s in (S_OUT - 1, FFN1 - 1)
                if not last and not early_att(s + 1):
                    pre(s + 3)
                if S_PA <= s < S_OUT:
                    mp(s - S_PA)
                if s >= S_OUT:
                    i = s - S_OUT
                    norm_hi(1, pcol[:, G2:G2 + KD], pairs[2][0], (2 * i, 2 * i + 1))
                    squares(1, i)
                if last:
                    pre(s + 3)
                if s < S_PR:
                    i = s - S_GATE
                    e.wait_ge(bank_free["dve"], emptied(GROUP_OF[(s, 0)])[1])
                    e.activation(gate_tile(i), gate_tile(i), ACT.Tanh, scale=0.5).then_inc(gate_t, 1)

            def ffn(which, base, n0, func):
                g_up = GROUP_OF[(base, 0)]
                free0 = emptied(g_up)[1]

                def post(j, pre_a, pre_b, pre_c, last=False):
                    pre_a()
                    if not last:
                        pre_b()
                    if which == 1:
                        e.wait_ge(f_conv, j + 1)
                    else:
                        e.wait_ge(bank_free["dve"], j * 2 + (free0 + 1))
                    buf = cv if which == 1 else gt
                    e.activation(buf, buf, func).then_inc(f_glu, 1)
                    if not last:
                        pre_c()
                    e.wait_ge(f_act, j + (n0 + 1))
                    if not last and not (isinstance(j, int) and j == 0):
                        e.wait_ge(down_used, j + n0 // STEPS * (STEPS - 1))
                    e.activation(act_parts[last][0], actf, ACT.Copy).then_inc(f_hi, 1)
                    if last:
                        pre_b()
                        pre_c()

                roots(which * 2 - 1, False)
                post(0, lambda: pre(base + 3), lambda: pre(base + 4), lambda: None)

                def hi_at(j, off):
                    used = (down_used, j + n0 // STEPS * (STEPS - 1)) if off == 4 else (group_done, j * 2 + (g_up + off - 1))
                    hi((base + off) % RING, j * 32 + 32 * ((base + off) // RING + 1), used)

                with e.Fori(1, STEPS - 1) as j:
                    post(j, lambda: hi_at(j, 2), lambda: hi_at(j, 3), lambda: hi_at(j, 4))
                last = base + 3 * (STEPS - 1) - 1
                post(STEPS - 1, lambda: pre(last + 3), lambda: pre(last + 4), lambda: pre(last + 5), True)

            ffn(1, FFN1, 0, ACT.Gelu_apprx_tanh)

            norm_hi(2, pcol[:, MIXG:MIXG + KD], pairs[0][0], range(KD))
            for i in range(4):
                squares(2, i)
            pre(S2_SEQ + 2)
            for s in range(S2_SEQ, S2_GA):
                pre(s + 3)
                if s == S2_SEQ:
                    roots(2, True)
                    e.wait_ge(rstd2_ready, 2)
                g = GROUP_OF[(s, 0)]
                i = s - S2_SEQ
                width = min(WIDE, SEQ_COLS - WIDE * i)
                e.wait_ge(group_done, g + 1)
                for h in range(HALVES):
                    ins = e.activation(u2[:, h, WIDE * i:WIDE * i + width], ps[g % 2][:, 256 * h:256 * h + width],
                                       ACT.Copy, scale=rstd_sq[:, h:h + 1])
                free_bank(ins)
            e.wait_ge(bank_free["act"], U2_FREE[5])
            for h in range(HALVES):
                link(e.activation(junk[:, 0:QLAT], u2[:, h, OFF_QL:OFF_QL + QLAT], ACT.Square,
                                  accum_out=ss2[:, 0, h:h + 1]))
                link(e.activation(junk[:, 0:KVLAT], u2[:, h, OFF_KVL:OFF_KVL + KVLAT], ACT.Square,
                                  accum_out=ss2[:, 1, h:h + 1]))
            e.activation(r2[:, 0, :], ss2[:, 0, :], ACT.Sqrt, bias=epst[:, :], scale=1.0 / QLAT)
            e.activation(r2[:, 1, :], ss2[:, 1, :], ACT.Sqrt, bias=epst[:, :], scale=1.0 / KVLAT).then_inc(cq_ss, 1)
            e.wait_ge(cq_r, 1)
            for h in range(HALVES):
                e.activation(u2[:, h, OFF_QL:OFF_QL + QLAT], u2[:, h, OFF_QL:OFF_QL + QLAT], ACT.Copy,
                             scale=ss2[:, 0, h:h + 1])
                ins = e.activation(u2[:, h, OFF_KVL:OFF_KVL + KVLAT], u2[:, h, OFF_KVL:OFF_KVL + KVLAT], ACT.Copy,
                                   scale=ss2[:, 1, h:h + 1])
            ins.then_inc(cq_s, 1)
            mp2 = merge_parts(S2_OMLA, 4)

            def cq_parts(r):
                e.wait_ge(cq_T, r + 1)
                for c in CQ_ROUND[r]:
                    e.activation(pairs[1][0][:, c, :], (PSA, PSPT[0], PSA)[r][:, SEQ * (c % 2):SEQ * (c % 2) + SEQ],
                                 ACT.Copy, scale=pcol[:, QLG + c:QLG + c + 1]).then_inc(cq_hi, 1)

            for s in range(S2_GA, FFN2):
                steps = steps_at(s)
                for step in steps[:1]:
                    att(step)
                if early_att(s) and not late_cut(s):
                    pre(s + 2)
                for step in steps[1:]:
                    att(step)
                if s == S2_GA + 1:
                    cq_parts(0)
                    cq_parts(1)
                if s == S2_GA + 2:
                    cq_parts(2)
                if S2_UQ <= s < S2_UKV:
                    for h in range(HALVES):
                        g = GROUP_OF[(s, h)]
                        e.wait_ge(group_done, g + 1)
                        i = s - S2_UQ
                        free_bank(e.activation(qbf[:, h, QLAT * i:QLAT * i + QLAT], ps[g % 2][:, 0:QLAT], ACT.Copy))
                if s == S2_UKV:
                    for i in (1, 3):
                        g = GROUP_OF[(s, i)]
                        e.wait_ge(group_done, g + 1)
                        for dst, src in kv_parts(ps[g % 2], i // 2, 1):
                            ins = e.activation(dst, src, ACT.Copy)
                        free_bank(ins)
                if S2_UQ <= s <= S2_UKV:
                    pre(s + 2)
                last = s in (S2_OUT - 1, FFN2 - 1)
                if S2_OUT <= s < FFN2 - 1:
                    pre(s + 3)
                if S2_OMLA <= s < S2_OUT:
                    for i in range(2):
                        mp2(2 * (s - S2_OMLA) + i)
                if s >= S2_OUT:
                    i = s - S2_OUT
                    norm_hi(3, pcol[:, FFNG:FFNG + KD], pairs[2][0], (2 * i, 2 * i + 1))
                    squares(3, i)
                if last:
                    pre(s + 3)
                if gate_of(s) is not None:
                    i = gate_of(s)
                    e.wait_ge(bank_free["dve"], emptied(GROUP_OF[(s, 0)])[1])
                    e.activation(gate_tile(i), gate_tile(i), ACT.Tanh, scale=0.5).then_inc(gate_t, 1)
            ffn(2, FFN2, STEPS, ACT.Silu)
            for h in range(HALVES):
                e.wait_ge(down_bank, 4 + h + 1)
                for c in range(2):
                    ins = e.activation(VV[:, 0:512], ps[2 + 2 * h + c][:, :], ACT.Square,
                                       accum_out=fin[:, 2 * h + c:2 * h + c + 1])
                    link(ins)
                link(e.activation(fin2[:, h:h + 1], fin[:, 2 * h:2 * h + 1], ACT.Identity,
                                  bias=fin[:, 2 * h + 1:2 * h + 2]))
                e.activation(fin2[:, 2 + h:3 + h], fin2[:, h:h + 1], ACT.Sqrt, bias=epst[:, :],
                             scale=1.0 / D).then_inc(fin_root, 1)

        @block.vector
        def _(e):
            count = [0]

            def link(ins):
                count[0] += 1
                ins.then_inc(dve_step, 1)
                e.wait_ge(dve_step, count[0])

            def lo(s, slot):
                e.wait_ge(hi_ready, s + 1)
                e.tensor_tensor(wlo[slot][:, :], raw[slot][:, :], whi[slot][:, :].bitcast(f32),
                                ALU.subtract).then_inc(lo_ready, 1)

            def pre(s):
                if s < SLABS:
                    lo(s, s % RING)

            def bc2(ap, n):
                return ap.unsqueeze(1).to_broadcast([P, n, SEQ])

            def norm_lo(n, gains, lo_dst, hi_src, chunks):
                for c in chunks:
                    e.wait_ge(*x_value(n, c))
                    e.wait_ge(h_hi, KD * n + c + 1)
                    e.scalar_tensor_tensor(lo_dst[:, c, :], X[:, c, :], gains[:, c:c + 1],
                                           hi_src[:, c, :].bitcast(f32), ALU.mult, ALU.subtract).then_inc(h_lo, 1)

            def inv(n, seq):
                if seq:
                    e.wait_ge(rms_root2, n // 2 + 1)
                    e.reciprocal(rstd_sq[:, :], root2[:, :]).then_inc(rstd2_ready, 1)
                e.wait_ge(rms_root, n + 1)
                e.reciprocal(rstd_bc[:, :], root[:, :]).then_inc(rstd_ready, 1)
                e.wait_ge(rstd_ready, n + 1)

            def normed(g, dst):
                e.wait_ge(group_done, g + 1)
                e.tensor_tensor(dst, ps[g % 2][:, :].rearrange("p (m n) -> p m n", m=2), bc2(rstd_bc[:, :], 2),
                                ALU.mult).then_inc(bank_free["dve"], 1)

            def att(step):
                kind_base = 0 if step < 100 else 100
                u, un, ul = (unit_of(step - lag) if step - lag >= kind_base else None
                             for lag in (LAG_S, LAG_N, LAG_PV))
                if un is not None:
                    e.wait_ge(aE, un + 1)
                    if 8 <= un < 16:
                        link(e.tensor_tensor(sums[:, un % 3, :], sums[:, un % 3, :], esink[:, un % 3, :], ALU.add))
                    link(e.reciprocal(rinv[:, un % 2, :], sums[:, un % 3, :]))
                    e.tensor_scalar(pr[:, un % 3, 0:P], pr[:, un % 3, 0:P], rinv[:, un % 2, 0:1], None, ALU.mult)
                    e.tensor_scalar(pr[:, un % 3, P:3 * P], pr[:, un % 3, P:3 * P], rinv[:, un % 2, 1:2], None,
                                    ALU.mult).then_inc(aN, 1)
                if u is not None:
                    e.wait_ge(aS, u + 1)
                    if u >= 2:
                        e.wait_ge(aE, u - 1)
                    link(e.tensor_tensor(sm[:, u % 2, :], PSS[u % 2][:, 0:3 * P],
                                         masks[:, 1 if 8 <= u < 16 else 0, :], ALU.add))
                    e.reduce_max(mx[:, u % 2, 0:1], sm[:, u % 2, 0:P], AX)
                    link(e.reduce_max(mx[:, u % 2, 1:2], sm[:, u % 2, P:3 * P], AX))
                    if u < 8:
                        e.tensor_tensor(nb[:, u % 3, :], mx[:, u % 2, :], cq[:, 1, :, u], ALU.mult).then_inc(aM, 1)
                    elif u < 16:
                        hd = swa_head(u)
                        e.tensor_scalar(nb[:, u % 3, :], mx[:, u % 2, :], -(64 ** -0.5), sinks[:, 1, hd:hd + 1],
                                        ALU.mult, ALU.min).then_inc(aM, 1)
                    else:
                        e.tensor_scalar(nb[:, u % 3, :], mx[:, u % 2, :], -(MLA_D ** -0.5), None,
                                        ALU.mult).then_inc(aM, 1)
                if ul is not None:
                    e.wait_ge(aH, ul + 1)
                    rows, chunk = yb_place(ul)
                    e.tensor_tensor(pairs[2][1][rows, chunk, :], PSPV[rows, 0:SEQ],
                                    pairs[2][0][rows, chunk, :].bitcast(f32), ALU.subtract).then_inc(aL, 1)

            e.memset(epst[:, :], EPS)
            for b in range(2):
                e.memset(xrp[:, b, :, 0:KW - 1], 0.0)
            e.memset(ones[:, :], 1.0).then_inc(consts, 1)
            e.wait_ge(in_par, 16)
            for half, cut, done in ((0, first_hi, first_lo), (1, hi_ready, lo_ready)):
                cols = slice(SLAB // 2 * half, SLAB // 2 * (half + 1))
                e.wait_ge(cut, 1)
                e.tensor_tensor(wlo[0][:, cols], raw[0][:, cols], whi[0][:, cols].bitcast(f32),
                                ALU.subtract).then_inc(done, 1)
                norm_lo(0, pcol[:, G1:G1 + KD], pairs[0][1], pairs[0][0], range(4 * half, 4 * half + 4))
            e.tensor_scalar(halfb[:, :], pcol[:, BR:BR + 16], 0.5, None, ALU.mult)
            e.tensor_tensor(qkg[:, :], pcol[:, QG:QG + 1], pcol[:, KG:KG + 1], ALU.mult)
            link(e.tensor_scalar(sp[:, 2, :], pcol[:, LAM:LAM + KD], -1.0, None, ALU.mult))
            link(e.tensor_tensor(sp[:, 0, :], sp[:, 2, :], pcol[:, LAM:LAM + KD], ALU.max))
            e.tensor_scalar(sp[:, 3, :], sp[:, 2, :], 0.0, None, ALU.max).then_inc(sp_in, 1)
            pre(1)
            pre(2)
            inv(0, True)

            def taps(s):
                e.wait_ge(tap0, s + 1)
                for k in range(1, KW):
                    for m in range(2):
                        c = 2 * s + m
                        w = CONVW + KD * k + c
                        if k > 1:
                            e.wait_ge(dve_step, count[0] - 1)
                        ins = e.scalar_tensor_tensor(xa[:, c, :], xrp[:, s % 2, m, k:k + SEQ], pcol[:, w:w + 1],
                                                     xa[:, c, :], ALU.mult, ALU.add)
                        if (k, m) != (KW - 1, 1):
                            count[0] += 1
                            ins.then_inc(dve_step, 1)
                ins.then_inc(xa_ready, 1)

            for s in range(S_XR, S_G):
                if s >= 2:
                    e.wait_ge(xa_ready, s - 1)
                normed(GROUP_OF[(s, 0)], xrp[:, s % 2, :, KW - 1:])
                if s:
                    taps(s - 1)
                pre(s + 3)
            for s in range(S_G, S_RI):
                i = s - S_G
                normed(GROUP_OF[(s, 0)], gg[:, 2 * i:2 * i + 2, :])
                if i == 0:
                    taps(S_G - 1)
                if s < S_RI - 1:
                    pre(s + 3)
            e.wait_ge(sp_exp, 1)
            link(e.tensor_scalar(sp[:, 4, :], sp[:, 1, :], 2.0, None, ALU.add))
            link(e.reciprocal(sp[:, 5, :], sp[:, 4, :]))
            link(e.tensor_tensor(sp[:, 4, :], sp[:, 1, :], sp[:, 5, :], ALU.mult))
            link(e.tensor_tensor(sp[:, 5, :], sp[:, 4, :], sp[:, 4, :], ALU.mult))
            link(e.tensor_scalar(sp[:, 6, :], sp[:, 5, :], 1.0 / 17, 1.0 / 15, ALU.mult, ALU.add))
            for odd in (13, 11, 9, 7, 5, 3, 1):
                link(e.tensor_tensor(sp[:, 6, :], sp[:, 6, :], sp[:, 5, :], ALU.mult))
                link(e.tensor_scalar(sp[:, 6, :], sp[:, 6, :], 1.0 / odd, None, ALU.add))
            link(e.tensor_tensor(sp[:, 6, :], sp[:, 6, :], sp[:, 4, :], ALU.mult))
            link(e.scalar_tensor_tensor(sp[:, 6, :], sp[:, 6, :], 2.0, sp[:, 3, :], ALU.mult, ALU.add))
            e.tensor_scalar(sp[:, 2, :], sp[:, 6, :], -4.0, None, ALU.mult)
            e.tensor_scalar(sp[:, 7, :], sp[:, 6, :], 2.0, None, ALU.mult).then_inc(sp_ready, 1)
            pre(S_RI + 2)
            pre(S_RI + 3)

            def rnn_chunk(m):
                e.wait_ge(t_ready, m + 1)
                e.wait_ge(sqt_ready, m + 1)
                if m == 0:
                    e.wait_ge(g_ready, 4)
                if m >= 2:
                    e.wait_ge(ya_lo, m - 1)
                h, root_a, ya = rnn_t[:, 0, :], rnn_t[:, 1, :], rnn_t[:, 2 + m % 2, :]
                a, z = decay[:, m, :], T1[:, m, :]
                e.scalar_tensor_tensor(z, z, 1.0, xa[:, m, :], ALU.add, ALU.mult)
                link(e.scalar_tensor_tensor(root_a, a, 1.0, rnn_sq[:, m % 2, :], ALU.add, ALU.mult))
                link(e.tensor_tensor(z, z, root_a, ALU.mult))
                link(e.tensor_tensor_scan(h, a, z, 0.0, ALU.mult, ALU.add))
                e.scalar_tensor_tensor(ya, h, 0.5, gg[:, m, :], ALU.mult, ALU.mult).then_inc(ya_ready, 1)

            for s in range(S_Q, S_GATE):
                pre(s + 3)
                if 0 <= s - S_RNN < KD:
                    rnn_chunk(s - S_RNN)
                if s == S_V:
                    e.wait_ge(qk_ss, 1)
                    link(e.reciprocal(ssqk[:, :, :, :], rqk[:, :, :, :]))
                    e.tensor_scalar(cq[:, 0], ssqk[:, 0], P ** -0.5, None, ALU.mult)
                    e.tensor_scalar(cq[:, 1], ssqk[:, 0], -(P ** -0.5), None, ALU.mult)
                    for h in range(HALVES):
                        kk = k_s[:, h, :].rearrange("p (n d) -> p n d", n=HEADS)
                        ins = e.tensor_tensor(kk, kk, ssqk[:, 1, h, :].unsqueeze(2).to_broadcast([P, HEADS, P]),
                                              ALU.mult)
                    ins.then_inc(qk_scaled, 1)

            def gate_tile(i):
                return (T0 if i < 4 else T1)[:, 2 * (i % 4):2 * (i % 4) + 2, :]

            def gate(s, i):
                normed(GROUP_OF[(s, 0)], gate_tile(i))

            def branch(g, tiles, dst):
                e.wait_ge(group_done, g + 1)
                e.scalar_tensor_tensor(dst[:, tiles, :], dst[:, tiles, :], 1.0,
                                       ps[g % 2][:, :].rearrange("p (m n) -> p m n", m=2),
                                       ALU.add, ALU.mult).then_inc(bank_free["dve"], 1)
                e.wait_ge(bank_free["dve"], emptied(g)[1])

            def nothing():
                pass

            def merge(i, n0, cut):
                tiles = slice(2 * i, 2 * i + 2)
                e.tensor_tensor(T0[:, tiles, :], T0[:, tiles, :], T1[:, tiles, :], ALU.add).then_inc(merged, 1)
                cut()
                if i >= POOL_MERGES:
                    e.wait_ge(m_hi, n0 + i + 1)
                    e.tensor_tensor(pairs[0][1][:, tiles, :], T0[:, tiles, :], pairs[0][0][:, tiles, :].bitcast(f32),
                                    ALU.subtract).then_inc(m_lo, 1)

            def residual(s, i):
                g = GROUP_OF[(s, 0)]
                e.wait_ge(group_done, g + 1)
                e.scalar_tensor_tensor(X[:, 2 * i:2 * i + 2, :], ps[g % 2][:, :].rearrange("p (m n) -> p m n", m=2),
                                       0.5, X[:, 2 * i:2 * i + 2, :], ALU.mult, ALU.add).then_inc(bank_free["dve"], 1)

            e.wait_ge(sink_T, 1)
            link(e.tensor_copy(sinks[:, 0, :], PSB[:, 8:8 + HEADS]))
            e.tensor_scalar(sinks[:, 1, :], sinks[:, 0, :], -1.0, None, ALU.mult).then_inc(sink_ready, 1)
            for s in range(S_GATE, FFN1):
                for step in steps_at(s):
                    att(step)
                if early_att(s):
                    pre(s + 2)
                last = s in (S_OUT - 1, FFN1 - 1)
                cut = nothing if last or early_att(s + 1) else lambda: pre(s + 3)
                if s < S_PR:
                    gate(s, s - S_GATE)
                if S_PR <= s < S_PA:
                    i = s - S_PR
                    e.wait_ge(gate_t, 4)
                    branch(GROUP_OF[(s, 0)], slice(2 * i, 2 * i + 2), T0)
                if S_PA <= s < S_OUT:
                    i = s - S_PA
                    e.wait_ge(gate_t, 8)
                    branch(GROUP_OF[(s, 0)], slice(2 * i, 2 * i + 2), T1)
                    merge(i, 0, cut)
                if S_OUT <= s < FFN1:
                    i = s - S_OUT
                    residual(s, i)
                    cut()
                    norm_lo(1, pcol[:, G2:G2 + KD], pairs[2][1], pairs[2][0], (2 * i, 2 * i + 1))
                if s < S_PA:
                    cut()
                if last:
                    pre(s + 3)

            def ffn(which, base, n0, n):
                g_up = GROUP_OF[(base, 0)]
                free0 = emptied(g_up)[1]
                if which == 1:
                    e.memset(upn[:, :, 0:FKW - 1], 0.0)
                chain = dve_loop[which - 1]
                LINKS = 5
                state = [0]

                def llink(j, ins):
                    state[0] += 1
                    ins.then_inc(chain, 1)
                    e.wait_ge(chain, j * LINKS + state[0])

                def post(j, pre_a, pre_b, pre_c, last=False):
                    state[0] = 0
                    if not last:
                        pre_a()
                    bank_u, bank_g = ps[g_up % 2], ps[(g_up + 1) % 2]
                    e.wait_ge(group_done, j * 2 + (g_up + 1))
                    dst = upn[:, :, FKW - 1:] if which == 1 else cv
                    e.tensor_tensor(dst, bank_u[:, :].rearrange("p (m n) -> p m n", m=2), bc2(rstd_bc[:, :], 2),
                                    ALU.mult).then_inc(bank_free["dve"], 1)
                    e.wait_ge(bank_free["dve"], j * 2 + free0)
                    if which == 1:
                        for m in range(2):
                            def col(k):
                                c = j * 2 + (k * FT + m)
                                return fcol[:, bass.ds(c, 1)]
                            llink(j, e.tensor_scalar(cv[:, m, :], upn[:, m, 0:SEQ], col(0), col(FKW), ALU.mult, ALU.add))
                            llink(j, e.scalar_tensor_tensor(cv[:, m, :], upn[:, m, 1:1 + SEQ], col(1), cv[:, m, :],
                                                            ALU.mult, ALU.add))
                            ins = e.scalar_tensor_tensor(cv[:, m, :], upn[:, m, 2:2 + SEQ], col(2), cv[:, m, :],
                                                         ALU.mult, ALU.add)
                            if m == 0:
                                llink(j, ins)
                        ins.then_inc(f_conv, 1)
                    if last:
                        pre_a()
                    else:
                        pre_b()
                    e.wait_ge(group_done, j * 2 + (g_up + 2))
                    e.tensor_tensor(gt, bank_g[:, :].rearrange("p (m n) -> p m n", m=2), bc2(rstd_bc[:, :], 2),
                                    ALU.mult).then_inc(bank_free["dve"], 1)
                    e.wait_ge(bank_free["dve"], j * 2 + (free0 + 1))
                    e.wait_ge(f_glu, j + (n0 + 1))
                    e.tensor_tensor(actf, cv, gt, ALU.mult).then_inc(f_act, 1)
                    if not last:
                        pre_c()
                    e.wait_ge(f_hi, j + (n0 + 1))
                    e.tensor_tensor(act_parts[last][1], actf, act_parts[last][0].bitcast(f32), ALU.subtract).then_inc(f_lo, 1)
                    if last:
                        pre_b()
                        pre_c()
                    assert state[0] == (LINKS if which == 1 else 0)

                inv(n, False)
                post(0, lambda: pre(base + 3), lambda: pre(base + 4), lambda: None)
                with e.Fori(1, STEPS - 1) as j:
                    s = j * 3 + (base - 1)
                    post(j, lambda: lo(s + 3, (base + 2) % RING), lambda: lo(s + 4, (base + 3) % RING),
                         lambda: lo(s + 5, (base + 4) % RING))
                last = base + 3 * (STEPS - 1) - 1
                post(STEPS - 1, lambda: pre(last + 3), lambda: pre(last + 4), lambda: None, True)

            ffn(1, FFN1, 0, 1)
            for b in range(4):
                e.wait_ge(down_bank, b + 1)
                e.tensor_copy(X[:, 2 * b:2 * b + 2, :],
                              ps[2 + b][:, :].rearrange("p (m n) -> p m n", m=2)).then_inc(x_ready, 1)
                if b:
                    norm_lo(2, pcol[:, MIXG:MIXG + KD], pairs[0][1], pairs[0][0], (2 * b - 2, 2 * b - 1))
            norm_lo(2, pcol[:, MIXG:MIXG + KD], pairs[0][1], pairs[0][0], (6, 7))
            pre(S2_SEQ + 1)
            pre(S2_SEQ + 2)
            for s in range(S2_SEQ, S2_GA):
                if s == S2_SEQ:
                    inv(2, True)
                pre(s + 3)
            e.wait_ge(cq_ss, 1)
            e.reciprocal(ss2[:, :, :], r2[:, :, :]).then_inc(cq_r, 1)

            def cq_parts(r):
                e.wait_ge(cq_hi, (2, 4, 5)[r])
                for c in CQ_ROUND[r]:
                    e.scalar_tensor_tensor(pairs[1][1][:, c, :],
                                           (PSA, PSPT[0], PSA)[r][:, SEQ * (c % 2):SEQ * (c % 2) + SEQ],
                                           pcol[:, QLG + c:QLG + c + 1],
                                           pairs[1][0][:, c, :].bitcast(f32), ALU.mult,
                                           ALU.subtract).then_inc(cq_lo, 1)

            def kv_evac(i):
                g = GROUP_OF[(S2_UKV, i)]
                e.wait_ge(group_done, g + 1)
                for dst, src in kv_parts(ps[g % 2], i // 2, 0):
                    ins = e.tensor_copy(dst, src)
                ins.then_inc(bank_free["dve"], 1)

            for s in range(S2_GA, FFN2):
                steps = steps_at(s)
                if s == S2_UKV:
                    kv_evac(0)
                for step in steps[:1]:
                    att(step)
                if early_att(s) and not late_cut(s) and s < S2_OUT - 1:
                    pre(s + 2)
                for step in steps[1:]:
                    att(step)
                if S2_OSWA <= s < S2_OMLA:
                    e.wait_ge(gate_t, 12)
                    c = 4 * (s - S2_OSWA)
                    branch(GROUP_OF[(s, 0)], slice(c, c + 2), T0)
                if s == S2_GA + 1:
                    cq_parts(0)
                    cq_parts(1)
                if s == S2_GA + 2:
                    cq_parts(2)
                if gate_of(s) is not None:
                    gate(s, gate_of(s))
                if s == S2_UKV:
                    kv_evac(2)
                if S2_UQ <= s <= S2_UKV:
                    pre(s + 2)
                if S2_OSWA <= s < S2_OMLA:
                    c = 4 * (s - S2_OSWA) + 2
                    branch(GROUP_OF[(s, 1)], slice(c, c + 2), T0)
                if S2_OMLA <= s < S2_OUT:
                    e.wait_ge(gate_t, 16)
                    for i in range(2):
                        c = 2 * (s - S2_OMLA) + i
                        branch(GROUP_OF[(s, i)], slice(2 * c, 2 * c + 2), T1)
                        merge(c, 4, (lambda: pre(s + 2)) if s == S2_OUT - 1 and i == 0 else nothing)
                if S2_OUT <= s < FFN2:
                    i = s - S2_OUT
                    residual(s, i)
                    if s < FFN2 - 1:
                        pre(s + 3)
                    norm_lo(3, pcol[:, FFNG:FFNG + KD], pairs[2][1], pairs[2][0], (2 * i, 2 * i + 1))
                if s in (S2_OUT - 1, FFN2 - 1):
                    pre(s + 3)
            ffn(2, FFN2, STEPS, 3)
            e.wait_ge(fin_T, 1)
            e.tensor_copy(fing[:, 0:512], ps[0][:, :])
            e.tensor_copy(fing[:, 512:D], ps[1][:, :]).then_inc(fin_Te, 1)
            e.wait_ge(fin_Te, 1)
            for h in range(HALVES):
                e.wait_ge(fin_root, h + 1)
                link(e.reciprocal(finr[:, h:h + 1], fin2[:, 2 + h:3 + h]))
                for c in range(2):
                    cols = slice(512 * c, 512 * c + 512)
                    e.scalar_tensor_tensor(outp[:, h, cols], ps[2 + 2 * h + c][:, :], finr[:, h:h + 1],
                                           fing[:, cols], ALU.mult, ALU.mult).then_inc(y_ready, 1)

        @block.gpsimd
        def _(e):
            def fold(n):
                for i in range(1, 4):
                    e.wait_ge(sq_ready, 4 * n + i + 1)
                    if i > 1:
                        e.wait_ge(folded, 3 * n + i - 1)
                    e.tensor_tensor(SQ[:, 0:2, :], SQ[:, 0:2, :], SQ[:, 2 * i:2 * i + 2, :], ALU.add).then_inc(folded, 1)
                e.wait_ge(folded, 3 * n + 3)
                e.tensor_tensor(SQ[:, 0, :], SQ[:, 0, :], SQ[:, 1, :], ALU.add).then_inc(sq_fold, 1)

            fold(0)
            for s in range(S_XR, S_G):
                e.wait_ge(xa_hi, s + 1)
                e.tensor_tensor(pairs[1][1][:, 2 * s:2 * s + 2, :], xa[:, 2 * s:2 * s + 2, :],
                                pairs[1][0][:, 2 * s:2 * s + 2, :].bitcast(f32), ALU.subtract).then_inc(xa_lo, 1)
            e.wait_ge(group_done, GROUP_OF[(S_RI, 7)] + 1)
            for m in range(KD):
                ya = rnn_t[:, 2 + m % 2, :]
                e.wait_ge(ya_ready, m + 1)
                e.tensor_copy(pairs[1][0][:, m, :], ya).then_inc(ya_hi, 1)
                e.wait_ge(ya_hi, m + 1)
                e.tensor_tensor(pairs[1][1][:, m, :], ya, pairs[1][0][:, m, :].bitcast(f32),
                                ALU.subtract).then_inc(ya_lo, 1)

            def merge_parts(n0):
                for i in range(POOL_MERGES):
                    tiles = slice(2 * i, 2 * i + 2)
                    e.wait_ge(m_hi, n0 + i + 1)
                    e.tensor_tensor(pairs[0][1][:, tiles, :], T0[:, tiles, :], pairs[0][0][:, tiles, :].bitcast(f32),
                                    ALU.subtract).then_inc(m_lo_pool, 1)

            merge_parts(0)
            fold(1)
            fold(2)
            steps = [0]

            def link(ins):
                steps[0] += 1
                ins.then_inc(pool_step, 1)
                e.wait_ge(pool_step, steps[0])

            def rotate(src1, src2, dst1, dst2, cos, sin, n, w, done=None):
                def t3(i):
                    return rope_t[:, i, 0:n * w].rearrange("p (n w) -> p n w", n=n)
                c = cos.unsqueeze(1).to_broadcast([P, n, w])
                s_ = sin.unsqueeze(1).to_broadcast([P, n, w])
                e.tensor_tensor(t3(0), src1, c, ALU.mult)
                e.tensor_tensor(t3(1), src2, s_, ALU.mult)
                e.tensor_tensor(t3(2), src2, c, ALU.mult)
                link(e.tensor_tensor(t3(3), src1, s_, ALU.mult))
                link(e.tensor_tensor(dst1, t3(0), t3(1), ALU.subtract))
                ins = e.tensor_tensor(dst2, t3(2), t3(3), ALU.add)
                if done:
                    ins.then_inc(done, 1)
                    e.wait_ge(done, 1)
                else:
                    link(ins)

            e.wait_ge(in_misc, 16 * 7)
            for a in range(2):
                e.wait_ge(bank_free["act"], U2_FREE[a])
                for h in range(HALVES):
                    src = u2[:, h, 256 * a:256 * a + 256].rearrange("p (n d) -> p n d", n=4)
                    dst = q_r[:, h, :].rearrange("p (n b d) -> p b n d", b=2, d=64)[:, a]
                    rotate(src[:, :, 0:32], src[:, :, 32:64], dst[:, :, 0:32], dst[:, :, 32:64],
                           ropeA[:, 0, h, :], ropeA[:, 1, h, :], 4, 32)
            e.wait_ge(bank_free["act"], U2_FREE[2])
            for h in range(HALVES):
                src = u2[:, h, OFF_KA:OFF_KA + P].rearrange("p (n d) -> p n d", n=2)
                dst = k_r[:, h, :].rearrange("p (n d) -> p n d", n=2)
                rotate(src[:, :, 0:32], src[:, :, 32:64], dst[:, :, 0:32], dst[:, :, 32:64],
                       ropeA[:, 0, h, :], ropeA[:, 1, h, :], 2, 32, rope_q if h else None)
            e.wait_ge(bank_free["act"], U2_FREE[5])
            for h in range(HALVES):
                src = u2[:, h, OFF_KR:OFF_KR + ROPE].unsqueeze(1)
                dst = krr[:, h, :].unsqueeze(1)
                rotate(src[:, :, 0:16], src[:, :, 16:32], dst[:, :, 0:16], dst[:, :, 16:32],
                       ropeB[:, 0, h, :], ropeB[:, 1, h, :], 1, 16)
                ins = e.tensor_copy(kf[:, h, :, NOPE:MLA_D],
                                    krr[:, h, :].unsqueeze(1).to_broadcast([P, HEADS, ROPE]))
            ins.then_inc(rope_k, 1)
            for i in range(2):
                for h in range(HALVES):
                    e.wait_ge(bank_free["act"], emptied(GROUP_OF[(S2_UQ + i, h)])[1])
                    src = qb[:, h, 4 * i:4 * i + 4]
                    rotate(src[:, :, 64:80], src[:, :, 80:96], src[:, :, 64:80], src[:, :, 80:96],
                           ropeB[:, 0, h, :], ropeB[:, 1, h, :], 4, 16, mla_ready if i and h else None)
            merge_parts(4)
            fold(3)

        @block.tensor
        def _(e):
            def three(out, lhs, rhs, first, last):
                e.matmul(out, lhs[0], rhs[0], start=first, stop=False, skip_group_check=True)
                e.matmul(out, lhs[0], rhs[1], start=False, stop=False, skip_group_check=True)
                return e.matmul(out, lhs[1], rhs[0], start=False, stop=last, skip_group_check=True)

            def bank_ready(g):
                if g >= 2:
                    who, n = emptied(g - 2)
                    e.wait_ge(bank_free[who], n)

            def weights(slot, k, cols, width):
                return tuple(w[slot][:, width * k:width * (k + 1)][:, cols] for w in (whi, wlo))

            def always(k):
                pass

            def feature_tiles(out, slot, kk, width, act, tiles, k0=0, ready=always):
                for k in range(kk):
                    ready(k)
                    for n, (c, o) in enumerate(tiles):
                        ins = three(out[:, o:o + SEQ], weights(slot, k, slice(c, c + P), width),
                                    (act[0][:, k0 + k, :], act[1][:, k0 + k, :]), n == 0 and k == 0, k == kk - 1)
                return ins

            def positions(out, slot, kk, width, act, cols, halves_, k0=0, ready=always):
                for k in range(kk):
                    ready(k)
                    for n, (h, o) in enumerate(halves_):
                        ins = three(out[:, o:o + cols.stop - cols.start],
                                    tuple(a[:, k0 + k, P * h:P * h + P] for a in act),
                                    weights(slot, k, cols, width), n == 0 and k == 0, k == kk - 1)
                return ins

            def sums(n, seq):
                e.wait_ge(sq_fold, n + 1)
                e.wait_ge(consts, 1)
                if seq:
                    for h in range(HALVES):
                        e.matmul(PSB[:, h:h + 1], SQ[:, 0, P * h:P * h + P], ones[:, 0:1], start=True, stop=True,
                                 skip_group_check=True)
                e.matmul(PSA[:, 0:SEQ], ones[:, :], SQ[:, 0, :], start=True, stop=True).then_inc(ssum, 1)

            def att(step):
                kind_base = 0 if step < 100 else 100
                u = unit_of(step)
                if u is not None and not (8 <= u < 16 and u % 2):
                    n_t = t_count(u)
                    if n_t >= 2:
                        e.wait_ge(aTe, n_t - 1)
                    if u == 0:
                        e.wait_ge(qk_scaled, 1)
                    if u == 8:
                        e.wait_ge(rope_q, 1)
                    if u == 16:
                        e.wait_ge(mla_ready, 1)
                        e.wait_ge(rope_k, 1)
                        for i in (2, 3):
                            who, n = emptied(GROUP_OF[(S2_UKV, i)])
                            e.wait_ge(bank_free[who], n)
                    for h in range(HALVES):
                        for i in range(2):
                            if u < 8:
                                src = (q_s, k_s)[i][:, h, P * u:P * u + P]
                            elif u < 16:
                                c = (u - 8) // 2
                                src = q_r[:, h, P * c:P * c + P] if i == 0 else k_r[:, h, :]
                            else:
                                src = (qb, kf)[i][:, h, u - 16, :]
                            d = MLA_D if u >= 16 else P
                            ins = e.transpose(PST[0:d, SEQ * i + P * h:SEQ * i + P * h + P], src, ident[:, :])
                    ins.then_inc(aT, 1)
                u = unit_of(step - LAG_S) if step - LAG_S >= kind_base else None
                if u is not None:
                    e.wait_ge(aTe, t_count(u))
                    if u >= 2:
                        e.wait_ge(aM, u - 1)
                    b = tbuf(u)
                    rows = slice(0, P) if u < 8 else slice(64 * (u % 2), 64 * (u % 2) + 64) if u < 16 \
                        else slice(0, MLA_D)
                    e.matmul(PSS[u % 2][:, 0:P], qT[rows, b, 0:P], kT[rows, b, 0:P], start=True, stop=True)
                    e.matmul(PSS[u % 2][:, P:3 * P], qT[rows, b, P:SEQ], kT[rows, b, :], start=True,
                             stop=True).then_inc(aS, 1)
                u = unit_of(step - LAG_PT) if step - LAG_PT >= kind_base else None
                if u is not None:
                    e.wait_ge(aN, u + 1)
                    if u >= 2:
                        e.wait_ge(aPTe, u - 1)
                    if u == 9:
                        e.wait_ge(cq_lo, 5)
                    for i in range(3):
                        ins = e.transpose(PSPT[u % 2][:, P * i:P * i + P], pr[:, u % 3, P * i:P * i + P], ident[:, :])
                    ins.then_inc(aPT, 1)
                u = unit_of(step - LAG_PV) if step - LAG_PV >= kind_base else None
                if u is not None:
                    e.wait_ge(aPTe, u + 1)
                    if u >= 1:
                        e.wait_ge(aL, u)
                    if u < 8:
                        v = [v_s[:, h, P * u:P * u + P] for h in range(2)]
                    elif u < 16:
                        v = [u2[:, h, OFF_VA:OFF_VA + P] for h in range(2)]
                    else:
                        c = (u - 16) // 2
                        v = [vb[:, h, P * c:P * c + P] for h in range(2)]
                    e.matmul(PSPV[:, 0:SEQ], v[0], pT[:, u % 2, 0:SEQ], start=True, stop=False,
                             skip_group_check=True)
                    e.matmul(PSPV[:, P:SEQ], v[1], pT[:, u % 2, SEQ:3 * P], start=False, stop=True,
                             skip_group_check=True).then_inc(aPV, 1)

            def merge_ready(block, k):
                i = k // 2
                if i < POOL_MERGES:
                    e.wait_ge(m_lo_pool, POOL_MERGES * block + i + 1)
                else:
                    e.wait_ge(m_lo, (4 - POOL_MERGES) * block + i - POOL_MERGES + 1)

            def slab(s, act, layout="feature", ready=always, hook=None):
                if s:
                    e.wait_ge(lo_ready, s + 1)
                else:
                    e.wait_ge(first_lo, 1)
                slot = s % RING
                kind = PLAN[s][1]
                n = sum(1 for x in GROUPS if x[0] == s)
                for i in range(n):
                    g = GROUP_OF[(s, i)]
                    bank_ready(g)
                    out = ps[g % 2]
                    steps = steps_at(s)

                    def at(k, steps=steps, i=i):
                        places = [(0, 0), (0, 4) if n == 1 else (1, 0)]
                        for place, step in zip(places, steps):
                            if place == (i, k):
                                att(step)
                        if hook and (i, k) == (0, 6 if s == S2_SEQ + 1 else 4):
                            hook()
                        if s == 0 and k == KD // 2:
                            e.wait_ge(lo_ready, 1)
                        ready(k)

                    if kind == "blocks":
                        for m in range(2):
                            blk = 2 * (i % 4) + m
                            c = 1024 * (i // 4) + P * blk
                            ins = three(out[:, SEQ * m:SEQ * m + SEQ], tuple(w[slot][:, c:c + P] for w in (whi, wlo)),
                                        (act[0][:, blk, :], act[1][:, blk, :]), m == 0, True)
                    elif layout == "feature" and kind == "cols":
                        ins = feature_tiles(out, slot, KD, WIDE, act, [(0, 0), (P, SEQ)], ready=at)
                    elif layout == "feature":
                        k0 = 4 if s >= S2_OMLA else 0
                        ins = feature_tiles(out, slot, 4, 512, act, [(2 * P * i, 0), (2 * P * i + P, SEQ)], k0=k0,
                                            ready=at)
                    elif kind == "cols":
                        width = min(WIDE, t[PLAN[s][0]].shape[2] - PLAN[s][2])
                        if s == S2_GA - 1:
                            width = SEQ_COLS - PLAN[s][2]
                        ins = positions(out, slot, KD, WIDE, act, slice(0, width), [(0, 0), (1, 256)],
                                        ready=at)
                    elif kind == "rows3":
                        ins = positions(out, slot, 3, QLAT, act, slice(0, QLAT), [(i, 0)], ready=at)
                    else:
                        h, c = divmod(i, 2)
                        ins = positions(out, slot, 2, 1024, act, slice(512 * c, 512 * c + 512), [(h, 0)], k0=3,
                                        ready=at)
                    ins.then_inc(group_done, 1)

            for s in range(S_XR, FFN1):
                if s == S_RI:
                    e.wait_ge(xa_lo, 4)
                if s == S_V:
                    e.wait_ge(in_misc, 16 * 7)
                    e.wait_ge(rstd_ready, 1)
                    e.matmul(PSB[:, 8:8 + HEADS], ones[0:1, :], rowt[:, :], start=True, stop=True).then_inc(sink_T, 1)
                ready = {
                    S_XR: lambda k: e.wait_ge(h_lo, k + 1),
                    S_PR: lambda k: e.wait_ge(ya_lo, k + 1),
                    S_PA: lambda k: e.wait_ge(aL, k + 1),
                    S_OUT: lambda k: merge_ready(0, k),
                }.get(s, always)
                act = pairs[1] if s == S_RI or S_PR <= s < S_PA else pairs[2] if S_PA <= s < S_OUT else pairs[0]
                slab(s, act, "position" if S_Q <= s < S_GATE else "feature", ready)
                if s == S_XR:
                    sums(0, True)

            def final_gains():
                e.wait_ge(in_fing, 16)
                e.wait_ge(bank_free["dve"], emptied(GROUP_OF[(FFN2, 2 * STEPS - 1)])[1])
                for c in range(2):
                    ins = e.matmul(ps[c][:, :], ones[0:1, :], frow_g[:, 512 * c:512 * c + 512], start=True, stop=True)
                ins.then_inc(fin_T, 1)

            def ffn(which, base, n, n0):
                act = pairs[2]
                g_up = GROUP_OF[(base, 0)]
                free0 = emptied(g_up)[1]
                def residual():
                    if which == 1:
                        for c in range(KD):
                            e.wait_ge(*x_value(n, c))
                            e.matmul(ps[2 + c // 2][:, SEQ * (c % 2):SEQ * (c % 2) + SEQ], ident[:, :], X[:, c, :],
                                     start=(c % 2 == 0), stop=False, skip_group_check=True)
                    else:
                        for c in range(KD):
                            e.wait_ge(*x_value(n, c))
                            for h in range(HALVES):
                                e.matmul(ps[2 + 2 * h + c // 4][:, P * (c % 4):P * (c % 4) + P],
                                         X[:, c, P * h:P * h + P], ident[:, :], start=(c % 4 == 0), stop=False,
                                         skip_group_check=True)

                def wide(j, s, slot, i, free, ready=always):
                    e.wait_ge(lo_ready, s + 1)
                    free()
                    feature_tiles(ps[(g_up + i) % 2], slot, KD, WIDE, act, [(0, 0), (P, SEQ)],
                                  ready=ready).then_inc(group_done, 1)

                def down(j, s, slot, last=False):
                    e.wait_ge(lo_ready, s + 1)
                    e.wait_ge(f_lo, j + (n0 + 1))
                    acthi, actlo = act_parts[last]
                    if which == 1:
                        for c in range(KD):
                            for k in range(2):
                                ins = three(ps[2 + c // 2][:, SEQ * (c % 2):SEQ * (c % 2) + SEQ],
                                            weights(slot, k, slice(P * c, P * c + P), D),
                                            (acthi[:, k, :], actlo[:, k, :]), False, False)
                            if last and c % 2 and c < KD - 1:
                                ins.then_inc(down_bank, 1)
                    else:
                        for h in range(HALVES):
                            if last and h:
                                ins.then_inc(down_bank, 1)
                                final_gains()
                            for k in range(2):
                                for c in range(2):
                                    ins = three(ps[2 + 2 * h + c][:, :],
                                                (acthi[:, k, P * h:P * h + P], actlo[:, k, P * h:P * h + P]),
                                                weights(slot, k, slice(512 * c, 512 * c + 512), D), False, False)
                    ins.then_inc(down_bank if last else down_used, 1)

                residual()
                for i in range(2):
                    g = g_up + i
                    wide(0, base + i, (base + i) % RING, i, lambda: bank_ready(g),
                         (lambda k: e.wait_ge(h_lo, KD * n + k + 1)) if i == 0 else always)
                    if i == 0:
                        sums(n, False)
                with e.Fori(1, STEPS) as j:
                    s = j * 3 + (base - 1)
                    for i in range(2):
                        wide(j, s + i, (base + 2 + i) % RING, i,
                             lambda: e.wait_ge(bank_free["dve"], (j - 1) * 2 + (free0 + i)))
                    down(j - 1, s + 2, (base + 4) % RING)
                last = base + 3 * STEPS - 1
                down(STEPS - 1, last, last % RING, True)

            ffn(1, FFN1, 1, 0)

            def cq_transposes(r):
                e.wait_ge(cq_s, 1)
                if r == 2:
                    e.wait_ge(cq_lo, 4)
                for c in CQ_ROUND[r]:
                    for h in range(HALVES):
                        o = SEQ * (c % 2) + P * h
                        ins = e.transpose((PSA, PSPT[0], PSA)[r][:, o:o + P],
                                          u2[:, h, OFF_QL + P * c:OFF_QL + P * c + P], ident[:, :])
                ins.then_inc(cq_T, 1)

            for s in range(S2_SEQ, FFN2):
                ready = {
                    S2_SEQ: lambda k: e.wait_ge(h_lo, 2 * KD + k + 1),
                    S2_UQ: lambda k: e.wait_ge(cq_lo, k + 1),
                    S2_UKV: lambda k: e.wait_ge(cq_lo, 3 + k + 1),
                    S2_OSWA: lambda k: e.wait_ge(aL, 8 + 2 * k + 2),
                    S2_OMLA: lambda k: e.wait_ge(aL, 16 + 2 * k + 2),
                    S2_OUT: lambda k: merge_ready(1, k),
                }.get(s, always)
                hook = {S2_SEQ + 1: lambda: sums(2, True),
                        S2_GA + 1: lambda: (cq_transposes(0), cq_transposes(1)),
                        S2_GA + 2: lambda: cq_transposes(2)}.get(s)
                act = pairs[1] if S2_UQ <= s <= S2_UKV else pairs[2] if S2_OSWA <= s < S2_OUT else pairs[0]
                slab(s, act, "position" if s < S2_GA or S2_UQ <= s <= S2_UKV else "feature", ready, hook)
            ffn(2, FFN2, 3, STEPS)


def t_count(u):
    return u + 1 if u < 8 else 8 + (u - 8) // 2 + 1 if u < 16 else 12 + u - 16 + 1


def tbuf(u):
    return (t_count(u) - 1) % 2


def last_reader_of_tbuf(u):
    n = t_count(u) - 2
    return max(v for v in range(24) if t_count(v) == n) + 1


def swa_head(u):
    return (u - 8) // 2 + 4 * ((u - 8) % 2)


def yb_place(u):
    if u < 8:
        return slice(0, P), u
    b = u % 2
    return slice(64 * b, 64 * b + 64), (u - 8) // 2


_INS = ['w_in', 'w_r', 'w_i', 'w_proj_rnn', 'w_proj_attn', 'w_out', 'w_up', 'w_gate', 'w_down', 'w_in_2',
        'swa_sinks_2', 'w_uq_2', 'w_ukv_2', 'w_o_swa_2', 'w_o_mla_2', 'w_out_2', 'w_gate_2', 'w_up_2',
        'w_down_2', 'final_norm_g_2']


def feature_columns(a):
    return np.asarray(a).reshape(-1, P).T


def constants():
    q = np.arange(P)[:, None]
    k = np.arange(P)[None, :]
    causal = np.where(k <= q, 0.0, NEG)
    before = np.where(k > q, 0.0, NEG)
    masks = np.stack([np.concatenate([causal, 0 * causal, causal], 1),
                      np.concatenate([causal, before, causal], 1)], 1).astype(np.float32)

    def rope(dim):
        inv = np.float32(10000.0) ** (-np.arange(0, dim, 2, dtype=np.float32) / np.float32(dim))
        ang = np.arange(SEQ, dtype=np.float32)[:, None] * inv.astype(np.float32)[None, :]
        return np.stack([np.cos(ang), np.sin(ang)]).astype(np.float32)
    return {"ident": np.eye(P, dtype=np.float32), "masks": masks, "rope_a": rope(64), "rope_b": rope(32)}


def kernel(**inputs):
    import concourse.bacc as _bacc
    from concourse.bass_utils import run_bass_kernel_spmd as _run

    nc = _bacc.Bacc("TRN2", target_bir_lowering=False, num_devices=1)
    arrays, t = {}, {}
    given = {n: np.ascontiguousarray(inputs[n]) for n in _INS}
    given.update(constants())
    given["params"] = np.ascontiguousarray(np.concatenate([feature_columns(inputs[n]) for n in PARAMS], axis=1))
    given["xT"] = np.ascontiguousarray(np.asarray(inputs["x"])[0].T.reshape(KD, P, SEQ).transpose(1, 0, 2))
    for name, a in given.items():
        arrays[f"in_{name}"] = a
        t[name] = nc.dram_tensor(f"in_{name}", a.shape, mybir.dt.from_np(a.dtype), kind="ExternalInput").ap()
    t["final_norm_g"] = t["final_norm_g_2"]
    t["out"] = nc.dram_tensor("out", (1, SEQ, D), mybir.dt.float32, kind="ExternalOutput").ap()
    program(nc, t)
    r = _run(nc, [arrays], core_ids=[0])
    return r.results[0]["out"]
```
